# Optimizing a Trainium2 kernel written in Bass

```python
import jax, jax.numpy as jnp
from jax import lax
import numpy as np
import jax
import jax.numpy as jnp

D_MODEL = 1024
BATCH = 1
SEQ = 256
DEPTH = 2

GRID_W = 64
CTX_LEN = 256
HEAD_DIM = 64
MIX_WIDTH = D_MODEL
A_HEADS = MIX_WIDTH // (2 * HEAD_DIM)
A_WIDTH = A_HEADS * HEAD_DIM
DECAY_LORA = 64
ICLR_LORA = 64
GATE_LORA = 128
B_HEADS = MIX_WIDTH // (2 * HEAD_DIM)
B_KV_HEADS = 2
WINDOW = 128
BLOCK = 128
C_HEADS = MIX_WIDTH // (2 * HEAD_DIM)
NA_KH = 8
NA_KW = 16
NA_QC = 16
NA_KC = 32
D_HEADS = MIX_WIDTH // (2 * HEAD_DIM)
D_KV_HEADS = 2
D_FF = 4 * D_MODEL
ROPE_BASE = 10000.0
NORM_EPS = 1e-6
GN_EPS = 64e-5
NEG_INF = -1e30
ATTN_SCALE = HEAD_DIM ** -0.5
N_EVEN = (DEPTH + 1) // 2
N_ODD = DEPTH // 2
A_IN = 3 * A_WIDTH + 2 * DECAY_LORA + 2 * ICLR_LORA + GATE_LORA
B_IN = (B_HEADS + 2 * B_KV_HEADS) * HEAD_DIM
C_IN = 3 * C_HEADS * HEAD_DIM
D_IN = (D_HEADS + 2 * D_KV_HEADS) * HEAD_DIM
EVEN_IN = A_IN + B_IN
ODD_IN = C_IN + D_IN
A_SPLITS = (A_WIDTH, 2 * A_WIDTH, 3 * A_WIDTH, 3 * A_WIDTH + 2 * DECAY_LORA,
            3 * A_WIDTH + 2 * DECAY_LORA + 2 * ICLR_LORA)


def rms_norm(x, g):
    xf = x.astype(jnp.float32)
    y = xf * lax.rsqrt(jnp.mean(xf * xf, axis=-1, keepdims=True) + NORM_EPS)
    return (y * g.astype(jnp.float32)).astype(x.dtype)

def modulate(h, gain, shift, scale):
    return rms_norm(h, gain) * (1 + scale) + shift

def sqrelu_mlp(u, w1, w2):
    return jnp.square(jax.nn.relu(u @ w1)) @ w2

def axial_angles(n_tok):
    t = jnp.arange(n_tok, dtype=jnp.int32)
    n_freq = HEAD_DIM // 4
    inv_freq = ROPE_BASE ** (-jnp.arange(n_freq, dtype=jnp.float32) / n_freq)
    row = (t // GRID_W).astype(jnp.float32)[:, None] * inv_freq
    col = (t % GRID_W).astype(jnp.float32)[:, None] * inv_freq
    return row, col

def _rotate(x, ang):
    f = ang.shape[-1]
    cos = jnp.cos(ang)[None, :, None, :]
    sin = jnp.sin(ang)[None, :, None, :]
    x1 = x[..., :f].astype(jnp.float32)
    x2 = x[..., f:].astype(jnp.float32)
    return jnp.concatenate([x1 * cos - x2 * sin, x1 * sin + x2 * cos], axis=-1).astype(x.dtype)

def axial_rope(x, ang):
    half = HEAD_DIM // 2
    return jnp.concatenate([_rotate(x[..., :half], ang[0]), _rotate(x[..., half:], ang[1])], axis=-1)

def split_qkv(p, hq, hkv):
    bn, s, _ = p.shape
    q, k, v = jnp.split(p, [hq * HEAD_DIM, (hq + hkv) * HEAD_DIM], axis=-1)
    return (q.reshape(bn, s, hq, HEAD_DIM), k.reshape(bn, s, hkv, HEAD_DIM), v.reshape(bn, s, hkv, HEAD_DIM))

def softmax_with_sink(s, sink):
    sk = jnp.broadcast_to(sink.astype(jnp.float32)[:, :, None, None], s.shape[:-1] + (1,))
    return jax.nn.softmax(jnp.concatenate([s, sk], axis=-1), axis=-1)[..., :-1]

def context_attention(q, k, v, sink=None):
    bn, l, h, d = q.shape
    hkv = k.shape[2]
    qg = q.reshape(bn, l, hkv, h // hkv, d)
    s = jnp.einsum('blkgd,bckd->bkglc', qg, k).astype(jnp.float32) * ATTN_SCALE
    p = jax.nn.softmax(s, axis=-1) if sink is None else softmax_with_sink(s, sink)
    o = jnp.einsum('bkglc,bckd->blkgd', p.astype(v.dtype), v)
    return o.reshape(bn, l, h * d)

def centred_shift(p, mu_prev, mu_next):
    prev = jnp.pad(p, ((0, 0), (1, 0), (0, 0)))[:, :-1]
    nxt = jnp.pad(p, ((0, 0), (0, 1), (0, 0)))[:, 1:]
    return p + mu_prev * (prev - p) + mu_next * (nxt - p)

def rwkv7_prepare(pa, prm):
    p = centred_shift(pa, prm['mu_prev'], prm['mu_next']).astype(jnp.float32)
    bn, s, _ = p.shape
    r, k, v, wl, al, gl = jnp.split(p, A_SPLITS, axis=-1)
    wl = wl.reshape(bn, s, 2, DECAY_LORA)
    al = al.reshape(bn, s, 2, ICLR_LORA)
    w_raw = prm['w0'] + jnp.einsum('bsdl,dlc->bsdc', jnp.tanh(wl), prm['w2'])
    decay = jnp.exp(-jnp.exp(-jax.nn.softplus(-w_raw) - 0.5))
    iclr = jax.nn.sigmoid(prm['a0'] + jnp.einsum('bsdl,dlc->bsdc', al, prm['a2']))
    g = jax.nn.sigmoid(gl) @ prm['g2']
    kk = (k * prm['k_k']).reshape(bn, s, A_HEADS, HEAD_DIM)
    kk = kk / jnp.maximum(jnp.sqrt(jnp.sum(kk * kk, axis=-1, keepdims=True)), 1e-12)
    k_dir = k[:, :, None, :] * (1 + (iclr - 1) * prm['k_a'])
    heads = lambda t: t.reshape(t.shape[:-1] + (A_HEADS, HEAD_DIM))
    return dict(r=heads(r), v=heads(v), g=g, kk=kk, k=heads(k_dir), w=heads(decay), a=heads(iclr))

def rwkv7_scan(f, d, s0, reverse):
    def step(state, inp):
        r_t, w_t, k_t, v_t, kk_t, a_t = inp
        sa = jnp.einsum('bhvk,bhk->bhv', state, -kk_t)
        state = (state * w_t[:, :, None, :] + sa[..., None] * (kk_t * a_t)[:, :, None, :]
                 + v_t[..., None] * k_t[:, :, None, :])
        return state, jnp.einsum('bhvk,bhk->bhv', state, r_t)
    seq = (f['r'], f['w'][:, :, d], f['k'][:, :, d], f['v'], f['kk'], f['a'][:, :, d])
    xs = tuple(jnp.moveaxis(t, 1, 0) for t in seq)
    s_last, ys = lax.scan(step, s0, xs, reverse=reverse)
    return s_last, jnp.moveaxis(ys, 0, 1)

def rwkv7_output(f, y, prm, dtype):
    bn, s = y.shape[:2]
    mu = jnp.mean(y, axis=-1, keepdims=True)
    var = jnp.mean(jnp.square(y - mu), axis=-1, keepdims=True)
    yn = ((y - mu) * lax.rsqrt(var + GN_EPS)).reshape(bn, s, A_WIDTH) * prm['gn_w'] + prm['gn_b']
    bonus = jnp.sum(f['r'][:, :, None] * f['k'] * prm['r_k'], axis=(2, 4))
    yn = yn + (bonus[..., None] * f['v']).reshape(bn, s, A_WIDTH)
    return (yn * f['g']).astype(dtype)

def rwkv7_mixer(pa_ctx, pa_lat, prm, need_ctx):
    fc = rwkv7_prepare(pa_ctx, prm)
    fl = rwkv7_prepare(pa_lat, prm)
    zero = jnp.zeros((pa_lat.shape[0], A_HEADS, HEAD_DIM, HEAD_DIM), jnp.float32)
    s_cf, yc_f = rwkv7_scan(fc, 0, zero, False)
    _, yl_f = rwkv7_scan(fl, 0, s_cf, False)
    s_cb, yc_b = rwkv7_scan(fc, 1, zero, True)
    _, yl_b = rwkv7_scan(fl, 1, s_cb, True)
    out_lat = rwkv7_output(fl, yl_f + yl_b, prm, pa_lat.dtype)
    out_ctx = rwkv7_output(fc, yc_f + yc_b, prm, pa_ctx.dtype) if need_ctx else None
    return out_lat, out_ctx

def banded_window_attention(q, k, v, k_ctx, v_ctx, sink):
    bn, s, h, d = q.shape
    hkv = k.shape[2]
    nb = s // BLOCK
    qb = q.reshape(bn, nb, BLOCK, hkv, h // hkv, d)

    def band(t):
        tp = jnp.pad(t, ((0, 0), (BLOCK, BLOCK), (0, 0), (0, 0)))
        return jnp.concatenate([tp[:, j * BLOCK: j * BLOCK + s].reshape(bn, nb, BLOCK, hkv, d)
                                for j in range(3)], axis=2)
    kb, vb = band(k), band(v)
    qi = np.arange(BLOCK)[:, None]
    kj = np.arange(3 * BLOCK)[None, :]
    kpos = (np.arange(nb) * BLOCK)[:, None, None] - BLOCK + kj[None]
    ok = (np.abs(kj - BLOCK - qi) <= WINDOW)[None] & (kpos >= 0) & (kpos < s)
    s_lat = jnp.einsum('bnqkgd,bnjkd->bnkgqj', qb, kb).astype(jnp.float32) * ATTN_SCALE
    s_lat = jnp.where(ok[None, :, None, None], s_lat, NEG_INF)
    s_ctx = jnp.einsum('bnqkgd,bckd->bnkgqc', qb, k_ctx).astype(jnp.float32) * ATTN_SCALE
    p = softmax_with_sink(jnp.concatenate([s_lat, s_ctx], axis=-1), sink)
    p_lat, p_ctx = p[..., :3 * BLOCK].astype(v.dtype), p[..., 3 * BLOCK:].astype(v.dtype)
    o = (jnp.einsum('bnkgqj,bnjkd->bnqkgd', p_lat, vb)
         + jnp.einsum('bnkgqc,bckd->bnqkgd', p_ctx, v_ctx))
    return o.reshape(bn, s, h * d)

def neighbourhood_tables(rows):
    kh = min(NA_KH, rows)
    r = np.arange(rows)
    row_idx = np.clip(r - kh // 2, 0, rows - kh)[:, None] + np.arange(kh)[None, :]
    dr = row_idx - r[:, None] + NA_KH - 1
    ncb = GRID_W // NA_QC
    q_col = np.arange(ncb)[:, None] * NA_QC + np.arange(NA_QC)[None, :]
    key_col = (np.clip(np.arange(ncb) * NA_QC - NA_KW // 2, 0, GRID_W - NA_KC)[:, None]
               + np.arange(NA_KC)[None, :])
    win_start = np.clip(q_col - NA_KW // 2, 0, GRID_W - NA_KW)[:, :, None]
    kc = key_col[:, None, :]
    col_ok = (kc >= win_start) & (kc < win_start + NA_KW)
    dc = np.clip(kc - q_col[:, :, None] + NA_KW - 1, 0, 2 * NA_KW - 2)
    return row_idx, dr, key_col, col_ok, dc

def neighbourhood_attention(q, k, v, k_ctx, v_ctx, rpb):
    bn, s, h, d = q.shape
    rows = s // GRID_W
    ncb = GRID_W // NA_QC
    row_idx, dr, key_col, col_ok, dc = neighbourhood_tables(rows)
    kh = row_idx.shape[1]

    def gather(t):
        return t.reshape(bn, rows, GRID_W, h, d)[:, row_idx][:, :, :, key_col]
    kg, vg = gather(k), gather(v)
    qg = q.reshape(bn, rows, ncb, NA_QC, h, d)
    s_lat = jnp.einsum('brmqhd,brtmjhd->brmhqtj', qg, kg).astype(jnp.float32) * ATTN_SCALE
    bias = rpb[:, dr[:, None, None, :, None], dc[None, :, :, None, :]]
    s_lat = s_lat + bias.transpose(1, 2, 0, 3, 4, 5).astype(jnp.float32)
    s_lat = jnp.where(col_ok[:, None, :, None, :], s_lat, NEG_INF)
    s_lat = s_lat.reshape(s_lat.shape[:-2] + (kh * NA_KC,))
    s_ctx = jnp.einsum('brmqhd,bchd->brmhqc', qg, k_ctx).astype(jnp.float32) * ATTN_SCALE
    p = jax.nn.softmax(jnp.concatenate([s_lat, s_ctx], axis=-1), axis=-1)
    p_lat = p[..., :kh * NA_KC].reshape(p.shape[:-1] + (kh, NA_KC)).astype(v.dtype)
    p_ctx = p[..., kh * NA_KC:].astype(v.dtype)
    o = (jnp.einsum('brmhqtj,brtmjhd->brmqhd', p_lat, vg)
         + jnp.einsum('brmhqc,bchd->brmqhd', p_ctx, v_ctx))
    return o.reshape(bn, s, h * d)

def global_block_attention(q, k, v, k_ctx, v_ctx):
    bn, s, h, d = q.shape
    hkv = k.shape[2]
    nb = s // BLOCK
    k_all = jnp.concatenate([k_ctx, k], axis=1)
    v_all = jnp.concatenate([v_ctx, v], axis=1)
    qb = q.reshape(bn, nb, BLOCK, hkv, h // hkv, d).transpose(1, 0, 2, 3, 4, 5)

    def one_block(qblk):
        sc = jnp.einsum('bqkgd,bskd->bkgqs', qblk, k_all).astype(jnp.float32) * ATTN_SCALE
        p = jax.nn.softmax(sc, axis=-1).astype(v_all.dtype)
        return jnp.einsum('bkgqs,bskd->bqkgd', p, v_all)
    o = lax.map(one_block, qb)
    return o.transpose(1, 0, 2, 3, 4, 5).reshape(bn, s, h * d)

def even_mixer(u_ctx, u_lat, w_in, w_out, a_prm, sink, rope_ang, need_ctx):
    p_ctx = u_ctx @ w_in
    p_lat = u_lat @ w_in
    a_lat, a_ctx = rwkv7_mixer(p_ctx[..., :A_IN], p_lat[..., :A_IN], a_prm, need_ctx)
    qc, kc, vc = split_qkv(p_ctx[..., A_IN:], B_HEADS, B_KV_HEADS)
    ql, kl, vl = split_qkv(p_lat[..., A_IN:], B_HEADS, B_KV_HEADS)
    ql, kl = axial_rope(ql, rope_ang), axial_rope(kl, rope_ang)
    sink_g = sink.reshape(B_KV_HEADS, B_HEADS // B_KV_HEADS)
    b_lat = banded_window_attention(ql, kl, vl, kc, vc, sink_g)
    out_lat = jnp.concatenate([a_lat, b_lat], axis=-1) @ w_out
    if not need_ctx:
        return out_lat, None
    b_ctx = context_attention(qc, kc, vc, sink_g)
    return out_lat, jnp.concatenate([a_ctx, b_ctx], axis=-1) @ w_out

def odd_mixer(u_ctx, u_lat, w_in, w_out, rpb, q_gain, k_gain, rope_ang, need_ctx):
    p_ctx = u_ctx @ w_in
    p_lat = u_lat @ w_in
    cq_c, ck_c, cv_c = split_qkv(p_ctx[..., :C_IN], C_HEADS, C_HEADS)
    cq_l, ck_l, cv_l = split_qkv(p_lat[..., :C_IN], C_HEADS, C_HEADS)
    c_lat = neighbourhood_attention(cq_l, ck_l, cv_l, ck_c, cv_c, rpb)
    dq_c, dk_c, dv_c = split_qkv(p_ctx[..., C_IN:], D_HEADS, D_KV_HEADS)
    dq_l, dk_l, dv_l = split_qkv(p_lat[..., C_IN:], D_HEADS, D_KV_HEADS)
    dq_c, dk_c = rms_norm(dq_c, q_gain), rms_norm(dk_c, k_gain)
    dq_l = axial_rope(rms_norm(dq_l, q_gain), rope_ang)
    dk_l = axial_rope(rms_norm(dk_l, k_gain), rope_ang)
    d_lat = global_block_attention(dq_l, dk_l, dv_l, dk_c, dv_c)
    out_lat = jnp.concatenate([c_lat, d_lat], axis=-1) @ w_out
    if not need_ctx:
        return out_lat, None
    c_ctx_o = context_attention(cq_c, ck_c, cv_c)
    d_ctx_o = context_attention(dq_c, dk_c, dv_c)
    return out_lat, jnp.concatenate([c_ctx_o, d_ctx_o], axis=-1) @ w_out

def first_inputs(seed: int = 0) -> dict:
    key = jax.random.key(seed)
    ks = iter(jax.random.split(key, 40))
    nrm = lambda shape, scale: scale * jax.random.normal(next(ks), shape, jnp.float32)
    unif = lambda shape, lo, hi: jax.random.uniform(next(ks), shape, jnp.float32, lo, hi)
    D = D_MODEL
    return {
        "x": nrm((BATCH, SEQ, D), 1.0),
        "c": nrm((BATCH, D), 1.0),
        "ctx": nrm((BATCH, CTX_LEN, D), 1.0),
        "c_ctx": nrm((D,), 1.0),
        "w_ada": nrm((DEPTH, D, 6 * D), 0.5 * D ** -0.5),
        "b_ada": nrm((DEPTH, 6 * D), 0.02),
        "g_pre_mix": 1.0 + nrm((DEPTH, D), 0.05),
        "g_post_mix": 1.0 + nrm((DEPTH, D), 0.05),
        "g_pre_ff": 1.0 + nrm((DEPTH, D), 0.05),
        "g_post_ff": 1.0 + nrm((DEPTH, D), 0.05),
        "w_in_even": nrm((N_EVEN, D, EVEN_IN), D ** -0.5),
        "w_in_odd": nrm((N_ODD, D, ODD_IN), D ** -0.5),
        "w_out": nrm((DEPTH, MIX_WIDTH, D), MIX_WIDTH ** -0.5),
        "w_ff1": nrm((DEPTH, D, D_FF), D ** -0.5),
        "w_ff2": nrm((DEPTH, D_FF, D), D_FF ** -0.5),
        "a_mu_prev": unif((N_EVEN, A_IN), 0.05, 0.45),
        "a_mu_next": unif((N_EVEN, A_IN), 0.05, 0.45),
        "a_w0": unif((N_EVEN, 2, A_WIDTH), -5.0, -0.5),
        "a_w2": nrm((N_EVEN, 2, DECAY_LORA, A_WIDTH), 0.1 * DECAY_LORA ** -0.5),
        "a_a0": nrm((N_EVEN, 2, A_WIDTH), 0.1),
        "a_a2": nrm((N_EVEN, 2, ICLR_LORA, A_WIDTH), 0.5 * ICLR_LORA ** -0.5),
        "a_g2": nrm((N_EVEN, GATE_LORA, A_WIDTH), GATE_LORA ** -0.5),
        "a_k_k": 0.85 + nrm((N_EVEN, A_WIDTH), 0.05),
        "a_k_a": 1.0 + nrm((N_EVEN, A_WIDTH), 0.05),
        "a_r_k": nrm((N_EVEN, A_HEADS, HEAD_DIM), 0.1),
        "a_gn_w": 1.0 + nrm((N_EVEN, A_WIDTH), 0.05),
        "a_gn_b": nrm((N_EVEN, A_WIDTH), 0.02),
        "b_sink": nrm((N_EVEN, B_HEADS), 0.5),
        "c_rpb": nrm((N_ODD, C_HEADS, 2 * NA_KH - 1, 2 * NA_KW - 1), 0.5),
        "d_q_gain": 1.0 + nrm((N_ODD, HEAD_DIM), 0.05),
        "d_k_gain": 1.0 + nrm((N_ODD, HEAD_DIM), 0.05),
    }

def first_block(x, c, ctx, c_ctx, w_ada, b_ada, g_pre_mix, g_post_mix, g_pre_ff, g_post_ff,
              w_in_even, w_in_odd, w_out, w_ff1, w_ff2,
              a_mu_prev, a_mu_next, a_w0, a_w2, a_a0, a_a2, a_g2, a_k_k, a_k_a, a_r_k, a_gn_w, a_gn_b,
              b_sink, c_rpb, d_q_gain, d_k_gain):
    rope_ang = axial_angles(x.shape[1])
    s_lat = jax.nn.silu(c)[:, None, :]
    s_ctx = jax.nn.silu(c_ctx)[None, None, :]
    h_lat, h_ctx = x, ctx
    for i in range(DEPTH):
        need_ctx = i < DEPTH - 1
        j = i // 2
        ml = jnp.split(s_lat @ w_ada[i] + b_ada[i], 6, axis=-1)
        mc = jnp.split(s_ctx @ w_ada[i] + b_ada[i], 6, axis=-1)
        u_lat = modulate(h_lat, g_pre_mix[i], ml[0], ml[1])
        u_ctx = modulate(h_ctx, g_pre_mix[i], mc[0], mc[1])
        if i % 2 == 0:
            a_prm = dict(mu_prev=a_mu_prev[j], mu_next=a_mu_next[j], w0=a_w0[j], w2=a_w2[j],
                         a0=a_a0[j], a2=a_a2[j], g2=a_g2[j], k_k=a_k_k[j], k_a=a_k_a[j],
                         r_k=a_r_k[j], gn_w=a_gn_w[j], gn_b=a_gn_b[j])
            o_lat, o_ctx = even_mixer(u_ctx, u_lat, w_in_even[j], w_out[i], a_prm, b_sink[j], rope_ang, need_ctx)
        else:
            o_lat, o_ctx = odd_mixer(u_ctx, u_lat, w_in_odd[j], w_out[i], c_rpb[j], d_q_gain[j], d_k_gain[j],
                                     rope_ang, need_ctx)
        h_lat = h_lat + ml[2] * rms_norm(o_lat, g_post_mix[i])
        f_lat = sqrelu_mlp(modulate(h_lat, g_pre_ff[i], ml[3], ml[4]), w_ff1[i], w_ff2[i])
        h_lat = h_lat + ml[5] * rms_norm(f_lat, g_post_ff[i])
        if need_ctx:
            h_ctx = h_ctx + mc[2] * rms_norm(o_ctx, g_post_mix[i])
            f_ctx = sqrelu_mlp(modulate(h_ctx, g_pre_ff[i], mc[3], mc[4]), w_ff1[i], w_ff2[i])
            h_ctx = h_ctx + mc[5] * rms_norm(f_ctx, g_post_ff[i])
    return h_lat


DEPTH_2 = 1

NSA_HEADS = 8
NSA_KV_GROUPS = 2
NSA_GROUP = NSA_HEADS // NSA_KV_GROUPS
NSA_HEAD_DIM = 64
ROPE_DIM = NSA_HEAD_DIM // 4
ROPE_THETA = 500000.0
CMP_BLOCK = 32
CMP_STRIDE = 16
CMP_HIDDEN = 256
SLC_BLOCK = 64
SLC_TOPK = 16
WINDOW_2 = 512
Q_BLOCK = 128

RET_HEADS = 4
RET_QK_DIM = 128
RET_V_DIM = 256
RET_CHUNK = 128
RET_ROPE_THETA = 10000.0

D_FF_2 = 2816
CONV_WIDTH = 3

EPS = 1e-6
NEG = -1e30

NSA_Q_W = NSA_HEADS * NSA_HEAD_DIM
NSA_KV_W = NSA_KV_GROUPS * NSA_HEAD_DIM
RET_QK_W = RET_HEADS * RET_QK_DIM
RET_V_W = RET_HEADS * RET_V_DIM
IN_SPLITS = (NSA_Q_W, 6 * NSA_KV_W, 3 * NSA_HEADS, RET_QK_W, RET_QK_W, RET_V_W, RET_V_W, 2 * D_MODEL)
IN_PROJ_W = sum(IN_SPLITS)


def rms_norm_2(x, w):
    xf = x.astype(jnp.float32)
    y = xf * lax.rsqrt(jnp.mean(xf * xf, axis=-1, keepdims=True) + EPS)
    return (y * w.astype(jnp.float32)).astype(x.dtype)

def rope(x, rot_dim, theta):
    S = x.shape[1]
    half = rot_dim // 2
    inv = jnp.power(jnp.float32(theta), -jnp.arange(half, dtype=jnp.float32) / half)
    ang = jnp.arange(S, dtype=jnp.float32)[:, None] * inv[None, :]
    cos = jnp.cos(ang)[None, :, None, :]
    sin = jnp.sin(ang)[None, :, None, :]
    xr = x[..., :rot_dim].astype(jnp.float32)
    x1, x2 = xr[..., :half], xr[..., half:]
    rot = jnp.concatenate([x1 * cos - x2 * sin, x1 * sin + x2 * cos], axis=-1).astype(x.dtype)
    return jnp.concatenate([rot, x[..., rot_dim:]], axis=-1)

def masked_softmax(s, mask):
    p = jax.nn.softmax(jnp.where(mask, s, NEG), axis=-1)
    return jnp.where(mask, p, 0.0)

def nsa_attention(q, k_cmp, v_cmp, k_slc, v_slc, k_win, v_win, gates,
                  pe_k, w1_k, w2_k, pe_v, w1_v, w2_v):
    B, S = q.shape[0], q.shape[1]
    H, G, dh = NSA_KV_GROUPS, NSA_GROUP, NSA_HEAD_DIM
    scale = dh ** -0.5
    pos = jnp.arange(S)
    qg = q.reshape(B, S, H, G, dh)

    n_cmp = (S - CMP_BLOCK) // CMP_STRIDE + 1
    cmp_start = np.arange(n_cmp) * CMP_STRIDE
    cmp_idx = cmp_start[:, None] + np.arange(CMP_BLOCK)[None, :]

    def compress(t, pe, w1, w2):
        blk = t[:, cmp_idx] + pe[:, None, :]
        blk = jnp.swapaxes(blk, 2, 3).reshape(B, n_cmp, H, CMP_BLOCK * dh)
        return jax.nn.gelu(blk @ w1) @ w2

    kc = compress(k_cmp, pe_k, w1_k, w2_k)
    vc = compress(v_cmp, pe_v, w1_v, w2_v)
    s_cmp = jnp.einsum('bshgd,bchd->bhgsc', qg, kc).astype(jnp.float32) * scale
    mask_cmp = jnp.asarray(cmp_start + CMP_BLOCK - 1)[None, :] <= pos[:, None]
    p_cmp = masked_softmax(s_cmp, mask_cmp)
    o_cmp = jnp.einsum('bhgsc,bchd->bshgd', p_cmp.astype(vc.dtype), vc)

    n_slc = S // SLC_BLOCK
    slc_start = np.arange(n_slc) * SLC_BLOCK
    overlap = np.clip(np.minimum(cmp_start[:, None] + CMP_BLOCK, slc_start[None, :] + SLC_BLOCK)
                      - np.maximum(cmp_start[:, None], slc_start[None, :]), 0, None) / CMP_BLOCK
    imp = jnp.einsum('bhgsc,cj->bhsj', p_cmp, jnp.asarray(overlap, dtype=jnp.float32))
    cur = (pos // SLC_BLOCK)[:, None]
    jb = jnp.arange(n_slc)[None, :]
    forced = (jb == 0) | (jb == cur) | (jb == cur - 1)
    valid = jb <= cur
    imp = jnp.where(forced, jnp.inf, jnp.where(valid, imp, -jnp.inf))
    top_n = min(SLC_TOPK, n_slc)
    _, sel = lax.top_k(imp, top_n)

    k_blocks = jnp.swapaxes(k_slc.reshape(B, n_slc, SLC_BLOCK, H, dh), 1, 3)
    k_blocks = jnp.swapaxes(k_blocks, 2, 3)
    v_blocks = jnp.swapaxes(jnp.swapaxes(v_slc.reshape(B, n_slc, SLC_BLOCK, H, dh), 1, 3), 2, 3)
    n_q = S // Q_BLOCK
    q_chunks = jnp.moveaxis(qg.reshape(B, n_q, Q_BLOCK, H, G, dh), 1, 0)
    sel_chunks = jnp.moveaxis(sel.reshape(B, H, n_q, Q_BLOCK, top_n), 2, 0)
    pos_chunks = pos.reshape(n_q, Q_BLOCK)
    gather = jax.vmap(jax.vmap(lambda blocks, ix: blocks[ix]))

    def selected_block(args):
        qb, ib, tb = args
        kg = gather(k_blocks, ib)
        vg = gather(v_blocks, ib)
        s = jnp.einsum('bqhgd,bhqnkd->bhgqnk', qb, kg).astype(jnp.float32) * scale
        kpos = ib[..., None] * SLC_BLOCK + jnp.arange(SLC_BLOCK)
        mask = (kpos <= tb[None, None, :, None, None]).reshape(B, H, 1, Q_BLOCK, top_n * SLC_BLOCK)
        p = masked_softmax(s.reshape(B, H, G, Q_BLOCK, top_n * SLC_BLOCK), mask)
        return jnp.einsum('bhgqm,bhqmd->bqhgd', p.astype(vg.dtype),
                          vg.reshape(B, H, Q_BLOCK, top_n * SLC_BLOCK, dh))

    o_slc = lax.map(selected_block, (q_chunks, sel_chunks, pos_chunks))
    o_slc = jnp.moveaxis(o_slc, 0, 1).reshape(B, S, H, G, dh)

    kw = jnp.pad(k_win, ((0, 0), (WINDOW_2, 0), (0, 0), (0, 0)))
    vw = jnp.pad(v_win, ((0, 0), (WINDOW_2, 0), (0, 0), (0, 0)))
    band_len = Q_BLOCK + WINDOW_2
    band = np.arange(n_q)[:, None] * Q_BLOCK + np.arange(band_len)[None, :]
    kb = kw[:, band]
    vb = vw[:, band]
    qb = qg.reshape(B, n_q, Q_BLOCK, H, G, dh)
    s_win = jnp.einsum('bnqhgd,bnkhd->bnhgqk', qb, kb).astype(jnp.float32) * scale
    qi = np.arange(Q_BLOCK)[:, None]
    ki = np.arange(band_len)[None, :]
    k_abs = np.arange(n_q)[:, None, None] * Q_BLOCK + ki[None] - WINDOW_2
    win_mask = ((ki > qi) & (ki <= qi + WINDOW_2))[None] & (k_abs >= 0)
    p_win = masked_softmax(s_win, jnp.asarray(win_mask)[None, :, None, None])
    o_win = jnp.einsum('bnhgqk,bnkhd->bnqhgd', p_win.astype(vb.dtype), vb).reshape(B, S, H, G, dh)

    g = gates.reshape(B, S, H, G, 3)
    o = g[..., 0:1] * o_cmp + g[..., 1:2] * o_slc + g[..., 2:3] * o_win
    return o.reshape(B, S, NSA_HEADS * dh)

def retention(q, k, v):
    B, S, H, dk = q.shape
    dv = v.shape[-1]
    C = RET_CHUNK
    n = S // C
    f32 = jnp.float32
    q = rope(q, dk, RET_ROPE_THETA).astype(f32)
    k = rope(k, dk, RET_ROPE_THETA).astype(f32) * (dk ** -0.5)
    v = v.astype(f32)
    log_gamma = jnp.log1p(-jnp.exp2(-5.0 - jnp.arange(H, dtype=f32)))
    idx = jnp.arange(C, dtype=f32)
    diff = idx[:, None] - idx[None, :]
    decay_in = jnp.where(diff >= 0, jnp.exp(log_gamma[:, None, None] * jnp.maximum(diff, 0.0)), 0.0)
    q_decay = jnp.exp(log_gamma[None, :] * (idx[:, None] + 1.0))
    k_decay = jnp.exp(log_gamma[None, :] * (C - 1.0 - idx[:, None]))
    chunk_decay = jnp.exp(log_gamma * C)
    qc = q.reshape(B, n, C, H, dk)
    kc = k.reshape(B, n, C, H, dk)
    vc = v.reshape(B, n, C, H, dv)
    scores = jnp.einsum('bnihd,bnjhd->bnhij', qc, kc) * decay_in
    o_inner = jnp.einsum('bnhij,bnjhe->bnihe', scores, vc)

    def step(state, xs):
        qn, kn, vn = xs
        cross = jnp.einsum('bihd,bhde->bihe', qn, state) * q_decay[None, :, :, None]
        state = state * chunk_decay[None, :, None, None] + jnp.einsum(
            'bjhd,bjhe->bhde', kn * k_decay[None, :, :, None], vn)
        return state, cross

    state0 = jnp.zeros((B, H, dk, dv), f32)
    _, o_cross = lax.scan(step, state0, (jnp.moveaxis(qc, 1, 0), jnp.moveaxis(kc, 1, 0), jnp.moveaxis(vc, 1, 0)))
    o = o_inner + jnp.moveaxis(o_cross, 0, 1)
    return o.reshape(B, S, H, dv)

def head_group_norm(o, w):
    mean = jnp.mean(o, axis=-1, keepdims=True)
    var = jnp.mean(jnp.square(o - mean), axis=-1, keepdims=True)
    return (o - mean) * lax.rsqrt(var + EPS) * w.astype(jnp.float32)

def causal_dwconv(u, w, b):
    S = u.shape[1]
    up = jnp.pad(u, ((0, 0), (CONV_WIDTH - 1, 0), (0, 0)))
    y = b
    for j in range(CONV_WIDTH):
        y = y + w[j] * up[:, j:j + S]
    return y

def second_inputs(seed: int = 0) -> dict:
    key = jax.random.key(seed)
    ks = jax.random.split(key, 20)
    f32 = jnp.float32
    L = DEPTH_2

    def nrm(k, shape, fan_in):
        return jax.random.normal(k, shape, f32) * (fan_in ** -0.5)

    def gain(k, shape):
        return 1.0 + 0.02 * jax.random.normal(k, shape, f32)

    return {
        'x': jax.random.normal(ks[0], (BATCH, SEQ, D_MODEL), f32),
        'norm_mix_w': gain(ks[1], (L, D_MODEL)),
        'w_in': nrm(ks[2], (L, D_MODEL, IN_PROJ_W), D_MODEL),
        'cmp_pe_k': 0.02 * jax.random.normal(ks[3], (L, CMP_BLOCK, NSA_HEAD_DIM), f32),
        'cmp_w1_k': nrm(ks[4], (L, CMP_BLOCK * NSA_HEAD_DIM, CMP_HIDDEN), CMP_BLOCK * NSA_HEAD_DIM),
        'cmp_w2_k': nrm(ks[5], (L, CMP_HIDDEN, NSA_HEAD_DIM), CMP_HIDDEN),
        'cmp_pe_v': 0.02 * jax.random.normal(ks[6], (L, CMP_BLOCK, NSA_HEAD_DIM), f32),
        'cmp_w1_v': nrm(ks[7], (L, CMP_BLOCK * NSA_HEAD_DIM, CMP_HIDDEN), CMP_BLOCK * NSA_HEAD_DIM),
        'cmp_w2_v': nrm(ks[8], (L, CMP_HIDDEN, NSA_HEAD_DIM), CMP_HIDDEN),
        'w_nsa_branch': nrm(ks[9], (L, NSA_Q_W, D_MODEL), NSA_Q_W),
        'ret_gn_w': gain(ks[10], (L, RET_HEADS, RET_V_DIM)),
        'w_ret_branch': nrm(ks[11], (L, RET_V_W, D_MODEL), RET_V_W),
        'w_mix_out': nrm(ks[12], (L, D_MODEL, D_MODEL), D_MODEL),
        'norm_ffn_w': gain(ks[13], (L, D_MODEL)),
        'w_ffn_up': nrm(ks[14], (L, D_MODEL, 2 * D_FF_2), D_MODEL),
        'ffn_conv_w': nrm(ks[15], (L, CONV_WIDTH, 2 * D_FF_2), CONV_WIDTH),
        'ffn_conv_b': 0.01 * jax.random.normal(ks[16], (L, 2 * D_FF_2), f32),
        'w_ffn_down': nrm(ks[17], (L, D_FF_2, D_MODEL), D_FF_2),
        'norm_final_w': gain(ks[18], (D_MODEL,)),
    }

def second_block(x, norm_mix_w, w_in, cmp_pe_k, cmp_w1_k, cmp_w2_k, cmp_pe_v, cmp_w1_v, cmp_w2_v,
              w_nsa_branch, ret_gn_w, w_ret_branch, w_mix_out, norm_ffn_w, w_ffn_up, ffn_conv_w,
              ffn_conv_b, w_ffn_down, norm_final_w):
    B, S, _ = x.shape
    split_at = [int(v) for v in np.cumsum(IN_SPLITS)[:-1]]
    for layer in range(DEPTH_2):
        h = rms_norm_2(x, norm_mix_w[layer])
        proj = h @ w_in[layer]
        q_nsa, kv_nsa, g_nsa, q_ret, k_ret, v_ret, g_ret, g_merge = jnp.split(proj, split_at, axis=-1)

        q_nsa = rope(q_nsa.reshape(B, S, NSA_HEADS, NSA_HEAD_DIM), ROPE_DIM, ROPE_THETA)
        kv = kv_nsa.reshape(B, S, 6, NSA_KV_GROUPS, NSA_HEAD_DIM)
        k_cmp, v_cmp = kv[:, :, 0], kv[:, :, 1]
        k_slc = rope(kv[:, :, 2], ROPE_DIM, ROPE_THETA)
        v_slc = kv[:, :, 3]
        k_win = rope(kv[:, :, 4], ROPE_DIM, ROPE_THETA)
        v_win = kv[:, :, 5]
        nsa_gates = jax.nn.sigmoid(g_nsa.reshape(B, S, NSA_HEADS, 3))
        o_a = nsa_attention(q_nsa, k_cmp, v_cmp, k_slc, v_slc, k_win, v_win, nsa_gates,
                            cmp_pe_k[layer], cmp_w1_k[layer], cmp_w2_k[layer],
                            cmp_pe_v[layer], cmp_w1_v[layer], cmp_w2_v[layer])
        y_a = o_a @ w_nsa_branch[layer]

        o_r = retention(q_ret.reshape(B, S, RET_HEADS, RET_QK_DIM),
                        k_ret.reshape(B, S, RET_HEADS, RET_QK_DIM),
                        v_ret.reshape(B, S, RET_HEADS, RET_V_DIM))
        o_r = head_group_norm(o_r, ret_gn_w[layer]) * jax.nn.silu(
            g_ret.reshape(B, S, RET_HEADS, RET_V_DIM).astype(jnp.float32))
        y_b = o_r.astype(x.dtype).reshape(B, S, RET_V_W) @ w_ret_branch[layer]

        gate_a, gate_b = jnp.split(jax.nn.sigmoid(g_merge), 2, axis=-1)
        x = x + (gate_a * y_a + gate_b * y_b) @ w_mix_out[layer]

        h = rms_norm_2(x, norm_ffn_w[layer])
        u = causal_dwconv(h @ w_ffn_up[layer], ffn_conv_w[layer], ffn_conv_b[layer])
        u_gate, u_val = jnp.split(u, 2, axis=-1)
        x = x + (jax.nn.silu(u_gate) * u_val) @ w_ffn_down[layer]
    return rms_norm_2(x, norm_final_w)


def setup_inputs(seed=0):
    out = dict(first_inputs(seed))
    for name, value in second_inputs(seed + 1).items():
        if name != "x":
            out[name + "_2"] = value
    return out


def reference(
    x, c, ctx, c_ctx, w_ada, b_ada, g_pre_mix, g_post_mix, g_pre_ff, g_post_ff, w_in_even,
    w_in_odd, w_out, w_ff1, w_ff2, a_mu_prev, a_mu_next, a_w0, a_w2, a_a0, a_a2, a_g2, a_k_k,
    a_k_a, a_r_k, a_gn_w, a_gn_b, b_sink, c_rpb, d_q_gain, d_k_gain, norm_mix_w_2, w_in_2,
    cmp_pe_k_2, cmp_w1_k_2, cmp_w2_k_2, cmp_pe_v_2, cmp_w1_v_2, cmp_w2_v_2, w_nsa_branch_2,
    ret_gn_w_2, w_ret_branch_2, w_mix_out_2, norm_ffn_w_2, w_ffn_up_2, ffn_conv_w_2,
    ffn_conv_b_2, w_ffn_down_2, norm_final_w_2,
):
    x = first_block(
        x, c, ctx, c_ctx, w_ada, b_ada, g_pre_mix, g_post_mix, g_pre_ff, g_post_ff, w_in_even,
        w_in_odd, w_out, w_ff1, w_ff2, a_mu_prev, a_mu_next, a_w0, a_w2, a_a0, a_a2, a_g2,
        a_k_k, a_k_a, a_r_k, a_gn_w, a_gn_b, b_sink, c_rpb, d_q_gain, d_k_gain,
    )
    return second_block(
        x, norm_mix_w_2, w_in_2, cmp_pe_k_2, cmp_w1_k_2, cmp_w2_k_2, cmp_pe_v_2, cmp_w1_v_2,
        cmp_w2_v_2, w_nsa_branch_2, ret_gn_w_2, w_ret_branch_2, w_mix_out_2, norm_ffn_w_2,
        w_ffn_up_2, ffn_conv_w_2, ffn_conv_b_2, w_ffn_down_2, norm_final_w_2,
    )


_drawn_inputs = setup_inputs


def setup_inputs(seed=0):
    import zlib

    import numpy as np

    out = dict(_drawn_inputs(seed))
    spreads = {}
    factors = {'a_w2': 8.0,
     'a_a0': 4.377,
     'a_gn_w': 3.195,
     'a_gn_b': 6.48,
     'b_sink': 8.0,
     'd_q_gain': 8.0,
     'd_k_gain': 8.0,
     'norm_mix_w_2': 4.207,
     'cmp_pe_k_2': 64.0,
     'cmp_pe_v_2': 64.0,
     'ret_gn_w_2': 8.0,
     'norm_ffn_w_2': 13.117,
     'ffn_conv_b_2': 26.881,
     'norm_final_w_2': 7.788,
     'c_rpb': 3.006}
    for name, (base, spread) in spreads.items():
        noise = np.random.default_rng([zlib.crc32(name.encode()), seed]).standard_normal(out[name].shape)
        drawn = base * np.exp(spread * noise) if base else spread * noise
        out[name] = jnp.asarray(drawn.astype(out[name].dtype))
    for name, factor in factors.items():
        out[name] = (out[name] * factor).astype(out[name].dtype)
    return out
```

```python
def program(nc, I, C, out):
    import math
    import concourse.bass as bass
    from concourse import mybir
    from contextlib import ExitStack

    F32 = mybir.dt.float32
    ALU = mybir.AluOpType
    ACT = mybir.ActivationFunctionType
    AX = mybir.AxisListType
    MUL, ADD, SUB, MAX = ALU.mult, ALU.add, ALU.subtract, ALU.max

    ctx = ExitStack()
    AREA = 53200
    arena = ctx.enter_context(nc.sbuf_tensor("arena", [128, AREA], F32))
    banks = [ctx.enter_context(nc.psum_tensor(f"bank{i}", [128, 512], F32)) for i in range(8)]

    class Queue:
        def __init__(self, name, chain):
            self.name, self.chain, self.ops, self.tail, self.owed = name, chain, [], None, []
            self.sem = ctx.enter_context(nc.semaphore("s_" + name))

        def add(self, fn, after=(), compute=True):
            waits = [t for t in after if t is not None] + self.owed
            self.owed = []
            if self.chain and compute and self.tail is not None:
                waits.append((self, self.tail))
            for t in waits:
                if t[0] != "dma":
                    t[0].ops[t[1]][2] = True
            self.ops.append([fn, waits, False])
            if compute:
                self.tail = len(self.ops) - 1
            return (self, len(self.ops) - 1)

        def last(self):
            return None if self.tail is None else (self, self.tail)

    PE, VE, SC, GP, SP = Queue("pe", False), Queue("ve", True), Queue("sc", True), Queue("gp", True), Queue("sp", False)
    ENG = [PE, VE, SC, GP]

    def done():
        return [q.last() for q in ENG if q.last() is not None]

    def barrier():
        t = done()
        for q in ENG:
            q.owed = [x for x in t if x[0] is not q] + q.owed

    n_sem = [0]

    def new_sem():
        n_sem[0] += 1
        return ctx.enter_context(nc.semaphore(f"s_d{n_sem[0]}"))

    def load(q, pairs, after=()):
        s = new_sem()
        for i, (dst, src) in enumerate(pairs):
            q.add(lambda e, dst=dst, src=src: e.dma_start(dst, src).then_inc(s, 16) and None,
                  after if i == 0 else (), compute=False)
        return ("dma", s, 16 * len(pairs))

    top = [0]

    def sb(*shape):
        n = 1
        for x in shape:
            n *= x
        a = arena[:, top[0]:top[0] + n]
        top[0] += n
        assert top[0] <= AREA, top[0]
        if len(shape) == 2:
            a = a.rearrange("p (a b) -> p a b", a=shape[0])
        elif len(shape) == 3:
            a = a.rearrange("p (a b c) -> p a b c", a=shape[0], b=shape[1])
        return a

    idle = [(b, ()) for b in banks]

    def take():
        assert idle, "no bank"
        return idle.pop(0)

    def give(b, *t):
        idle.append((b, t))

    def mm(o, l, r, start=True, stop=True, after=(), skip=False):
        return PE.add(lambda e: e.matmul(o, l, r, start=start, stop=stop, skip_group_check=skip), after)

    def tr(o, i, idn, after=()):
        return PE.add(lambda e: e.transpose(o, i, idn), after)

    def act(o, i, f, after=(), **k):
        return SC.add(lambda e: e.activation(o, i, f, **k), after)

    def tt(o, a, b, op, after=(), q=VE):
        return q.add(lambda e: e.tensor_tensor(o, a, b, op), after)

    def ts(o, a, s1, s2, op0, op1=None, after=(), q=VE):
        if op1 is None:
            return q.add(lambda e: e.tensor_scalar(o, a, s1, None, op0), after)
        return q.add(lambda e: e.tensor_scalar(o, a, s1, s2, op0, op1), after)

    def stt(o, a, s, b, op0, op1, after=(), q=VE):
        return q.add(lambda e: e.scalar_tensor_tensor(out=o, in0=a, scalar=s, in1=b, op0=op0, op1=op1), after)

    def cp(o, i, after=(), q=VE):
        if q is SC:
            return act(o, i, ACT.Copy, after)
        return q.add(lambda e: e.tensor_copy(o, i), after)

    def recip(o, i, after=()):
        return VE.add(lambda e: e.reciprocal(o, i), after)

    def rmax(o, i, after=()):
        return VE.add(lambda e: e.tensor_reduce(o, i, AX.X, MAX), after)

    def zero(o, after=(), q=GP, v=0.0):
        return q.add(lambda e: e.memset(o, v), after)

    flip = [0]

    def ev(o, i, after=()):
        flip[0] ^= 1
        return cp(o, i, after, SC if flip[0] else VE)

    H = sb(4, 1024)
    xt_at = top[0]
    XT = sb(8, 512)
    VC = sb(512)
    MOD = [sb(48, 2), sb(48, 2)]
    DER = sb(4, 8, 2)
    gb_at = top[0]
    GB = sb(2, 1024)
    SV = sb(8, 2)
    tiny = sb(64)
    ident = sb(128)
    bones = sb(128)
    NSLOT = 4
    RING = [sb(2048) for _ in range(NSLOT)]
    ring_sem = [new_sem() for _ in range(NSLOT)]
    ring_n = [0] * NSLOT
    ring_free = [()] * NSLOT
    ring_at = [0]

    class Slot:
        pass

    def wload(parts):
        s = ring_at[0] % NSLOT
        ring_at[0] += 1
        for i, (dst, src) in enumerate(parts(RING[s])):
            SP.add(lambda e, dst=dst, src=src, s=s: e.dma_start(dst, src).then_inc(ring_sem[s], 16) and None,
                   ring_free[s] if i == 0 else (), compute=False)
            ring_n[s] += 16
        w = Slot()
        w.i, w.ap, w.tok = s, RING[s], ("dma", ring_sem[s], ring_n[s])
        return w

    def wfree(w, t):
        ring_free[w.i] = (t,)

    def cols(W, c0, n, k0=0, nk=8):
        src = W[k0 * 128:(k0 + nk) * 128, c0:c0 + n].rearrange("(k p) f -> p k f", p=128)
        w = wload(lambda r: [(r[:, 0:nk * n].rearrange("p (k f) -> p k f", k=nk), src)])
        w.v = w.ap[:, 0:nk * n].rearrange("p (k f) -> p k f", k=nk)
        return w

    def cols_of(W, pieces, nk=8):
        tot = sum(n for _, n in pieces)

        def parts(r):
            v = r[:, 0:nk * tot].rearrange("p (k f) -> p k f", k=nk)
            at, res = 0, []
            for c0, n in pieces:
                res.append((v[:, :, at:at + n], W[0:nk * 128, c0:c0 + n].rearrange("(k p) f -> p k f", p=128)))
                at += n
            return res
        w = wload(parts)
        w.v = w.ap[:, 0:nk * tot].rearrange("p (k f) -> p k f", k=nk)
        return w

    def fm(w, f0, xT, n, after=()):
        b, free = take()
        nk = w.v.shape[1]
        for k in range(nk):
            t = mm(b[:, 0:n], w.v[:, k, f0:f0 + 128], xT[:, k, 0:n], k == 0, k == nk - 1,
                   [w.tok, *free, *after] if k == 0 else ())
        return b, t

    def tm(w, f0, nf, xT, tok, after=()):
        b, free = take()
        nk = w.v.shape[1]
        for k in range(nk):
            t = mm(b[:, 0:nf], xT[:, k, tok * 128:tok * 128 + 128], w.v[:, k, f0:f0 + nf], k == 0, k == nk - 1,
                   [w.tok, *free, *after] if k == 0 else ())
        return b, t

    t_id = load(SC, [(ident, C["ident"]), (bones, C["bones"])])
    t_h = load(SC, [(H[:, 0:2, :], I["x"][0].rearrange("(t p) d -> p t d", p=128)),
                    (H[:, 2:4, :], I["ctx"][0].rearrange("(t p) d -> p t d", p=128))])
    mark = top[0]
    VR = [sb(128) for _ in range(4)]
    place, row, pairs = {}, 0, []

    def vec(name, ap):
        nonlocal row
        n = ap.shape[0]
        place[name] = (row, n)
        done_ = 0
        while done_ < n:
            m = min(n - done_, 128 - row % 128)
            pairs.append((VR[row // 128][row % 128:row % 128 + m, :], ap[done_:done_ + m, :]))
            row += m
            done_ += m

    def rows(ap):
        return ap.rearrange("(n q) -> n q", q=128)

    vec("c", rows(I["c"][0]))
    vec("c_ctx", rows(I["c_ctx"]))
    for i in range(2):
        for g in ("g_pre_mix", "g_post_mix", "g_pre_ff", "g_post_ff", "b_ada"):
            vec(g + str(i), rows(I[g][i]))
    for g in ("a_mu_prev", "a_mu_next", "a_k_k", "a_k_a", "a_gn_w", "a_gn_b"):
        vec(g, rows(I[g][0]))
    for g in ("a_w0", "a_a0"):
        vec(g, I[g][0].rearrange("d (n q) -> (d n) q", q=128))
    vec("a_r_k", I["a_r_k"][0].rearrange("(n a) q -> n (a q)", a=2))
    for g in ("norm_mix_w_2", "norm_ffn_w_2", "ffn_conv_b_2"):
        vec(g, rows(I[g][0]))
    vec("norm_final_w_2", rows(I["norm_final_w_2"]))
    vec("ffn_conv_w_2", I["ffn_conv_w_2"][0].rearrange("j (n q) -> (j n) q", q=128))
    vec("ret_gn_w_2", I["ret_gn_w_2"][0].rearrange("h (n q) -> (h n) q", q=128))
    for g in ("cmp_pe_k_2", "cmp_pe_v_2"):
        vec(g, I[g][0].rearrange("(n a) q -> n (a q)", a=2))
    for g in ("d_q_gain", "d_k_gain"):
        place[g] = (row, 1)
        for a in range(2):
            pairs.append((VR[row // 128][row % 128:row % 128 + 1, a * 64:a * 64 + 64], I[g]))
        row += 1
    assert row <= 512
    t_v = load(SC, pairs)
    b, free = take()
    for i in range(4):
        n = min(128, row - i * 128)
        t = tr(b[:, i * 128:i * 128 + n], VR[i][0:n, :], ident[0:n, 0:n], [t_v, t_id, *free] if i == 0 else ())
    t = cp(VC[:, 0:row], b[:, 0:row], [t])
    give(b, t)

    def col(name, j=0, n=1):
        r = place[name][0]
        return VC[:, r + j:r + j + n]

    act(SV[:, :, 0], col("c", 0, 8), ACT.Silu, [t])
    t_sv = act(SV[:, :, 1], col("c_ctx", 0, 8), ACT.Silu)
    barrier()
    top[0] = mark

    def modulation(i, f0=0, f1=24):
        b, free = take()
        for s in range(f0, f1):
            w = cols(I["w_ada"][i], s * 256, 256)
            for f in range(2):
                j = 2 * s + f
                for k in range(8):
                    t = mm(b[:, 2 * j:2 * j + 2], w.v[:, k, f * 128:f * 128 + 128], SV[:, k, :], k == 0, k == 7,
                           [w.tok, t_sv, *free] if k == 0 else ())
            wfree(w, t)
        j0, j1 = 2 * f0, 2 * f1
        bias = col("b_ada" + str(i), j0, j1 - j0).unsqueeze(2).to_broadcast([128, j1 - j0, 2])
        t = tt(MOD[i][:, j0:j1, :], b[:, 2 * j0:2 * j1].rearrange("p (a s) -> p a s", s=2), bias, ADD, [t])
        give(b, t)
        return t

    def gains(i, g, part, d):
        return stt(DER[:, d, :, :], MOD[i][:, part * 8:part * 8 + 8, :], 1.0,
                   col(g + str(i), 0, 8).unsqueeze(2).to_broadcast([128, 8, 2]), ADD, MUL)

    def spread(vecs, dst, after=()):
        for half in range(2):
            b, free = take()
            for j in range(4):
                t = mm(b[:, j * 128:j * 128 + 128], vecs(half * 4 + j).to_broadcast([128, 128]), ident,
                       after=[*after, *free] if j == 0 else ())
            t = ev(dst[:, half * 512:half * 512 + 512], b[:, :], [t])
            give(b, t)
        return t

    def gate_rows(i, g, part, d, streams):
        t = tt(DER[:, d, :, :], MOD[i][:, part * 8:part * 8 + 8, :],
               col(g + str(i), 0, 8).unsqueeze(2).to_broadcast([128, 8, 2]), MUL, done())
        for s in range(streams):
            spread(lambda k: DER[:, d, k, s:s + 1], GB[:, s, :], [t])
        return [SC.last(), VE.last()]

    def rstd_of(x, n, eps, k, junk, after=()):
        a, b_ = tiny[:, 4 * k:4 * k + 1], tiny[:, 4 * k + 1:4 * k + 2]
        t = act(junk, x, ACT.Square, after, accum_out=a)
        t = ts(b_, a, 1.0 / n, eps, MUL, ADD, [t])
        t = act(b_, b_, ACT.Sqrt, [t])
        return recip(tiny[:, 4 * k + 2:4 * k + 3], b_, [t]), tiny[:, 4 * k + 2:4 * k + 3]

    def turn(src, ntok, dst, gain=None, shift=None, after=(), nf=8):
        for k in range(ntok):
            for q in range(0, nf, 4):
                b, free = take()
                for j in range(4):
                    t = tr(b[:, j * 128:j * 128 + 128], src[:, k, (q + j) * 128:(q + j) * 128 + 128], ident,
                           [*after, *free] if j == 0 else ())
                if gain is None:
                    tv = ev(dst[:, q:q + 4, k * 128:k * 128 + 128],
                            b[:, :].rearrange("p (a c) -> p a c", a=4), [t])
                    give(b, tv)
                    continue
                for j in range(4):
                    o, i = dst[:, q + j, k * 128:k * 128 + 128], b[:, j * 128:j * 128 + 128]
                    s = 0 if k < 2 else 1
                    g = gain(q + j, s)
                    if q:
                        t1 = act(o, i, ACT.Identity, [t], scale=g, bias=shift(q + j, s) if shift else 0.0)
                    elif shift:
                        t1 = ts(o, i, g, shift(q + j, s), MUL, ADD, [t])
                    else:
                        t1 = ts(o, i, g, None, MUL, None, [t])
                give(b, t1)
        return [SC.last(), VE.last()]

    def norm_turn(ntok, gain, shift, after=()):
        m = top[0]
        xn, junk = sb(ntok, 1024), sb(1024)
        for k in range(ntok):
            t, r = rstd_of(H[:, k, :], 1024, 1e-6, k, junk, [*after, *done()] if k == 0 else ())
            t = ts(xn[:, k, :], H[:, k, :], r, None, MUL, None, [t])
        r = turn(xn, ntok, XT, gain, shift, [t, *done()])
        barrier()
        top[0] = m
        return r

    def out_proj(parts, xT, ntok, O, after):
        for c in range(4):
            bs = [take() for _ in range(ntok)]
            for pi, (W, k0, nk) in enumerate(parts):
                w = cols(W, c * 256, 256, k0, nk)
                for k in range(nk):
                    for m_ in range(ntok):
                        b, free = bs[m_]
                        t = mm(b[:, 0:256], xT[:, k0 + k, m_ * 128:m_ * 128 + 128], w.v[:, k, :],
                               pi == 0 and k == 0, pi == len(parts) - 1 and k == nk - 1,
                               [w.tok, *free, *after] if k == 0 else ())
                wfree(w, t)
            for m_ in range(ntok):
                te = ev(O[:, m_, c * 256:c * 256 + 256], bs[m_][0][:, 0:256], [t])
                give(bs[m_][0], te)
        return [SC.last(), VE.last()]

    def add_normed(O, ntok, after):
        m = top[0]
        junk = sb(1024)
        for k in range(ntok):
            t, r = rstd_of(O[:, k, :], 1024, 1e-6, k, junk, after if k == 0 else ())
            t = stt(O[:, k, :], O[:, k, :], r, GB[:, 0 if k < 2 else 1, :], MUL, MUL, [t])
            t = tt(H[:, k, :], H[:, k, :], O[:, k, :], ADD, [t])
        top[0] = m
        return t

    def ffn(i, ntok):
        n = ntok * 128
        gains(i, "g_pre_ff", 4, 1)
        norm_turn(ntok, lambda f, s: DER[:, 1, f, s:s + 1], lambda f, s: MOD[i][:, 24 + f, s:s + 1])
        m = top[0]
        h1 = sb(32, n)
        for s in range(16):
            w = cols(I["w_ff1"][i], s * 256, 256)
            for f in range(2):
                b, t = fm(w, f * 128, XT, n, done() if s == 0 and f == 0 else ())
                j = 2 * s + f
                if j % 2:
                    t1 = act(h1[:, j, :], b[:, 0:n], ACT.Relu, [t])
                    tt(h1[:, j, :], h1[:, j, :], h1[:, j, :], MUL, [t1], q=GP)
                else:
                    t1 = act(h1[:, j, :], b[:, 0:n], ACT.Relu, [t])
                    tt(h1[:, j, :], h1[:, j, :], h1[:, j, :], MUL, [t1])
                give(b, t1)
            wfree(w, t)
        gate_rows(i, "g_post_ff", 5, 3, 1 if ntok == 2 else 2)
        O = sb(ntok, 1024)
        W = I["w_ff2"][i]
        r = out_proj([(W, 0, 8), (W, 8, 8), (W, 16, 8), (W, 24, 8)], h1, ntok, O, [VE.last(), GP.last()])
        add_normed(O, ntok, r)
        barrier()
        top[0] = m

    def attend(items, after):
        m = top[0]
        NP, NT = 4, 3
        P = [sb(512) for _ in range(NP)]
        PT = [sb(512) for _ in range(NT)]
        st = sb(NP, 8)
        p_free, pt_free = [()] * NP, [()] * NT
        live, obank = {}, [None]

        def first(i):
            it = items[i]
            n = it["n"]
            b, free = take()
            for x, (l, r, c0, c1) in enumerate(it["mms"]):
                t = mm(b[:, c0:c1], l, r, x == 0, x == len(it["mms"]) - 1,
                       [*free, *(after if i == 0 else ())] if x == 0 else ())
            s = st[:, i % NP, :]
            p = P[i % NP][:, 0:n]
            rmax(s[:, 0:1], b[:, 0:n], [t, *p_free[i % NP]])
            if it.get("sink") is not None:
                t = ts(s[:, 1:2], s[:, 0:1], it["sink"], -1.0, MAX, MUL)
            else:
                t = ts(s[:, 1:2], s[:, 0:1], -1.0, None, MUL)
            t = act(p, b[:, 0:n], ACT.Exp, [t], bias=s[:, 1:2], accum_out=s[:, 2:3])
            give(b, t)
            if it.get("sink") is not None:
                t = act(s[:, 3:4], it["sink"], ACT.Exp, bias=s[:, 1:2])
                t = tt(s[:, 2:3], s[:, 2:3], s[:, 3:4], ADD, [t])
            if it.get("m01") is not None:
                t = tt(p, p, it["m01"], MUL, [t])
            recip(s[:, 4:5], s[:, 2:3], [t])
            if it.get("gate") is not None:
                t = ts(p, p, s[:, 4:5], it["gate"], MUL, MUL)
            else:
                t = ts(p, p, s[:, 4:5], None, MUL)
            live[i] = t

        def second(i):
            it = items[i]
            b, free = take()
            for x, (c0, kw, _) in enumerate(it["kts"]):
                t = tr(b[0:kw, x * 128:x * 128 + 128], P[i % NP][:, c0:c0 + kw], ident,
                       [live[i], *free] if x == 0 else ())
            p_free[i % NP] = (t,)
            nk = len(it["kts"])
            kw = max(k for _, k, _ in it["kts"])
            t = act(PT[i % NT][0:kw, 0:nk * 128], b[0:kw, 0:nk * 128], ACT.Copy, [t, *pt_free[i % NT]])
            give(b, t)
            live[i] = t

        def third(i):
            it = items[i]
            if it["open"]:
                obank[0] = take()
            b, free = obank[0]
            po, oc = it["po"], it["oc"]
            for x, (c0, kw, v) in enumerate(it["kts"]):
                t = mm(b[po:po + 64, oc:oc + 128], v, PT[i % NT][0:kw, x * 128:x * 128 + 128],
                       it["begin"] and x == 0, it["end"] and x == len(it["kts"]) - 1,
                       [live[i], *free] if x == 0 else ())
            pt_free[i % NT] = (t,)
            if it["close"] is not None:
                tv = cp(it["close"], b[:, 0:256], [t])
                give(b, tv)

        for i in range(len(items) + 3):
            if i < len(items):
                first(i)
            if 0 <= i - 2 < len(items):
                second(i - 2)
            if 0 <= i - 3 < len(items):
                third(i - 3)
        barrier()
        top[0] = m

    def rotate(x, n, R, cos, sin, tmp, after):
        b, free = take()
        t = mm(b[:, 0:n], R, x, after=[*after, *free])
        t1 = tt(tmp, b[:, 0:n], sin, MUL, [t])
        give(b, t1)
        tt(x, x, cos, MUL)
        return tt(x, x, tmp, ADD)

    def head_sums(x, sq, n, after, scale=None):
        k = {} if scale is None else {"scale": scale}
        t = act(sq, x, ACT.Square, after, **k)
        b, free = take()
        t = mm(b[:, 0:n], bones, sq, after=[t, *free])
        return b, t

    stores = []

    modulation(0, 0, 8)
    gains(0, "g_pre_mix", 1, 0)
    norm_turn(4, lambda f, s: DER[:, 0, f, s:s + 1], lambda f, s: MOD[0][:, f, s:s + 1], [t_h])
    m_layer = top[0]
    OT = sb(8, 512)
    pA = sb(15, 512)
    m_b = top[0]
    qB = sb(4, 512)
    kB = sb(2, 512)
    vB = sb(4, 128)
    Rx, cosx, sinx, wmask = sb(128), sb(256), sb(256), sb(2, 256)
    snk = sb(8)
    mu0 = sb(15)
    t_c = load(SC, [(Rx, C["Rax"]), (cosx, C["cosax"]), (sinx, C["sinax"]), (wmask, C["wmask"]),
                    (snk[0:1, :], I["b_sink"])], done())
    tt(mu0, col("a_mu_prev", 0, 15), col("a_mu_next", 0, 15), ADD)
    ts(mu0, mu0, -1.0, 1.0, MUL, ADD)
    W = I["w_in_even"][0]
    first_w = done()
    for j in range(15):
        if j % 2 == 0:
            w = cols(W, j * 128, min(256, 1920 - j * 128))
        b, t = fm(w, (j % 2) * 128, XT, 512, first_w if j == 0 else ())
        if j % 2 or j == 14:
            wfree(w, t)
        o = pA[:, j, :].rearrange("p (s t) -> p s t", s=2)
        i = b[:, :].rearrange("p (s t) -> p s t", s=2)
        t = act(pA[:, j, :], b[:, :], ACT.Identity, [t], scale=mu0[:, j:j + 1])
        stt(o[:, :, 1:256], i[:, :, 0:255], col("a_mu_prev", j), o[:, :, 1:256], MUL, ADD, [t])
        t = stt(o[:, :, 0:255], i[:, :, 1:256], col("a_mu_next", j), o[:, :, 0:255], MUL, ADD)
        give(b, t)
    for j in range(4):
        if j % 2 == 0:
            w = cols(W, 1920 + j * 128, 256)
        b, t = fm(w, (j % 2) * 128, XT, 512)
        if j % 2:
            wfree(w, t)
        t = ts(qB[:, j, :], b[:, :], 0.125, None, MUL, None, [t])
        give(b, t)
    w = cols_of(W, [(2432, 64), (2432, 64), (2496, 64), (2496, 64)])
    for g in range(2):
        b, t = fm(w, g * 128, XT, 512)
        t1 = ev(kB[:, g, :], b[:, :], [t])
        give(b, t1)
    wfree(w, t)
    w = cols(W, 2560, 128)
    for k in range(4):
        b, t = tm(w, 0, 128, XT, k)
        t1 = ev(vB[:, k, :], b[:, 0:128], [t])
        give(b, t1)
    wfree(w, t)
    b, free = take()
    zero(tiny[0:1, 63:64], done(), VE)
    one = sb(128)
    t = zero(one, (), VE, 1.0)
    t = mm(b[:, 0:8], one[0:1, :], snk[0:1, :], after=[t, t_c, *free])
    snkb = sb(8)
    t = cp(snkb, b[:, 0:8], [t])
    give(b, t)
    m = top[0]
    tmp = sb(256)
    t = [t_c, *done()]
    for j in range(4):
        rotate(qB[:, j, 0:256], 256, Rx, cosx, sinx, tmp, t)
        t = [VE.last()]
    for g in range(2):
        rotate(kB[:, g, 0:256], 256, Rx, cosx, sinx, tmp, t)
        t = [VE.last()]
    items = []
    for pair in range(4):
        for h in (2 * pair, 2 * pair + 1):
            po, g = 64 * (h % 2), h // 4
            for qt in range(2):
                q = qB[po:po + 64, pair, qt * 128:qt * 128 + 128]
                items.append(dict(
                    n=512, mms=[(q, kB[po:po + 64, g, 0:512], 0, 512), (ident, wmask[:, qt, :], 0, 256)],
                    sink=snkb[:, h:h + 1], po=po, oc=qt * 128, begin=True, end=True,
                    kts=[(k * 128, 128, vB[:, k, g * 64:g * 64 + 64]) for k in range(4)],
                    open=h % 2 == 0 and qt == 0, close=OT[:, 4 + pair, 0:256] if h % 2 and qt else None))
        for h in (2 * pair, 2 * pair + 1):
            po, g = 64 * (h % 2), h // 4
            for qt in range(2):
                q = qB[po:po + 64, pair, 256 + qt * 128:256 + qt * 128 + 128]
                items.append(dict(
                    n=256, mms=[(q, kB[po:po + 64, g, 256:512], 0, 256)],
                    sink=snkb[:, h:h + 1], po=po, oc=qt * 128, begin=True, end=True,
                    kts=[(k * 128, 128, vB[:, 2 + k, g * 64:g * 64 + 64]) for k in range(2)],
                    open=h % 2 == 0 and qt == 0, close=OT[:, 4 + pair, 256:512] if h % 2 and qt else None))
    attend(items, done())
    modulation(0, 8, 24)
    barrier()
    top[0] = m_b

    CH0 = math.exp(-0.5)
    w2s, a2s, g2s = sb(512), sb(512), sb(512)
    scanm = sb(512)
    lvl = sb(2, 6, 64)
    tri = sb(2, 128)
    idst = sb(64)
    t_c = load(SC, [(w2s, I["a_w2"][0].rearrange("d l c -> (d l) c")), (a2s, I["a_a2"][0].rearrange("d l c -> (d l) c")),
                    (g2s, I["a_g2"][0]), (scanm, C["scanm"]), (lvl, C["lvl"]), (tri, C["tri"]), (idst, C["idst"])], done())
    ka1 = sb(4)
    ts(ka1, col("a_k_a", 0, 4), -1.0, 1.0, MUL, ADD)
    act(pA[:, 12, :], pA[:, 12, :], ACT.Tanh, done())
    act(pA[:, 14, :], pA[:, 14, :], ACT.Sigmoid)
    NCH, NSET = 4, 2
    S = []
    for _ in range(NSET):
        z = Slot()
        z.bd = [sb(NCH, 128) for _ in range(5)]
        z.tk = [sb(NCH, 128) for _ in range(3)]
        z.LT, z.LK = z.bd[1], z.bd[2]
        z.MK, z.MB, z.T, z.TT, z.X, z.W2, z.U2 = [sb(NCH, 64) for _ in range(7)]
        for a in z.bd:
            zero(a)
        z.free = [GP.last()]
        S.append(z)
    top_hi, top[0] = top[0], xt_at
    Vbd, FF, RT = sb(8, 128), [sb(8, 64) for _ in range(2)], [sb(8, 64) for _ in range(2)]
    Vst, kb = sb(8, 64), sb(512)
    assert top[0] <= xt_at + 4096
    top[0] = gb_at
    ar, be, ka = sb(8, 128), sb(512), sb(512)
    top[0] = top_hi
    ET = [sb(8, 128) for _ in range(2)]
    for a in ET:
        zero(a)
    vtmp = ET[0]
    PC = sb(2, 8)
    yacc = sb(512)
    sg, cu, ex, aa, kk = [sb(512) for _ in range(5)]
    Zs, Zb = sb(2, 2, 64), sb(2, 2, 128)
    zero(Zb)
    c8 = lambda a: a.rearrange("p (c t) -> p c t", t=64)
    HV = [(0, 64), (64, 128)]

    def unit(z, d, half):
        c0 = half * NCH
        al_b, be_b, ka_b, bp_b, kp_b = z.bd
        after = z.free
        arv, bev, kav = ar[:, c0:c0 + NCH, :], c8(be)[:, c0:c0 + NCH, :], c8(ka)[:, c0:c0 + NCH, :]
        pc = PC[:, d, c0:c0 + NCH].unsqueeze(2)
        dep = [*after, *done()]
        first = True
        for h0, h1 in HV:
            s = slice(h0, h1)
            cp(al_b[s, :, h0:h1], arv[s, :, 0:64], dep if first else (), SC)
            cp(be_b[s, :, h0:h1], bev[s], dep if first else (), GP)
            cp(ka_b[s, :, h0:h1], kav[s], (), GP)
            tt(bp_b[s, :, h0:h1], bev[s], pc[s].to_broadcast([64, NCH, 64]), MUL, dep if first else ())
            tt(kp_b[s, :, h0:h1], kav[s], pc[s].to_broadcast([64, NCH, 64]), MUL)
            first = False
        dep = [SC.last(), GP.last(), VE.last()]
        z.read = dep
        yield
        for n, (src, dst) in enumerate(zip((al_b, bp_b, kp_b), z.tk)):
            b, free = take()
            for c in range(NCH):
                t = tr(b[:, c * 128:c * 128 + 128], src[:, c, :], ident, [*dep, *free] if c == 0 else ())
            t1 = ev(dst, b[:, :].rearrange("p (c t) -> p c t", t=128), [t])
            give(b, t1)
        strict = tri[:, d, 0:64].unsqueeze(1)
        both = tri[:, d, :].unsqueeze(1)
        for src, L, M in ((be_b, z.LT, z.MB), (ka_b, z.LK, z.MK)):
            b, free = take()
            for c in range(NCH):
                t = mm(b[:, c * 128:c * 128 + 128], src[:, c, :], arv[:, c, :], after=[*dep, *free] if c == 0 else ())
            bv = b[:, :].rearrange("p (c t) -> p c t", t=128)
            for h0, h1 in HV:
                s = slice(h0, h1)
                tt(L[s, :, h0:h1], bv[s, :, 0:64], strict[s].to_broadcast([64, NCH, 64]), MUL, [t])
            t1 = tt(M, bv[:, :, 64:128], both[:, :, 64:128].to_broadcast([128, NCH, 64]), MUL)
            give(b, t1)
        yield
        Xb, Tb = al_b, bp_b
        cp(z.T, idst.unsqueeze(1).to_broadcast([128, NCH, 64]), (), GP)
        cp(z.TT, idst.unsqueeze(1).to_broadcast([128, NCH, 64]), (), GP)
        for h0, h1 in HV:
            cp(Tb[h0:h1, :, h0:h1], z.TT[h0:h1], [PE.last()], GP)
        r64 = lambda b: b[:, 0:NCH * 64].rearrange("p (c t) -> p c t", t=64)
        for l in range(6):
            b, free = take()
            dep = [SC.last(), GP.last(), VE.last(), *free]
            for c in range(NCH):
                t = mm(b[:, c * 64:c * 64 + 64], z.LT[:, c, :], z.T[:, c, :], after=dep if c == 0 else ())
            t1 = tt(z.X, r64(b), lvl[:, d, l, :].unsqueeze(1).to_broadcast([128, NCH, 64]), MUL, [t])
            give(b, t1)
            cp(Xb[0:64, :, 0:64], z.X[0:64], [t1], SC)
            cp(Xb[64:128, :, 64:128], z.X[64:128], [t1], GP)
            yield
            if l < 5:
                b, free = take()
                for c in range(NCH):
                    t = mm(b[:, c * 64:c * 64 + 64], Tb[:, c, :], z.X[:, c, :], after=[t1, GP.last(), *free] if c == 0 else ())
                t2 = tt(z.T, z.T, r64(b), SUB, [t])
                give(b, t2)
            b, free = take()
            for c in range(NCH):
                t = mm(b[:, c * 64:c * 64 + 64], Xb[:, c, :], z.TT[:, c, :],
                       after=[SC.last(), GP.last(), VE.last(), *free] if c == 0 else ())
            t2 = tt(z.TT, z.TT, r64(b), SUB, [t])
            give(b, t2)
            cp(Tb[0:64, :, 0:64], z.TT[0:64], [t2, PE.last()], SC)
            cp(Tb[64:128, :, 64:128], z.TT[64:128], [t2, PE.last()], GP)
            yield
        at, bt, kt = z.tk
        b, free = take()
        for c in range(NCH):
            cc = c0 + c
            t = mm(b[:, c * 64:c * 64 + 64], z.LK[:, c, :], Vst[:, cc, :], after=[*done(), *free] if c == 0 else ())
        t1 = cp(z.W2, r64(b), [t])
        give(b, t1)
        Gb, Ub = kp_b, be_b
        b, free = take()
        for c in range(NCH):
            t = mm(b[:, c * 128:c * 128 + 128], Tb[:, c, :], at[:, c, :], after=[SC.last(), GP.last(), *free] if c == 0 else ())
        t1 = act(Gb, b[:, :].rearrange("p (c t) -> p c t", t=128), ACT.Copy, [t], scale=-1.0)
        give(b, t1)
        b, free = take()
        for c in range(NCH):
            t = mm(b[:, c * 64:c * 64 + 64], Tb[:, c, :], z.W2[:, c, :], after=[VE.last(), *free] if c == 0 else ())
        t2 = ts(z.U2, r64(b), -1.0, None, MUL, None, [t])
        give(b, t2)
        for h0, h1 in HV:
            cp(Ub[h0:h1, :, h0:h1], z.U2[h0:h1], [t2], GP)
        yield
        dep = [SC.last(), VE.last(), GP.last()]
        b, free = take()
        for c in range(NCH):
            t = mm(b[:, c * 64:c * 64 + 64], Gb[:, c, :], z.MB[:, c, :], after=[*dep, *free] if c == 0 else ())
        t1 = tt(RT[d][:, c0:c0 + NCH, :], r64(b), arv[:, :, 64:128], ADD, [t])
        give(b, t1)
        b, free = take()
        for c in range(NCH):
            t = mm(b[:, c * 128:c * 128 + 128], Gb[:, c, :], bt[:, c, :], after=free if c == 0 else ())
        for c in range(NCH):
            t1 = stt(ET[d][:, c0 + c, :], ident, PC[:, d, c0 + c:c0 + c + 1], b[:, c * 128:c * 128 + 128], MUL, ADD, [t])
        give(b, t1)
        b, free = take()
        for c in range(NCH):
            mm(b[:, c * 64:c * 64 + 64], kt[:, c, :], Vst[:, c0 + c, :], True, False, free if c == 0 else ())
            t = mm(b[:, c * 64:c * 64 + 64], bt[:, c, :], z.U2[:, c, :], False, True)
        t1 = act(FF[d][:, c0:c0 + NCH, :], r64(b), ACT.Copy, [t])
        give(b, t1)
        b, free = take()
        for c in range(NCH):
            mm(b[:, c * 64:c * 64 + 64], Vbd[:, c0 + c, :], z.MK[:, c, :], True, False, free if c == 0 else ())
            t = mm(b[:, c * 64:c * 64 + 64], Ub[:, c, :], z.MB[:, c, :], False, True)
        y = yacc[:, c0 * 64:c0 * 64 + NCH * 64]
        t1 = cp(y, b[:, 0:NCH * 64], [t]) if d == 0 else tt(y, y, b[:, 0:NCH * 64], ADD, [t])
        give(b, t1)
        z.free = done()
        yield

    for p in range(4):
        r, k, v = pA[:, p, :], pA[:, 4 + p, :], pA[:, 8 + p, :]
        b, t = head_sums(k, sg, 512, done(), col("a_k_k", p))
        t = act(sg, b[:, :], ACT.Sqrt, [t])
        give(b, t)
        ts(sg, sg, 1e-12, None, MAX, None, [t])
        recip(sg, sg)
        stt(kk, k, col("a_k_k", p), sg, MUL, MUL)
        for h0, h1 in HV:
            cp(vtmp[h0:h1, :, h0:h1], c8(v)[h0:h1], done() if h0 == 0 else (), GP)
        for q in range(2):
            b, free = take()
            for c in range(4):
                t = tr(b[:, c * 128:c * 128 + 128], vtmp[:, 4 * q + c, :], ident, [GP.last(), *free] if c == 0 else ())
            t = cp(Vbd[:, 4 * q:4 * q + 4, :], b[:, :].rearrange("p (c t) -> p c t", t=128), [t, *done()])
            give(b, t)
        for h0, h1 in HV:
            t = cp(Vst[h0:h1], Vbd[h0:h1, :, h0:h1])
        for d in range(2):
            s = slice(64 * d, 64 * d + 64)
            b, free = take()
            t = mm(b[:, :], w2s[s, p * 128:p * 128 + 128], pA[s, 12, :], after=[t_c, *done(), *free])
            t = act(sg, b[:, :], ACT.Sigmoid, [t, *done()], bias=col("a_w0", 4 * d + p))
            give(b, t)
            b, free = take()
            t2 = mm(b[:, :], a2s[s, p * 128:p * 128 + 128], pA[s, 13, :], after=free)
            t2 = act(aa, b[:, :], ACT.Sigmoid, [t2], bias=col("a_a0", 4 * d + p))
            give(b, t2)
            VE.add(lambda e: e.tensor_tensor_scan(cu, scanm, sg, 0.0, MUL, ADD), [t, t_c])
            tot = c8(cu)[:, :, 63:64]
            if d == 0:
                t = tt(ex, cu, sg, SUB)
            else:
                tt(c8(ex), tot.to_broadcast([128, 8, 64]), c8(cu), SUB)
            t = act(PC[:, d, :], c8(cu)[:, :, 63], ACT.Exp, [VE.last()], scale=-CH0)
            if d == 1:
                t = tt(cu, ex, sg, ADD, [t])
            iv, kd = sg, aa
            act(iv, cu, ACT.Exp, [VE.last()], scale=CH0)
            act(cu, cu, ACT.Exp, scale=-CH0)
            t = act(ex, ex, ACT.Exp, scale=-CH0)
            tt(be, kk, aa, MUL, [t])
            ts(kd, aa, col("a_k_a", p), ka1[:, p:p + 1], MUL, ADD, [t])
            tt(kd, kd, k, MUL)
            if d == 0:
                cp(kb, kd)
            else:
                tt(kb, kb, kd, ADD)
            tt(ar[:, :, 0:64], c8(ex), c8(kk), MUL)
            tt(ar[:, :, 64:128], c8(cu), c8(r), MUL)
            tt(be, be, iv, MUL)
            tt(ka, kd, iv, MUL)
            g = [unit(S[0], d, 0), unit(S[1], d, 1)]
            while g:
                for x in list(g):
                    try:
                        next(x)
                    except StopIteration:
                        g.remove(x)
        order = [[4, 5, 6, 7, 0, 1, 2, 3], [7, 6, 5, 4, 3, 2, 1, 0]]
        for i in range(8):
            zs, zn = Zs[:, i % 2], Zs[:, (i + 1) % 2]
            if i == 0:
                for d in range(2):
                    cp(zn[:, d, :], FF[d][:, order[d][0], :], done() if d == 0 else ())
            else:
                b, free = take()
                for d in range(2):
                    t = mm(b[:, d * 64:d * 64 + 64], ET[d][:, order[d][i], :], zs[:, d, :],
                           after=[VE.last(), *free] if d == 0 else ())
                b2, free2 = take()
                for d in range(2):
                    t2 = mm(b2[:, d * 64:d * 64 + 64], Zb[:, i % 2, d, :], RT[d][:, order[d][i], :],
                            after=[GP.last(), *free2] if d == 0 else ())
                for d in range(2):
                    t = tt(zn[:, d, :], b[:, d * 64:d * 64 + 64], FF[d][:, order[d][i], :], ADD, [t])
                give(b, t)
                for d in range(2):
                    y = yacc[:, order[d][i] * 64:order[d][i] * 64 + 64]
                    t2 = tt(y, y, b2[:, d * 64:d * 64 + 64], ADD, [t2])
                give(b2, t2)
            if i < 7:
                for h0, h1 in HV:
                    cp(Zb[h0:h1, (i + 1) % 2, :, h0:h1], zn[h0:h1], [VE.last(), PE.last()], GP)
        b, free = take()
        t = mm(b[:, :], bones, yacc, after=[*done(), *free])
        t = stt(yacc, b[:, :], -1.0 / 64, yacc, MUL, ADD, [t])
        give(b, t)
        b, t = head_sums(yacc, sg, 512, [t])
        t = ts(sg, b[:, :], 1.0 / 64, 64e-5, MUL, ADD, [t])
        give(b, t)
        t = act(sg, sg, ACT.Sqrt, [t])
        recip(sg, sg, [t])
        tt(yacc, yacc, sg, MUL)
        ts(yacc, yacc, col("a_gn_w", p), col("a_gn_b", p), MUL, ADD)
        t = stt(kb, kb, col("a_r_k", p), r, MUL, MUL)
        b, free = take()
        t = mm(b[:, :], bones, kb, after=[t, *free])
        t = tt(sg, b[:, :], v, MUL, [t])
        give(b, t)
        tt(yacc, yacc, sg, ADD)
        b, free = take()
        t = mm(b[:, :], g2s[:, p * 128:p * 128 + 128], pA[:, 14, :], after=free)
        t = tt(OT[:, p, :], b[:, :], yacc, MUL, [t])
        give(b, t)
    barrier()
    top[0] = m_layer + 8 * 512
    gate_rows(0, "g_post_mix", 2, 2, 2)
    O = sb(4, 1024)
    r = out_proj([(I["w_out"][0], 0, 8)], OT, 4, O, done())
    add_normed(O, 4, r)
    barrier()
    top[0] = m_layer
    ffn(0, 4)

    modulation(1)
    gains(1, "g_pre_mix", 1, 0)
    norm_turn(4, lambda f, s: DER[:, 0, f, s:s + 1], lambda f, s: MOD[1][:, f, s:s + 1])
    OT = sb(8, 256)
    m_c = top[0]
    Rx, cosx, sinx, cmask, flipm = sb(128), sb(256), sb(256), sb(256), sb(128)
    t_c = load(SC, [(Rx, C["Rax"]), (cosx, C["cosax"]), (sinx, C["sinax"]), (cmask, C["cmask"]), (flipm, C["flip"])], done())
    bias = sb(2, 8, 256)
    rp = I["c_rpb"]
    pairs = []
    for qt in range(2):
        for rq in range(2):
            for h in range(8):
                src = bass.AP(tensor=rp.tensor, offset=rp.offset + (h * 15 + 7 - (2 * qt + rq)) * 31 + 15 - 63,
                              ap=[[1, 64], [31, 4], [1, 64]])
                pairs.append((bias[rq * 64:rq * 64 + 64, qt, h, :].rearrange("p (a b) -> p a b", a=4), src))
    t_b = load(SC, pairs)
    qC, kC, vC = sb(4, 256), sb(4, 512), sb(4, 512)
    qD, kD, vD = sb(4, 256), sb(2, 512), sb(4, 128)
    W = I["w_in_odd"][0]
    first_w = done()
    for j in range(4):
        if j % 2 == 0:
            w = cols(W, j * 128, 256)
        b, t = fm(w, (j % 2) * 128, XT, 256, first_w if j == 0 else ())
        if j % 2:
            wfree(w, t)
        t = ts(qC[:, j, :], b[:, 0:256], 0.125, None, MUL, None, [t])
        give(b, t)
    for j in range(4):
        if j % 2 == 0:
            w = cols(W, 512 + j * 128, 256)
        b, t = fm(w, (j % 2) * 128, XT, 512)
        if j % 2:
            wfree(w, t)
        t = ev(kC[:, j, :], b[:, :], [t])
        give(b, t)
    for j in range(2):
        w = cols(W, 1024 + j * 256, 256)
        for k in range(4):
            b, t = tm(w, 0, 256, XT, k)
            t1 = ev(vC[:, k, j * 256:j * 256 + 256], b[:, 0:256], [t])
            give(b, t1)
        wfree(w, t)
    for j in range(4):
        if j % 2 == 0:
            w = cols(W, 1536 + j * 128, 256)
        b, t = fm(w, (j % 2) * 128, XT, 256)
        if j % 2:
            wfree(w, t)
        t = ev(qD[:, j, :], b[:, 0:256], [t])
        give(b, t)
    w = cols_of(W, [(2048, 64), (2048, 64), (2112, 64), (2112, 64)])
    for g in range(2):
        b, t = fm(w, g * 128, XT, 512)
        t1 = ev(kD[:, g, :], b[:, :], [t])
        give(b, t1)
    wfree(w, t)
    w = cols(W, 2176, 128)
    for k in range(4):
        b, t = tm(w, 0, 128, XT, k)
        t1 = ev(vD[:, k, :], b[:, 0:128], [t])
        give(b, t1)
    wfree(w, t)
    for qt in range(2):
        tt(bias[:, qt, :, :], bias[:, qt, :, :], cmask.unsqueeze(1).to_broadcast([128, 8, 256]), ADD, [t_c, t_b], q=GP)
    m = top[0]
    tmp, sq = sb(512), sb(512)
    qg = sb(1)
    ts(qg, col("d_q_gain"), 0.125, None, MUL)
    for x, n, g in [(qD[:, j, :], 256, qg) for j in range(4)] + [(kD[:, j, :], 512, col("d_k_gain")) for j in range(2)]:
        b, t = head_sums(x, sq[:, 0:n], n, done())
        t = ts(tmp[:, 0:n], b[:, 0:n], 1.0 / 64, 1e-6, MUL, ADD, [t])
        give(b, t)
        t = act(tmp[:, 0:n], tmp[:, 0:n], ACT.Sqrt, [t])
        recip(tmp[:, 0:n], tmp[:, 0:n], [t])
        stt(x, x, g, tmp[:, 0:n], MUL, MUL)
        rotate(x[:, 0:256], 256, Rx, cosx, sinx, tmp[:, 0:256], [t_c, VE.last()])
    barrier()
    top[0] = m
    items = []
    for kind in "CD":
        for pair in range(4):
            for h in (2 * pair, 2 * pair + 1):
                po, g = 64 * (h % 2), h // 4
                for qt in range(2):
                    s = slice(qt * 128, qt * 128 + 128)
                    if kind == "C":
                        mms = [(qC[po:po + 64, pair, s], kC[po:po + 64, pair, :], 0, 512), (flipm, bias[:, qt, h, :], 0, 256)]
                        kts = [(k * 128, 128, vC[:, k, h * 64:h * 64 + 64]) for k in range(4)]
                    else:
                        mms = [(qD[po:po + 64, pair, s], kD[po:po + 64, g, :], 0, 512)]
                        kts = [(k * 128, 128, vD[:, k, g * 64:g * 64 + 64]) for k in range(4)]
                    dst = OT[:, (0 if kind == "C" else 4) + pair, :]
                    items.append(dict(n=512, mms=mms, po=po, oc=qt * 128, begin=True, end=True, kts=kts,
                                      open=h % 2 == 0 and qt == 0, close=dst if h % 2 and qt else None))
    attend(items, done())
    top[0] = m_c
    gate_rows(1, "g_post_mix", 2, 2, 1)
    O = sb(2, 1024)
    r = out_proj([(I["w_out"][1], 0, 8)], OT, 2, O, done())
    add_normed(O, 2, r)
    barrier()
    top[0] = m_layer
    ffn(1, 2)

    norm_turn(2, lambda f, s: col("norm_mix_w_2", f), None)
    W = I["w_in_2"][0]
    Z = sb(2, 1024)
    ga = sb(2, 2048)
    m_n = top[0]
    first_w = done()
    for j in range(8):
        w = cols(W, 4376 + j * 256, 256)
        for k in range(2):
            b, t = tm(w, 0, 256, XT, k, first_w if j == 0 else ())
            t1 = act(ga[:, k, j * 256:j * 256 + 256], b[:, 0:256], ACT.Sigmoid, [t])
            give(b, t1)
        wfree(w, t)
    oN = sb(4, 256)
    Rn, cosn, sinn, caus, cm, c01 = sb(128), sb(256), sb(256), sb(128), sb(2, 16), sb(2, 16)
    w2k, w2v = sb(2, 128), sb(2, 64)
    t_c = load(SC, [(Rn, C["Rnsa"]), (cosn, C["cosnsa"]), (sinn, C["sinnsa"]), (caus, C["caus"]), (cm, C["cmpm"]), (c01, C["cmp01"]),
                    (w2k[:, :, 0:64], I["cmp_w2_k_2"][0].rearrange("(t p) d -> p t d", p=128)),
                    (w2k[:, :, 64:128], I["cmp_w2_k_2"][0].rearrange("(t p) d -> p t d", p=128)),
                    (w2v, I["cmp_w2_v_2"][0].rearrange("(t p) d -> p t d", p=128))], done())
    q = sb(4, 256)
    for j in range(4):
        if j % 2 == 0:
            w = cols(W, j * 128, 256)
        b, t = fm(w, (j % 2) * 128, XT, 256)
        if j % 2:
            wfree(w, t)
        t = ts(q[:, j, :], b[:, 0:256], 0.125, None, MUL, None, [t])
        give(b, t)
    kv = {}
    for nm, c0 in (("kc", 512), ("vc", 640), ("ks", 768), ("kw", 1024)):
        kv[nm] = sb(2, 256)
        w = cols_of(W, [(c0, 64), (c0, 64), (c0 + 64, 64), (c0 + 64, 64)])
        for g in range(2):
            b, t = fm(w, g * 128, XT, 256)
            t1 = ev(kv[nm][:, g, :], b[:, 0:256], [t])
            give(b, t1)
        wfree(w, t)
    vsw = sb(2, 256)
    w = cols_of(W, [(896, 128), (1152, 128)])
    for k in range(2):
        b, t = tm(w, 0, 256, XT, k)
        t1 = ev(vsw[:, k, :], b[:, 0:256], [t])
        give(b, t1)
    wfree(w, t)
    gt = sb(2, 24)
    w = cols(W, 1280, 24)
    for k in range(2):
        b, t = tm(w, 0, 24, XT, k)
        t1 = act(gt[:, k, :], b[:, 0:24], ACT.Sigmoid, [t])
        give(b, t1)
    wfree(w, t)
    tmp = sb(256)
    t = [t_c, *done()]
    for x in [q[:, j, :] for j in range(4)] + [kv[n_][:, g, :] for n_ in ("ks", "kw") for g in range(2)]:
        rotate(x, 256, Rn, cosn, sinn, tmp, t)
        t = [VE.last()]
    blk = sb(16, 2, 15)
    hid, hidT = sb(256), sb(2, 30)
    kcT, vcm = sb(30), sb(2, 64)
    for nm, pe, w1 in (("kc", "cmp_pe_k_2", "cmp_w1_k_2"), ("vc", "cmp_pe_v_2", "cmp_w1_v_2")):
        dep = done()
        for h in range(2):
            v = kv[nm][:, h, :].rearrange("p (c s) -> p s c", s=16)
            for par in range(2):
                s = slice(par * 64, par * 64 + 64)
                for e_ in range(2):
                    tt(blk[s, e_ * 8:e_ * 8 + 8, h, :], v[s, par::2, e_:e_ + 15],
                       col(pe, e_ * 8, 8)[s].unsqueeze(2).to_broadcast([64, 8, 15]), ADD, dep)
        b, free = take()
        for half in range(2):
            w = cols(I[w1][0], 0, 256, half * 8, 8)
            for k in range(8):
                t = mm(b[0:30, 0:256], blk[:, half * 8 + k, :, :], w.v[:, k, :], half == 0 and k == 0, half == 1 and k == 7,
                       [w.tok, VE.last(), *free] if k == 0 else ())
            wfree(w, t)
        t = act(hid[0:30, :], b[0:30, 0:256], ACT.Gelu_apprx_tanh, [t])
        give(b, t)
        b, free = take()
        for k in range(2):
            t = tr(b[:, k * 32:k * 32 + 30], hid[0:30, k * 128:k * 128 + 128], ident[0:30, 0:30], [t, *free])
        t = cp(hidT, b[:, 0:64].rearrange("p (k c) -> p k c", k=2)[:, :, 0:30], [t])
        give(b, t)
        b, free = take()
        if nm == "kc":
            for k in range(2):
                t = mm(b[:, 0:30], w2k[:, k, :], hidT[:, k, :], k == 0, k == 1, [t, t_c, *free])
            t = cp(kcT, b[:, 0:30], [t])
        else:
            for h in range(2):
                for k in range(2):
                    t = mm(b[0:15, h * 64:h * 64 + 64], hidT[:, k, h * 15:h * 15 + 15], w2v[:, k, :], k == 0, k == 1, [t, t_c, *free])
            t = cp(vcm[0:15], b[0:15, 0:128].rearrange("p (h d) -> p h d", h=2), [t])
        give(b, t)
    items = []
    for pair in range(4):
        for h in (2 * pair, 2 * pair + 1):
            po, g = 64 * (h % 2), h // 4
            for qt in range(2):
                s = slice(qt * 128, qt * 128 + 128)
                ql = q[po:po + 64, pair, s]
                n = 128 * (qt + 1)
                base = dict(po=po, oc=qt * 128, open=False, close=None, begin=False, end=False)
                items.append({**base, "n": 15, "mms": [(ql, kcT[po:po + 64, g * 15:g * 15 + 15], 0, 15), (ident, cm[:, qt, 0:15], 0, 15)],
                              "m01": c01[:, qt, 0:15], "gate": gt[:, qt, 3 * h:3 * h + 1], "kts": [(0, 15, vcm[0:15, g, :])],
                              "begin": True, "open": h % 2 == 0 and qt == 0})
                for bi, (kn, vo) in enumerate((("ks", 0), ("kw", 128))):
                    items.append({**base, "n": n, "mms": [(ql, kv[kn][po:po + 64, g, 0:n], 0, n), (ident, caus, n - 128, n)],
                                  "gate": gt[:, qt, 3 * h + 1 + bi:3 * h + 2 + bi],
                                  "kts": [(k * 128, 128, vsw[:, k, vo + g * 64:vo + g * 64 + 64]) for k in range(qt + 1)],
                                  "end": bi == 1, "close": oN[:, pair, :] if bi == 1 and h % 2 and qt else None})
    attend(items, done())

    def branch(Wb, xT, nk, g0, add, after):
        for c in range(4):
            bs = [take() for _ in range(2)]
            w = cols(Wb, c * 256, 256, 0, nk)
            for k in range(nk):
                for m_ in range(2):
                    b, free = bs[m_]
                    t = mm(b[:, 0:256], xT[:, k, m_ * 128:m_ * 128 + 128], w.v[:, k, :], k == 0, k == nk - 1,
                           [w.tok, *free, *after] if k == 0 else ())
            wfree(w, t)
            for m_ in range(2):
                g = ga[:, m_, g0 + c * 256:g0 + c * 256 + 256]
                z = Z[:, m_, c * 256:c * 256 + 256]
                if add:
                    t1 = tt(g, bs[m_][0][:, 0:256], g, MUL, [t])
                    tt(z, z, g, ADD)
                else:
                    t1 = tt(z, bs[m_][0][:, 0:256], g, MUL, [t])
                give(bs[m_][0], t1)

    branch(I["w_nsa_branch_2"][0], oN, 4, 0, False, done())
    barrier()
    top[0] = m_n
    Rr, cosr, sinr = sb(128), sb(256), sb(256)
    dec = sb(4, 384)
    gw = sb(1024)
    t_c = load(SC, [(Rr, C["Rret"]), (cosr, C["cosret"]), (sinr, C["sinret"]), (dec, C["dec"])], done())
    spread(lambda k: col("ret_gn_w_2", k), gw, done())
    qr, kr, vr, gr = sb(4, 256), sb(4, 256), sb(2, 1024), sb(2, 1024)
    for dst, c0, sc in ((qr, 1304, 1.0), (kr, 1816, 128 ** -0.5)):
        for j in range(4):
            if j % 2 == 0:
                w = cols(W, c0 + j * 128, 256)
            b, t = fm(w, (j % 2) * 128, XT, 256)
            if j % 2:
                wfree(w, t)
            t = ts(dst[:, j, :], b[:, 0:256], sc, None, MUL, None, [t, *done()])
            give(b, t)
    for dst, c0, f in ((vr, 2328, ACT.Copy), (gr, 3352, ACT.Silu)):
        for j in range(4):
            w = cols(W, c0 + j * 256, 256)
            for k in range(2):
                b, t = tm(w, 0, 256, XT, k)
                t1 = act(dst[:, k, j * 256:j * 256 + 256], b[:, 0:256], f, [t])
                give(b, t1)
            wfree(w, t)
    tmp = sb(256)
    t = [t_c, *done()]
    for x in [qr[:, j, :] for j in range(4)] + [kr[:, j, :] for j in range(4)]:
        rotate(x, 256, Rr, cosr, sinr, tmp, t)
        t = [VE.last()]
    ST = [sb(384) for _ in range(2)]
    oR, junk = sb(2, 1024), sb(256)
    st_free = [(), ()]
    for h in range(4):
        s = ST[h % 2]
        b, free = take()
        mm(b[:, 0:256], kr[:, h, 0:128], qr[:, h, :], after=[*done(), *free])
        t = mm(b[:, 256:384], kr[:, h, 128:256], qr[:, h, 128:256])
        t = tt(s, b[:, 0:384], dec[:, h, :], MUL, [t, t_c, *st_free[h % 2]])
        give(b, t)
        for i in range(2):
            b, free = take()
            v = lambda k: vr[:, k, h * 256:h * 256 + 256]
            if i == 0:
                t1 = mm(b[:, 0:256], s[:, 0:128], v(0), after=[t, *free])
            else:
                mm(b[:, 0:256], s[:, 128:256], v(0), True, False, [t, *free])
                t1 = mm(b[:, 0:256], s[:, 256:384], v(1), False, True)
                st_free[h % 2] = (t1,)
            o = oR[:, i, h * 256:h * 256 + 256]
            k0 = 4 * (2 * h + i)
            a0, a1, a2 = [tiny[:, k0 + x:k0 + x + 1] for x in range(3)]
            t1 = act(o, b[:, 0:256], ACT.Copy, [t1], accum_out=a0)
            give(b, t1)
            ts(a0, a0, -1.0 / 256, None, MUL, None, [t1])
            t1 = ts(o, o, a0, None, ADD)
            t1 = act(junk, o, ACT.Square, [t1], accum_out=a1)
            t1 = ts(a1, a1, 1.0 / 256, 1e-6, MUL, ADD, [t1])
            t1 = act(a1, a1, ACT.Sqrt, [t1])
            recip(a2, a1, [t1])
            stt(o, o, a2, gw[:, h * 256:h * 256 + 256], MUL, MUL)
            tt(o, o, gr[:, i, h * 256:h * 256 + 256], MUL)
    oT = sb(8, 256)
    r = turn(oR, 2, oT, after=done())
    branch(I["w_ret_branch_2"][0], oT, 8, 1024, True, r)
    zT = sb(8, 256)
    r = turn(Z, 2, zT, after=done())
    for c in range(4):
        w = cols(I["w_mix_out_2"][0], c * 256, 256)
        for m_ in range(2):
            b, t = tm(w, 0, 256, zT, m_, r)
            t1 = tt(H[:, m_, c * 256:c * 256 + 256], H[:, m_, c * 256:c * 256 + 256], b[:, 0:256], ADD, [t])
            give(b, t1)
        wfree(w, t)
    barrier()
    top[0] = m_layer
    norm_turn(2, lambda f, s: col("norm_ffn_w_2", f), None)
    aT = sb(22, 256)
    U = [sb(256) for _ in range(3)]
    u_free = [()] * 3
    W = I["w_ffn_up_2"][0]
    first_w = done()
    for j in range(44):
        if j % 2 == 0:
            w = cols(W, j * 128, 256)
        b, t = fm(w, (j % 2) * 128, XT, 256, first_w if j == 0 else ())
        if j % 2:
            wfree(w, t)
        u = U[j % 3]
        t = act(u, b[:, 0:256], ACT.Identity, [t, *u_free[j % 3]], scale=col("ffn_conv_w_2", 88 + j), bias=col("ffn_conv_b_2", j))
        stt(u[:, 1:256], b[:, 0:255], col("ffn_conv_w_2", 44 + j), u[:, 1:256], MUL, ADD, [t])
        t = stt(u[:, 2:256], b[:, 0:254], col("ffn_conv_w_2", j), u[:, 2:256], MUL, ADD)
        give(b, t)
        if j < 22:
            t = act(aT[:, j, :], u, ACT.Silu, [t])
        else:
            t = tt(aT[:, j - 22, :], aT[:, j - 22, :], u, MUL, [t], q=GP)
        u_free[j % 3] = (t,)
    W = I["w_ffn_down_2"][0]
    O = sb(2, 1024)
    out_proj([(W, 0, 8), (W, 8, 8), (W, 16, 6)], aT, 2, O, done())
    gw, junk, fin = sb(1024), sb(1024), sb(2, 1024)
    spread(lambda k: col("norm_final_w_2", k), gw, done())
    for k in range(2):
        t = tt(H[:, k, :], H[:, k, :], O[:, k, :], ADD, done())
        t, r = rstd_of(H[:, k, :], 1024, 1e-6, k, junk, [t])
        t = stt(fin[:, k, :], H[:, k, :], r, gw, MUL, MUL, [t])
        stores.append(load(SP, [(out[0, k * 128:k * 128 + 128, :], fin[:, k, :])], [t]))
    SP.ops.append([None, stores, False])

    for q_ in ENG + [SP]:
        n, q_.value = 0, []
        for op in q_.ops:
            n += op[2]
            q_.value.append(n)

    def emit(q_, e):
        seen = {}
        for fn, waits, marked in q_.ops:
            need = {}
            for w_ in waits:
                s_, v_ = (w_[1], w_[2]) if w_[0] == "dma" else (w_[0].sem, w_[0].value[w_[1]])
                if seen.get(id(s_), (s_, 0))[1] < v_ and need.get(id(s_), (s_, 0))[1] < v_:
                    need[id(s_)] = (s_, v_)
            for i_, (s_, v_) in need.items():
                e.wait_ge(s_, v_)
                seen[i_] = (s_, v_)
            if fn is not None:
                ins = fn(e)
                if marked:
                    ins.then_inc(q_.sem, 1)

    block = ctx.enter_context(nc.Block())
    block.sync(lambda e: emit(SP, e))
    block.scalar(lambda e: emit(SC, e))
    block.gpsimd(lambda e: emit(GP, e))
    block.vector(lambda e: emit(VE, e))
    block.tensor(lambda e: emit(PE, e))
    ctx.close()


def tables():
    import numpy as np
    f = np.float32
    p = np.arange(128)
    t = np.arange(256)
    T = {"ident": np.eye(128), "bones": np.kron(np.eye(2), np.ones((64, 64)))}

    def rot(n, half, width):
        m = np.zeros((128, 128))
        for base in range(0, 128, width):
            for i in range(half):
                m[base + half + i, base + i] = -1.0
                m[base + i, base + half + i] = 1.0
        return m

    T["Rax"] = rot(128, 16, 32)
    inv = f(10000.0) ** (-np.arange(16, dtype=f) / f(16))
    ang = np.zeros((128, 256), f)
    for i in range(128):
        pos = (t // 64 if (i % 64) < 32 else t % 64).astype(f)
        ang[i] = pos * inv[i % 16]
    T["cosax"], T["sinax"] = np.cos(ang), np.sin(ang)
    T["Rnsa"] = rot(128, 8, 64)
    inv = np.power(f(500000.0), -np.arange(8, dtype=f) / f(8))
    c, s = np.ones((128, 256), f), np.zeros((128, 256), f)
    for i in range(128):
        if i % 64 < 16:
            a = t.astype(f) * inv[i % 8]
            c[i], s[i] = np.cos(a), np.sin(a)
    T["cosnsa"], T["sinnsa"] = c, s
    T["Rret"] = rot(128, 64, 128)
    inv = np.power(f(10000.0), -np.arange(64, dtype=f) / f(64))
    ang = t.astype(f)[None, :] * inv[p % 64][:, None]
    T["cosret"], T["sinret"] = np.cos(ang), np.sin(ang)
    NEG = f(-1e30)
    q = p[:, None, None] + 128 * np.arange(2)[None, :, None]
    T["wmask"] = np.where(np.abs(q - t[None, None, :]) <= 128, 0, NEG)
    cq = (p % 64)[:, None]
    ck = (t % 64)[None, :]
    ws = np.clip(cq - 8, 0, 48)
    flip = np.kron(np.eye(2), np.eye(64)[::-1])
    T["flip"] = flip
    T["cmask"] = np.where((ck >= ws) & (ck < ws + 16), 0, NEG)[np.argmax(flip, axis=1)]
    T["caus"] = np.where(p[None, :] <= p[:, None], 0, NEG)
    ce = np.arange(16)[None, None, :] * 16 + 31
    ok = ce <= q
    T["cmpm"], T["cmp01"] = np.where(ok, 0, NEG), ok.astype(f)
    T["scanm"] = np.broadcast_to((np.arange(512) % 64 != 0), (128, 512))
    i, j = (p % 64)[:, None], np.arange(64)[None, :]
    L = np.zeros((128, 2, 6, 64))
    for l in range(6):
        s_ = 1 << l
        same = (i // (2 * s_)) == (j // (2 * s_))
        L[:, 0, l, :] = same & (i % (2 * s_) >= s_) & (j % (2 * s_) < s_)
        L[:, 1, l, :] = same & (i % (2 * s_) < s_) & (j % (2 * s_) >= s_)
    T["lvl"] = L
    tri = np.zeros((128, 2, 128))
    tri[:, 0, 0:64], tri[:, 0, 64:128] = i < j, i <= j
    tri[:, 1, 0:64], tri[:, 1, 64:128] = i > j, i >= j
    T["tri"] = tri
    T["idst"] = (i == j)
    lg = np.log1p(-np.exp2(-5.0 - np.arange(4)))
    dec = np.zeros((128, 4, 384))
    for h in range(4):
        d = t[None, :] - p[:, None]
        dec[:, h, 0:256] = np.where(d >= 0, np.exp(lg[h] * np.maximum(d, 0)), 0)
        dec[:, h, 256:384] = dec[:, h, 0:128]
    T["dec"] = dec
    return {k: np.ascontiguousarray(v, dtype=f) for k, v in T.items()}


_INS = ["x", "c", "ctx", "c_ctx", "w_ada", "b_ada", "g_pre_mix", "g_post_mix", "g_pre_ff", "g_post_ff", "w_in_even",
        "w_in_odd", "w_out", "w_ff1", "w_ff2", "a_mu_prev", "a_mu_next", "a_w0", "a_w2", "a_a0", "a_a2", "a_g2", "a_k_k",
        "a_k_a", "a_r_k", "a_gn_w", "a_gn_b", "b_sink", "c_rpb", "d_q_gain", "d_k_gain", "norm_mix_w_2", "w_in_2",
        "cmp_pe_k_2", "cmp_w1_k_2", "cmp_w2_k_2", "cmp_pe_v_2", "cmp_w1_v_2", "cmp_w2_v_2", "w_nsa_branch_2",
        "ret_gn_w_2", "w_ret_branch_2", "w_mix_out_2", "norm_ffn_w_2", "w_ffn_up_2", "ffn_conv_w_2",
        "ffn_conv_b_2", "w_ffn_down_2", "norm_final_w_2"]


def kernel(**inputs):
    import numpy as np
    import concourse.bacc as bacc
    from concourse import mybir
    from concourse.bass_utils import run_bass_kernel_spmd as run

    nc = bacc.Bacc("TRN2", target_bir_lowering=False, num_devices=1)
    arrays, I, C = {}, {}, {}
    for name in _INS:
        a = np.ascontiguousarray(inputs[name])
        arrays["in_" + name] = a
        I[name] = nc.dram_tensor("in_" + name, a.shape, mybir.dt.float32, kind="ExternalInput").ap()
    for name, a in tables().items():
        arrays["t_" + name] = a
        C[name] = nc.dram_tensor("t_" + name, a.shape, mybir.dt.float32, kind="ExternalInput").ap()
    out = nc.dram_tensor("out_0", (1, 256, 1024), mybir.dt.float32, kind="ExternalOutput").ap()
    program(nc, I, C, out)
    r = run(nc, [arrays], core_ids=[0])
    return r.results[0]["out_0"]
```

```python
def program(nc, I, C, out):
    import math
    import concourse.bass as bass
    from concourse import mybir
    from contextlib import ExitStack

    F32 = mybir.dt.float32
    ALU = mybir.AluOpType
    ACT = mybir.ActivationFunctionType
    AX = mybir.AxisListType
    MUL, ADD, SUB, MAX = ALU.mult, ALU.add, ALU.subtract, ALU.max

    ctx = ExitStack()
    AREA = 53200
    arena = ctx.enter_context(nc.sbuf_tensor("arena", [128, AREA], F32))
    banks = [ctx.enter_context(nc.psum_tensor(f"bank{i}", [128, 512], F32)) for i in range(8)]

    class Queue:
        def __init__(self, name, chain):
            self.name, self.chain, self.ops, self.tail, self.owed = name, chain, [], None, []
            self.sem = ctx.enter_context(nc.semaphore("s_" + name))

        def add(self, fn, after=(), compute=True):
            waits = [t for t in after if t is not None] + self.owed
            self.owed = []
            if self.chain and compute and self.tail is not None:
                waits.append((self, self.tail))
            for t in waits:
                if t[0] != "dma":
                    t[0].ops[t[1]][2] = True
            self.ops.append([fn, waits, False])
            if compute:
                self.tail = len(self.ops) - 1
            return (self, len(self.ops) - 1)

        def last(self):
            return None if self.tail is None else (self, self.tail)

    PE, VE, SC, GP, SP = Queue("pe", False), Queue("ve", True), Queue("sc", True), Queue("gp", True), Queue("sp", False)
    ENG = [PE, VE, SC, GP]

    def done():
        return [q.last() for q in ENG if q.last() is not None]

    def barrier():
        t = done()
        for q in ENG:
            q.owed = [x for x in t if x[0] is not q] + q.owed

    n_sem = [0]

    def new_sem():
        n_sem[0] += 1
        return ctx.enter_context(nc.semaphore(f"s_d{n_sem[0]}"))

    def load(q, pairs, after=()):
        s = new_sem()
        for i, (dst, src) in enumerate(pairs):
            q.add(lambda e, dst=dst, src=src: e.dma_start(dst, src).then_inc(s, 16) and None,
                  after if i == 0 else (), compute=False)
        return ("dma", s, 16 * len(pairs))

    top = [0]

    def sb(*shape):
        n = 1
        for x in shape:
            n *= x
        a = arena[:, top[0]:top[0] + n]
        top[0] += n
        assert top[0] <= AREA, top[0]
        if len(shape) == 2:
            a = a.rearrange("p (a b) -> p a b", a=shape[0])
        elif len(shape) == 3:
            a = a.rearrange("p (a b c) -> p a b c", a=shape[0], b=shape[1])
        return a

    idle = [(b, ()) for b in banks]

    def take():
        assert idle, "no bank"
        return idle.pop(0)

    def give(b, *t):
        idle.append((b, t))

    def mm(o, l, r, start=True, stop=True, after=(), skip=False):
        return PE.add(lambda e: e.matmul(o, l, r, start=start, stop=stop, skip_group_check=skip), after)

    def tr(o, i, idn, after=()):
        return PE.add(lambda e: e.transpose(o, i, idn), after)

    def act(o, i, f, after=(), **k):
        return SC.add(lambda e: e.activation(o, i, f, **k), after)

    def tt(o, a, b, op, after=(), q=VE):
        return q.add(lambda e: e.tensor_tensor(o, a, b, op), after)

    def ts(o, a, s1, s2, op0, op1=None, after=(), q=VE):
        if op1 is None:
            return q.add(lambda e: e.tensor_scalar(o, a, s1, None, op0), after)
        return q.add(lambda e: e.tensor_scalar(o, a, s1, s2, op0, op1), after)

    def stt(o, a, s, b, op0, op1, after=(), q=VE):
        return q.add(lambda e: e.scalar_tensor_tensor(out=o, in0=a, scalar=s, in1=b, op0=op0, op1=op1), after)

    def cp(o, i, after=(), q=VE):
        if q is SC:
            return act(o, i, ACT.Copy, after)
        return q.add(lambda e: e.tensor_copy(o, i), after)

    def recip(o, i, after=()):
        return VE.add(lambda e: e.reciprocal(o, i), after)

    def rmax(o, i, after=()):
        return VE.add(lambda e: e.tensor_reduce(o, i, AX.X, MAX), after)

    def zero(o, after=(), q=GP, v=0.0):
        return q.add(lambda e: e.memset(o, v), after)

    flip = [0]

    def ev(o, i, after=()):
        flip[0] ^= 1
        return cp(o, i, after, SC if flip[0] else VE)

    h_at = top[0]
    H = sb(4, 1024)
    xt_at = top[0]
    XT = sb(8, 512)
    VC = sb(512)
    MOD = [sb(48, 2), sb(48, 2)]
    DER = sb(4, 8, 2)
    gb_at = top[0]
    GB = sb(2, 1024)
    SV = sb(8, 32)
    arow, arow_free = [sb(256), sb(256)], [None, None]
    sel = sb(2)
    tiny = sb(64)
    ident = sb(128)
    bones = sb(128)
    NSLOT = 4
    RING = [sb(2048) for _ in range(NSLOT)]
    ring_top = top[0]
    ring_sem = [new_sem() for _ in range(NSLOT)]
    ring_n = [0] * NSLOT
    ring_free = [()] * NSLOT
    ring_at = [0]
    live = list(range(NSLOT))

    class Slot:
        pass

    def wload(parts):
        s = live[ring_at[0] % len(live)]
        ring_at[0] += 1
        for i, (dst, src) in enumerate(parts(RING[s])):
            SP.add(lambda e, dst=dst, src=src, s=s: e.dma_start(dst, src).then_inc(ring_sem[s], 16) and None,
                   ring_free[s] if i == 0 else (), compute=False)
            ring_n[s] += 16
        w = Slot()
        w.i, w.ap, w.tok = s, RING[s], ("dma", ring_sem[s], ring_n[s])
        return w

    def wfree(w, t):
        ring_free[w.i] = (t,)

    def cols(W, c0, n, k0=0, nk=8):
        src = W[k0 * 128:(k0 + nk) * 128, c0:c0 + n].rearrange("(k p) f -> p k f", p=128)
        w = wload(lambda r: [(r[:, 0:nk * n].rearrange("p (k f) -> p k f", k=nk), src)])
        w.v = w.ap[:, 0:nk * n].rearrange("p (k f) -> p k f", k=nk)
        return w

    def cols_of(W, pieces, nk=8):
        tot = sum(n for _, n in pieces)

        def parts(r):
            v = r[:, 0:nk * tot].rearrange("p (k f) -> p k f", k=nk)
            at, res = 0, []
            for c0, n in pieces:
                res.append((v[:, :, at:at + n], W[0:nk * 128, c0:c0 + n].rearrange("(k p) f -> p k f", p=128)))
                at += n
            return res
        w = wload(parts)
        w.v = w.ap[:, 0:nk * tot].rearrange("p (k f) -> p k f", k=nk)
        return w

    def fm(w, f0, xT, n, after=()):
        b, free = take()
        nk = w.v.shape[1]
        for k in range(nk):
            t = mm(b[:, 0:n], w.v[:, k, f0:f0 + 128], xT[:, k, 0:n], k == 0, k == nk - 1,
                   [w.tok, *free, *after] if k == 0 else ())
        return b, t

    def tm(w, f0, nf, xT, tok, after=()):
        b, free = take()
        nk = w.v.shape[1]
        for k in range(nk):
            t = mm(b[:, 0:nf], xT[:, k, tok * 128:tok * 128 + 128], w.v[:, k, f0:f0 + nf], k == 0, k == nk - 1,
                   [w.tok, *free, *after] if k == 0 else ())
        return b, t

    t_id = load(SC, [(ident, C["ident"]), (bones, C["bones"]), (sel, C["sel"])])

    def load_h(after=()):
        return load(SC, [(H[:, 0:2, :], I["x"][0].rearrange("(t p) d -> p t d", p=128)),
                         (H[:, 2:4, :], I["ctx"][0].rearrange("(t p) d -> p t d", p=128))], after)

    t_h = load_h()
    mark = top[0]
    VR = [sb(128) for _ in range(4)]
    place, row, pairs = {}, 0, []

    def vec(name, ap):
        nonlocal row
        n = ap.shape[0]
        place[name] = (row, n)
        done_ = 0
        while done_ < n:
            m = min(n - done_, 128 - row % 128)
            pairs.append((VR[row // 128][row % 128:row % 128 + m, :], ap[done_:done_ + m, :]))
            row += m
            done_ += m

    def rows(ap):
        return ap.rearrange("(n q) -> n q", q=128)

    vec("c", rows(I["c"][0]))
    vec("c_ctx", rows(I["c_ctx"]))
    for i in range(2):
        for g in ("g_pre_mix", "g_post_mix", "g_pre_ff", "g_post_ff", "b_ada"):
            vec(g + str(i), rows(I[g][i]))
    for g in ("a_mu_prev", "a_mu_next", "a_k_k", "a_k_a", "a_gn_w", "a_gn_b"):
        vec(g, rows(I[g][0]))
    for g in ("a_w0", "a_a0"):
        vec(g, I[g][0].rearrange("d (n q) -> (d n) q", q=128))
    vec("a_r_k", I["a_r_k"][0].rearrange("(n a) q -> n (a q)", a=2))
    for g in ("norm_mix_w_2", "norm_ffn_w_2", "ffn_conv_b_2"):
        vec(g, rows(I[g][0]))
    vec("norm_final_w_2", rows(I["norm_final_w_2"]))
    vec("ffn_conv_w_2", I["ffn_conv_w_2"][0].rearrange("j (n q) -> (j n) q", q=128))
    vec("ret_gn_w_2", I["ret_gn_w_2"][0].rearrange("h (n q) -> (h n) q", q=128))
    for g in ("cmp_pe_k_2", "cmp_pe_v_2"):
        vec(g, I[g][0].rearrange("(n a) q -> n (a q)", a=2))
    for g in ("d_q_gain", "d_k_gain"):
        place[g] = (row, 1)
        for a in range(2):
            pairs.append((VR[row // 128][row % 128:row % 128 + 1, a * 64:a * 64 + 64], I[g]))
        row += 1
    assert row <= 512
    t_v = load(SC, pairs)
    b, free = take()
    for i in range(4):
        n = min(128, row - i * 128)
        t = tr(b[:, i * 128:i * 128 + n], VR[i][0:n, :], ident[0:n, 0:n], [t_v, t_id, *free] if i == 0 else ())
    t = cp(VC[:, 0:row], b[:, 0:row], [t])
    give(b, t)

    def col(name, j=0, n=1):
        r = place[name][0]
        return VC[:, r + j:r + j + n]

    t = act(SV[:, :, 0], col("c", 0, 8), ACT.Silu, [t, zero(SV)])
    t_sv = act(SV[:, :, 1], col("c_ctx", 0, 8), ACT.Silu)
    barrier()
    top[0] = mark

    def modulation(i, f0=0, f1=24):
        for s in range(f0, f1):
            w = cols(I["w_ada"][i], s * 256, 256)
            b, free = take()
            for k in range(8):
                q = 32 * (k % 4)
                t = mm(b[q:q + 32, 0:256], SV[:, k, :], w.v[:, k, :], k < 4, k >= 4, [w.tok, t_sv, *free] if k == 0 else ())
            wfree(w, t)
            r = arow[s % 2]
            t = cp(r, b[:, 0:256], [t, arow_free[s % 2]], SC)
            give(b, t)
            b, free = take()
            for f in range(2):
                t = mm(b[:, 2 * f:2 * f + 2], r[:, f * 128:f * 128 + 128], sel, after=[t, t_id, *free])
            arow_free[s % 2] = t
            bias = col("b_ada" + str(i), 2 * s, 2).unsqueeze(2).to_broadcast([128, 2, 2])
            t = tt(MOD[i][:, 2 * s:2 * s + 2, :], b[:, 0:4].rearrange("p (a s) -> p a s", s=2), bias, ADD, [t])
            give(b, t)
            yield t

    def run(*gens):
        gens = list(gens)
        while gens:
            for g in list(gens):
                if next(g, done) is done:
                    gens.remove(g)

    def gains(i, g, part, d):
        return stt(DER[:, d, :, :], MOD[i][:, part * 8:part * 8 + 8, :], 1.0,
                   col(g + str(i), 0, 8).unsqueeze(2).to_broadcast([128, 8, 2]), ADD, MUL)

    def spread(vecs, dst, after=()):
        for half in range(2):
            b, free = take()
            for j in range(4):
                t = mm(b[:, j * 128:j * 128 + 128], vecs(half * 4 + j).to_broadcast([128, 128]), ident,
                       after=[*after, *free] if j == 0 else ())
            t = ev(dst[:, half * 512:half * 512 + 512], b[:, :], [t])
            give(b, t)
        return t

    def gate_rows(i, g, part, d, streams):
        t = tt(DER[:, d, :, :], MOD[i][:, part * 8:part * 8 + 8, :],
               col(g + str(i), 0, 8).unsqueeze(2).to_broadcast([128, 8, 2]), MUL, done())
        for s in range(streams):
            spread(lambda k: DER[:, d, k, s:s + 1], GB[:, s, :], [t])
        return [SC.last(), VE.last()]

    def rstd_of(x, n, eps, k, junk, after=()):
        a, b_ = tiny[:, 4 * k:4 * k + 1], tiny[:, 4 * k + 1:4 * k + 2]
        t = act(junk, x, ACT.Square, after, accum_out=a)
        t = ts(b_, a, 1.0 / n, eps, MUL, ADD, [t])
        t = act(b_, b_, ACT.Sqrt, [t])
        return recip(tiny[:, 4 * k + 2:4 * k + 3], b_, [t]), tiny[:, 4 * k + 2:4 * k + 3]

    def turn(src, ntok, dst, gain=None, shift=None, after=(), nf=8):
        for k in range(ntok):
            for q in range(0, nf, 4):
                b, free = take()
                for j in range(4):
                    t = tr(b[:, j * 128:j * 128 + 128], src[:, k, (q + j) * 128:(q + j) * 128 + 128], ident,
                           [*after, *free] if j == 0 else ())
                if gain is None:
                    tv = ev(dst[:, q:q + 4, k * 128:k * 128 + 128],
                            b[:, :].rearrange("p (a c) -> p a c", a=4), [t])
                    give(b, tv)
                    continue
                for j in range(4):
                    o, i = dst[:, q + j, k * 128:k * 128 + 128], b[:, j * 128:j * 128 + 128]
                    s = 0 if k < 2 else 1
                    g = gain(q + j, s)
                    if q:
                        t1 = act(o, i, ACT.Identity, [t], scale=g, bias=shift(q + j, s) if shift else 0.0)
                    elif shift:
                        t1 = ts(o, i, g, shift(q + j, s), MUL, ADD, [t])
                    else:
                        t1 = ts(o, i, g, None, MUL, None, [t])
                give(b, t1)
        return [SC.last(), VE.last()]

    def norm_turn(ntok, gain, shift, after=()):
        m = top[0]
        xn, junk = sb(ntok, 1024), sb(1024)
        for k in range(ntok):
            t, r = rstd_of(H[:, k, :], 1024, 1e-6, k, junk, [*after, *done()] if k == 0 else ())
            t = ts(xn[:, k, :], H[:, k, :], r, None, MUL, None, [t])
        r = turn(xn, ntok, XT, gain, shift, [t, *done()])
        barrier()
        top[0] = m
        return r

    def out_proj(parts, xT, ntok, O, after):
        for c in range(4):
            bs = [take() for _ in range(ntok)]
            for pi, (W, k0, nk) in enumerate(parts):
                w = cols(W, c * 256, 256, k0, nk)
                for k in range(nk):
                    for m_ in range(ntok):
                        b, free = bs[m_]
                        t = mm(b[:, 0:256], xT[:, k0 + k, m_ * 128:m_ * 128 + 128], w.v[:, k, :],
                               pi == 0 and k == 0, pi == len(parts) - 1 and k == nk - 1,
                               [w.tok, *free, *after] if k == 0 else ())
                wfree(w, t)
            for m_ in range(ntok):
                te = ev(O[:, m_, c * 256:c * 256 + 256], bs[m_][0][:, 0:256], [t])
                give(bs[m_][0], te)
        return [SC.last(), VE.last()]

    def add_normed(O, ntok, after):
        m = top[0]
        junk = sb(1024)
        for k in range(ntok):
            t, r = rstd_of(O[:, k, :], 1024, 1e-6, k, junk, after if k == 0 else ())
            t = stt(O[:, k, :], O[:, k, :], r, GB[:, 0 if k < 2 else 1, :], MUL, MUL, [t])
            t = tt(H[:, k, :], H[:, k, :], O[:, k, :], ADD, [t])
        top[0] = m
        return t

    def ffn(i, ntok):
        n = ntok * 128
        gains(i, "g_pre_ff", 4, 1)
        norm_turn(ntok, lambda f, s: DER[:, 1, f, s:s + 1], lambda f, s: MOD[i][:, 24 + f, s:s + 1])
        m = top[0]
        h1 = sb(32, n)
        for s in range(16):
            w = cols(I["w_ff1"][i], s * 256, 256)
            for f in range(2):
                b, t = fm(w, f * 128, XT, n, done() if s == 0 and f == 0 else ())
                j = 2 * s + f
                if j % 2:
                    t1 = act(h1[:, j, :], b[:, 0:n], ACT.Relu, [t])
                    tt(h1[:, j, :], h1[:, j, :], h1[:, j, :], MUL, [t1], q=GP)
                else:
                    t1 = act(h1[:, j, :], b[:, 0:n], ACT.Relu, [t])
                    tt(h1[:, j, :], h1[:, j, :], h1[:, j, :], MUL, [t1])
                give(b, t1)
            wfree(w, t)
        gate_rows(i, "g_post_ff", 5, 3, 1 if ntok == 2 else 2)
        O = sb(ntok, 1024)
        W = I["w_ff2"][i]
        r = out_proj([(W, 0, 8), (W, 8, 8), (W, 16, 8), (W, 24, 8)], h1, ntok, O, [VE.last(), GP.last()])
        add_normed(O, ntok, r)
        barrier()
        top[0] = m

    def attend(items, after):
        m = top[0]
        NP, NT = 4, 3
        P = [sb(512) for _ in range(NP)]
        PT = [sb(512) for _ in range(NT)]
        st = sb(NP, 8)
        p_free, pt_free = [()] * NP, [()] * NT
        ready, obank = {}, [None]

        def first(i):
            it = items[i]
            n = it["n"]
            b, free = take()
            for x, (l, r, c0, c1) in enumerate(it["mms"]):
                t = mm(b[:, c0:c1], l, r, x == 0, x == len(it["mms"]) - 1,
                       [*free, *(after if i == 0 else ())] if x == 0 else ())
            s = st[:, i % NP, :]
            p = P[i % NP][:, 0:n]
            rmax(s[:, 0:1], b[:, 0:n], [t, *p_free[i % NP]])
            if it.get("sink") is not None:
                t = ts(s[:, 1:2], s[:, 0:1], it["sink"], -1.0, MAX, MUL)
            else:
                t = ts(s[:, 1:2], s[:, 0:1], -1.0, None, MUL)
            t = act(p, b[:, 0:n], ACT.Exp, [t], bias=s[:, 1:2], accum_out=s[:, 2:3])
            give(b, t)
            if it.get("sink") is not None:
                t = act(s[:, 3:4], it["sink"], ACT.Exp, bias=s[:, 1:2])
                t = tt(s[:, 2:3], s[:, 2:3], s[:, 3:4], ADD, [t])
            if it.get("m01") is not None:
                t = tt(p, p, it["m01"], MUL, [t])
            recip(s[:, 4:5], s[:, 2:3], [t])
            if it.get("gate") is not None:
                t = ts(p, p, s[:, 4:5], it["gate"], MUL, MUL)
            else:
                t = ts(p, p, s[:, 4:5], None, MUL)
            ready[i] = t

        def second(i):
            it = items[i]
            b, free = take()
            for x, (c0, kw, _) in enumerate(it["kts"]):
                t = tr(b[0:kw, x * 128:x * 128 + 128], P[i % NP][:, c0:c0 + kw], ident,
                       [ready[i], *free] if x == 0 else ())
            p_free[i % NP] = (t,)
            nk = len(it["kts"])
            kw = max(k for _, k, _ in it["kts"])
            t = act(PT[i % NT][0:kw, 0:nk * 128], b[0:kw, 0:nk * 128], ACT.Copy, [t, *pt_free[i % NT]])
            give(b, t)
            ready[i] = t

        def third(i):
            it = items[i]
            if it["open"]:
                obank[0] = take()
            b, free = obank[0]
            po, oc = it["po"], it["oc"]
            for x, (c0, kw, v) in enumerate(it["kts"]):
                t = mm(b[po:po + 64, oc:oc + 128], v, PT[i % NT][0:kw, x * 128:x * 128 + 128],
                       it["begin"] and x == 0, it["end"] and x == len(it["kts"]) - 1,
                       [ready[i], *free] if x == 0 else ())
            pt_free[i % NT] = (t,)
            if it["close"] is not None:
                tv = cp(it["close"], b[:, 0:256], [t])
                give(b, tv)

        for i in range(len(items) + 3):
            if i < len(items):
                first(i)
            if 0 <= i - 2 < len(items):
                second(i - 2)
            if 0 <= i - 3 < len(items):
                third(i - 3)
        barrier()
        top[0] = m

    def rotate(x, n, R, cos, sin, tmp, after, outs=None):
        b, free = take()
        t = mm(b[:, 0:n], R, x, after=[*after, *free])
        t1 = tt(tmp, b[:, 0:n], sin, MUL, [t])
        give(b, t1)
        tt(x, x, cos, MUL)
        for i, o in enumerate(outs or ()):
            s = slice(64 * i, 64 * i + 64)
            t = tt(o[s], x[s], tmp[s], ADD)
        return t if outs else tt(x, x, tmp, ADD)

    def head_sums(x, sq, n, after, scale=None):
        k = {} if scale is None else {"scale": scale}
        t = act(sq, x, ACT.Square, after, **k)
        b, free = take()
        t = mm(b[:, 0:n], bones, sq, after=[t, *free])
        return b, t

    stores = []

    run(modulation(0, 0, 8))
    gains(0, "g_pre_mix", 1, 0)
    norm_turn(4, lambda f, s: DER[:, 0, f, s:s + 1], lambda f, s: MOD[0][:, f, s:s + 1], [t_h])
    m_layer = top[0]
    OT = sb(8, 512)
    pA = sb(15, 512)
    m_b = top[0]
    qB, qZ = sb(4, 256), sb(8, 512)
    kB = sb(2, 512)
    vB = sb(4, 128)
    Rx, cosx, sinx, wmask = sb(128), sb(256), sb(256), sb(2, 256)
    snk = sb(8)
    mu0 = sb(15)
    t_z = zero(qZ, done())
    t_c = load(SC, [(Rx, C["Rax"]), (cosx, C["cosax"]), (sinx, C["sinax"]), (wmask, C["wmask"]),
                    (snk[0:1, :], I["b_sink"])], done())
    tt(mu0, col("a_mu_prev", 0, 15), col("a_mu_next", 0, 15), ADD)
    ts(mu0, mu0, -1.0, 1.0, MUL, ADD)
    W = I["w_in_even"][0]
    first_w = done()
    for j in range(15):
        if j % 2 == 0:
            w = cols(W, j * 128, min(256, 1920 - j * 128))
        b, t = fm(w, (j % 2) * 128, XT, 512, first_w if j == 0 else ())
        if j % 2 or j == 14:
            wfree(w, t)
        o = pA[:, j, :].rearrange("p (s t) -> p s t", s=2)
        i = b[:, :].rearrange("p (s t) -> p s t", s=2)
        t = act(pA[:, j, :], b[:, :], ACT.Identity, [t], scale=mu0[:, j:j + 1])
        stt(o[:, :, 1:256], i[:, :, 0:255], col("a_mu_prev", j), o[:, :, 1:256], MUL, ADD, [t])
        t = stt(o[:, :, 0:255], i[:, :, 1:256], col("a_mu_next", j), o[:, :, 0:255], MUL, ADD)
        give(b, t)
    for j in range(4):
        if j % 2 == 0:
            w = cols(W, 1920 + j * 128, 256)
        b, t = fm(w, (j % 2) * 128, XT, 512)
        if j % 2:
            wfree(w, t)
        t = ts(qB[:, j, :], b[:, 0:256], 0.125, None, MUL, None, [t, t_z])
        for i in range(2):
            s = slice(64 * i, 64 * i + 64)
            t = ts(qZ[s, 2 * j + i, 256:512], b[s, 256:512], 0.125, None, MUL)
        give(b, t)
    w = cols_of(W, [(2432, 64), (2432, 64), (2496, 64), (2496, 64)])
    for g in range(2):
        b, t = fm(w, g * 128, XT, 512)
        t1 = ev(kB[:, g, :], b[:, :], [t])
        give(b, t1)
    wfree(w, t)
    w = cols(W, 2560, 128)
    for k in range(4):
        b, t = tm(w, 0, 128, XT, k)
        t1 = ev(vB[:, k, :], b[:, 0:128], [t])
        give(b, t1)
    wfree(w, t)
    b, free = take()
    zero(tiny[0:1, 63:64], done(), VE)
    one = sb(128)
    t = zero(one, (), VE, 1.0)
    t = mm(b[:, 0:8], one[0:1, :], snk[0:1, :], after=[t, t_c, *free])
    snkb = sb(8)
    t = cp(snkb, b[:, 0:8], [t])
    give(b, t)
    m = top[0]
    tmp = sb(256)
    t = [t_c, *done()]
    for j in range(4):
        rotate(qB[:, j, :], 256, Rx, cosx, sinx, tmp, t, [qZ[:, 2 * j + i, 0:256] for i in range(2)])
        t = [VE.last()]
    for g in range(2):
        rotate(kB[:, g, 0:256], 256, Rx, cosx, sinx, tmp, t)
        t = [VE.last()]
    items = []
    for pair in range(4):
        for h in (2 * pair, 2 * pair + 1):
            po, g = 64 * (h % 2), h // 4
            for qt in range(2):
                q = qZ[:, h, qt * 128:qt * 128 + 128]
                items.append(dict(
                    n=512, mms=[(q, kB[:, g, 0:512], 0, 512), (ident, wmask[:, qt, :], 0, 256)],
                    sink=snkb[:, h:h + 1], po=po, oc=qt * 128, begin=True, end=True,
                    kts=[(k * 128, 128, vB[:, k, g * 64:g * 64 + 64]) for k in range(4)],
                    open=h % 2 == 0 and qt == 0, close=OT[:, 4 + pair, 0:256] if h % 2 and qt else None))
        for h in (2 * pair, 2 * pair + 1):
            po, g = 64 * (h % 2), h // 4
            for qt in range(2):
                q = qZ[:, h, 256 + qt * 128:256 + qt * 128 + 128]
                items.append(dict(
                    n=256, mms=[(q, kB[:, g, 256:512], 0, 256)],
                    sink=snkb[:, h:h + 1], po=po, oc=qt * 128, begin=True, end=True,
                    kts=[(k * 128, 128, vB[:, 2 + k, g * 64:g * 64 + 64]) for k in range(2)],
                    open=h % 2 == 0 and qt == 0, close=OT[:, 4 + pair, 256:512] if h % 2 and qt else None))
    attend(items, done())
    barrier()
    top[0] = m_b

    CH0 = math.exp(-0.5)
    NCH = 4
    del live[2:]
    spare = [(xt_at, xt_at + 4096), (gb_at, gb_at + 2048), (h_at, h_at + 4096), (ring_top - 4096, ring_top)]

    def sp(*shape):
        n = 1
        for x in shape:
            n *= x
        for i, (a0, a1) in enumerate(spare):
            if a1 - a0 >= n:
                spare[i] = (a0 + n, a1)
                keep, top[0] = top[0], a0
                r = sb(*shape)
                top[0] = keep
                return r
        return sb(*shape)

    sets = []
    for _ in range(4):
        z = Slot()
        z.P, z.Q, z.T, z.TT, z.LT, z.LK, z.MB, z.MK = [sp(NCH, 128) for _ in range(8)]
        zero(z.P, done())
        z.free = [zero(z.Q)]
        sets.append(z)
    ar, be, ka = [sp(2, 512) for _ in range(2)], [sp(512) for _ in range(2)], [sp(512) for _ in range(2)]
    ET, FF, RT = [[sp(8, 128) for _ in range(2)] for _ in range(3)]
    Vbd = sp(8, 128)
    zero(Vbd)
    kb, sg, cu, ex, kk = [sp(512) for _ in range(5)]
    w2s, a2s, g2s, scanm = [sp(512) for _ in range(4)]
    lvl, tri = sp(2, 6, 64), sp(2, 2, 128)
    PC, PN = sp(2, 8), sp(2, 8)
    Zb = sp(2, 2, 128)
    ka1 = sp(4)
    t_c = load(SC, [(w2s, I["a_w2"][0].rearrange("d l c -> (d l) c")), (a2s, I["a_a2"][0].rearrange("d l c -> (d l) c")),
                    (g2s, I["a_g2"][0]), (scanm, C["scanm"]), (lvl, C["lvl"]), (tri, C["tri"])], done())
    ts(ka1, col("a_k_a", 0, 4), -1.0, 1.0, MUL, ADD)
    act(pA[:, 12, :], pA[:, 12, :], ACT.Tanh, done())
    act(pA[:, 14, :], pA[:, 14, :], ACT.Sigmoid)
    c8 = lambda a: a.rearrange("p (c t) -> p c t", t=64)
    v4 = lambda b: b[:, :].rearrange("p (c t) -> p c t", t=128)
    twice = lambda a: a.unsqueeze(2).to_broadcast([128, NCH, 2, 64])
    two = lambda a: a.rearrange("p c (h t) -> p c h t", h=2)
    HV = [(0, 64), (64, 128)]

    def product(l, r, after):
        b, free = take()
        l, r = (x if isinstance(x, list) else [x] for x in (l, r))
        for c in range(NCH):
            for i in range(len(l)):
                t = mm(b[:, c * 128:c * 128 + 128], l[i](c), r[i](c), i == 0, i == len(l) - 1,
                       [*after, *free] if c == 0 and i == 0 else ())
        return b, t

    def turned(src, dst, after):
        b, free = take()
        for c in range(3):
            mm(b[:, c * 128:c * 128 + 128], src[:, c * 64:c * 64 + 128], ident, after=[*after, *free] if c == 0 else ())
        mm(b[0:64, 384:512], src[:, 192:256], ident)
        t = mm(b[64:128, 384:512], src[:, 0:64], ident)
        cp(dst[0:64, :, 0:64], v4(b)[0:64, :, 0:64], [t], SC)
        cp(dst[64:128, 1:4, 64:128], v4(b)[64:128, 0:3, 64:128], (), SC)
        t = cp(dst[64:128, 0, 64:128], v4(b)[64:128, 3, 64:128], (), SC)
        give(b, t)
        return t

    at_ = lambda m: (lambda c: m[:, c, :])

    def unit(z, p, d, half, prepared):
        c0 = half * NCH
        w0, w1 = c0 * 64, c0 * 64 + 256
        arv = ar[d].rearrange("p a (c t) -> p c a t", t=64)[:, c0:c0 + NCH]
        bev, kav, vv = (a[:, c0:c0 + NCH, :] for a in (c8(be[d]), c8(ka[d]), Vbd))
        for h0, h1 in HV:
            cp(z.P[h0:h1, :, h0:h1], bev[h0:h1], [*z.free, *prepared], SC)
            cp(z.Q[h0:h1, :, h0:h1], kav[h0:h1], [*z.free, *prepared], GP)
        dep = [SC.last(), GP.last(), *prepared, *z.free]
        yield
        for src, L, M in ((z.P, z.LT, z.MB), (z.Q, z.LK, z.MK)):
            b, t = product(at_(src), at_(arv), dep)
            tt(two(L), twice(v4(b)[:, :, 0:64]), two(tri[:, d, 0:1, :].to_broadcast([128, NCH, 128])), MUL, [t, t_c])
            t1 = tt(two(M), twice(v4(b)[:, :, 64:128]), two(tri[:, d, 1:2, :].to_broadcast([128, NCH, 128])), MUL)
            give(b, t1)
        yield
        lm = lambda d_, l: lvl[:, d_, l, :].unsqueeze(1).unsqueeze(1).to_broadcast([128, NCH, 2, 64])
        idc = ident.unsqueeze(1).to_broadcast([128, NCH, 128])
        b, free = take()
        for c in range(NCH):
            t = tr(b[:, c * 128:c * 128 + 128], z.LT[:, c, :], ident, [VE.last(), *free] if c == 0 else ())
        tt(two(z.T), two(v4(b)), lm(d, 0), MUL, [t])
        give(b, VE.last())
        tt(z.T, idc, z.T, SUB)
        tt(two(z.TT), two(z.LT), lm(1 - d, 0), MUL)
        t = tt(z.TT, idc, z.TT, SUB)
        yield
        for l in range(1, 6):
            b, t = product(at_(z.LT), at_(z.T), [t])
            t = tt(two(z.P), two(v4(b)), lm(d, l), MUL, [t])
            give(b, t)
            yield
            if l < 5:
                b, t1 = product(at_(z.TT), at_(z.P), [t])
            b2, t2 = product(at_(z.P), at_(z.TT), [t])
            if l < 5:
                t1 = tt(z.T, z.T, v4(b), SUB, [t1])
                give(b, t1)
            t = tt(z.TT, z.TT, v4(b2), SUB, [t2])
            give(b2, t)
            yield
        b, t1 = product(at_(z.LK), at_(vv), [t])
        t1 = cp(z.Q, v4(b), [t1], SC)
        give(b, t1)
        t2 = turned(ar[d][:, 0, w0:w1], z.LT, [t])
        yield
        b, t3 = product(at_(z.TT), at_(z.LT), [t2])
        t3 = act(z.P, v4(b), ACT.Copy, [t3], scale=-1.0)
        give(b, t3)
        b, t4 = product(at_(z.TT), at_(z.Q), [t1])
        t4 = act(z.T, v4(b), ACT.Copy, [t4], scale=-1.0)
        give(b, t4)
        yield
        while chains:
            yield
        b, t = product(at_(z.P), at_(z.MB), [t3])
        t = tt(two(RT[d][:, c0:c0 + NCH, :]), two(v4(b)), twice(arv[:, :, 1, :]), ADD, [t, PE.last()])
        give(b, t)
        turned(be[d][:, w0:w1], z.LK, [t3])
        t5 = turned(ka[d][:, w0:w1], z.TT, [t4])
        yield
        b, t = product(at_(z.P), at_(z.LK), [t5])
        t = tt(ET[d][:, c0:c0 + NCH, :], v4(b), idc, ADD, [t])
        give(b, t)
        b, t = product([at_(z.TT), at_(z.LK)], [at_(vv), at_(z.T)], [t5])
        t = tt(FF[d][:, c0:c0 + NCH, :], v4(b), PN[:, d, c0:c0 + NCH].unsqueeze(2).to_broadcast([128, NCH, 128]), MUL, [t])
        give(b, t)
        b, t = product([at_(vv), at_(z.T)], [at_(z.MK), at_(z.MB)], [t4])
        y = c8(OT[:, p, :])[:, c0:c0 + NCH, :]
        for h0, h1 in HV:
            blk_ = v4(b)[h0:h1, :, h0:h1]
            t = cp(y[h0:h1], blk_, [t]) if d == 0 else tt(y[h0:h1], y[h0:h1], blk_, ADD, [t])
        give(b, t)
        z.free = done()

    def prepare(p):
        r, k, v = pA[:, p, :], pA[:, 4 + p, :], pA[:, 8 + p, :]
        b, t = head_sums(k, sg, 512, done(), col("a_k_k", p))
        t = act(sg, b[:, :], ACT.Sqrt, [t])
        give(b, t)
        ts(sg, sg, 1e-12, None, MAX, None, [t])
        recip(sg, sg)
        stt(kk, k, col("a_k_k", p), sg, MUL, MUL)
        for q in range(2):
            turned(v[:, 256 * q:256 * q + 256], Vbd[:, 4 * q:4 * q + 4, :], done())
        for d in range(2):
            s = slice(64 * d, 64 * d + 64)
            b, free = take()
            t = mm(b[:, :], w2s[s, p * 128:p * 128 + 128], pA[s, 12, :], after=[t_c, *done(), *free])
            t = act(sg, b[:, :], ACT.Sigmoid, [t, VE.last()], bias=col("a_w0", 4 * d + p))
            give(b, t)
            b, free = take()
            t2 = mm(b[:, :], a2s[s, p * 128:p * 128 + 128], pA[s, 13, :], after=free)
            t2 = act(be[d], b[:, :], ACT.Sigmoid, [t2], bias=col("a_a0", 4 * d + p))
            give(b, t2)
            VE.add(lambda e: e.tensor_tensor_scan(cu, scanm, sg, 0.0, MUL, ADD), [t])
            t = act(PC[:, d, :], c8(cu)[:, :, 63], ACT.Exp, [VE.last()], scale=-CH0)
            if d == 0:
                tt(c8(ex), c8(cu)[:, :, 63:64].to_broadcast([128, 8, 64]), c8(cu), SUB)
                tt(cu, ex, sg, ADD, [t])
            else:
                tt(ex, cu, sg, SUB)
            t = act(sg, ex, ACT.Exp, [VE.last()], scale=-CH0)
            act(ex, ex, ACT.Exp, scale=CH0)
            t1 = act(cu, cu, ACT.Exp, scale=CH0)
            ts(ka[d], be[d], col("a_k_a", p), ka1[:, p:p + 1], MUL, ADD, [t2])
            tt(ka[d], ka[d], k, MUL)
            if d == 0:
                cp(kb, ka[d])
            else:
                tt(kb, kb, ka[d], ADD)
            tt(be[d], be[d], kk, MUL)
            tt(be[d], be[d], sg, MUL, [t])
            tt(ka[d], ka[d], sg, MUL)
            tt(ar[d][:, 0, :], cu, kk, MUL, [t1])
            tt(ar[d][:, 1, :], ex, r, MUL)
            if d == 0:
                cp(PN[:, d, 0:7], PC[:, d, 1:8])
                cp(PN[:, d, 7:8], PC[:, d, 0:1])
            else:
                cp(PN[:, d, 1:8], PC[:, d, 0:7])
                cp(PN[:, d, 0:1], PC[:, d, 7:8])
        t = stt(kb, kb, col("a_r_k", p), r, MUL, MUL)
        b, free = take()
        t = mm(b[:, :], bones, kb, after=[t, *free])
        t = tt(k, b[:, :], v, MUL, [t])
        give(b, t)
        return done()

    order = [[4, 5, 6, 7, 0, 1, 2, 3], [7, 6, 5, 4, 3, 2, 1, 0]]
    chains = []

    def chain(p, finished, pn):
        dep = finished
        yacc, tmp = OT[:, p, :], pA[:, p, :]
        z = [FF[d][:, order[d][0], :] for d in range(2)]
        for i in range(1, 8):
            cs = [order[d][i] for d in range(2)]
            if i < 7:
                b, free = take()
                for d in range(2):
                    t = mm(b[:, d * 128:d * 128 + 128], ET[d][:, cs[d], :], z[d], after=[*dep, *free] if d == 0 else ())
                zn = [Zb[:, i % 2, d, :] for d in range(2)]
                for d in range(2):
                    tz = stt(zn[d], b[:, d * 128:d * 128 + 128], pn[:, d, cs[d]:cs[d] + 1], FF[d][:, cs[d], :], MUL, ADD, [t])
                give(b, tz)
            b2, free2 = take()
            for d in range(2):
                t = mm(b2[:, d * 128:d * 128 + 128], z[d], RT[d][:, cs[d], :], after=[*dep, *free2] if d == 0 else ())
            for d in range(2):
                for h0, h1 in HV:
                    y = yacc[h0:h1, cs[d] * 64:cs[d] * 64 + 64]
                    t = tt(y, y, b2[h0:h1, d * 128 + h0:d * 128 + h1], ADD, [t])
            give(b2, t)
            z, dep = zn, [tz]
            yield
        chains.pop(0)
        b, free = take()
        t = mm(b[:, :], bones, yacc, after=[VE.last(), *free])
        t = stt(yacc, b[:, :], -1.0 / 64, yacc, MUL, ADD, [t])
        give(b, t)
        yield
        b, t = head_sums(yacc, tmp, 512, [t])
        t = ts(tmp, b[:, :], 1.0 / 64, 64e-5, MUL, ADD, [t])
        give(b, t)
        t = act(tmp, tmp, ACT.Sqrt, [t])
        yield
        recip(tmp, tmp, [t])
        tt(yacc, yacc, tmp, MUL)
        ts(yacc, yacc, col("a_gn_w", p), col("a_gn_b", p), MUL, ADD)
        tt(yacc, yacc, pA[:, 4 + p, :], ADD)
        b, free = take()
        t = mm(b[:, :], g2s[:, p * 128:p * 128 + 128], pA[:, 14, :], after=free)
        t = tt(yacc, b[:, :], yacc, MUL, [t])
        give(b, t)

    PNs = [sp(2, 8) for _ in range(4)]
    pending = []
    for p in range(4):
        PN = PNs[p]
        ok = prepare(p)
        units = [unit(sets[2 * d + h], p, d, h, ok) for d in range(2) for h in range(2)]
        ada = modulation(0, 8 + 4 * p, 12 + 4 * p) if p < 4 else ()
        run(*pending, *units, ada, modulation(1, 6 * p, 6 * p + 6))
        chains.append(p)
        pending = [chain(p, done(), PN)]
    run(*pending)
    barrier()
    live.extend((2, 3))
    ring_free[2] = ring_free[3] = tuple(done())
    t_h = load_h(done())
    top[0] = m_layer + 8 * 512
    gate_rows(0, "g_post_mix", 2, 2, 2)
    O = sb(4, 1024)
    r = out_proj([(I["w_out"][0], 0, 8)], OT, 4, O, done())
    add_normed(O, 4, [*r, t_h])
    barrier()
    top[0] = m_layer
    ffn(0, 4)

    gains(1, "g_pre_mix", 1, 0)
    norm_turn(4, lambda f, s: DER[:, 0, f, s:s + 1], lambda f, s: MOD[1][:, f, s:s + 1])
    OT = sb(8, 256)
    m_c = top[0]
    Rx, cosx, sinx, cmask, flipm = sb(128), sb(256), sb(256), sb(256), sb(128)
    t_c = load(SC, [(Rx, C["Rax"]), (cosx, C["cosax"]), (sinx, C["sinax"]), (cmask, C["cmask"]), (flipm, C["flip"])], done())
    bias = sb(2, 8, 256)
    rp = I["c_rpb"]
    pairs = []
    for qt in range(2):
        for rq in range(2):
            for h in range(8):
                src = bass.AP(tensor=rp.tensor, offset=rp.offset + (h * 15 + 7 - (2 * qt + rq)) * 31 + 15 - 63,
                              ap=[[1, 64], [31, 4], [1, 64]])
                pairs.append((bias[rq * 64:rq * 64 + 64, qt, h, :].rearrange("p (a b) -> p a b", a=4), src))
    t_b = load(SC, pairs)
    qC, kC, vC = sb(8, 256), sb(4, 512), sb(4, 512)
    qD, qZ, kD, vD = sb(4, 256), sb(8, 256), sb(2, 512), sb(4, 128)
    zero(qC, done())
    t_z = zero(qZ)
    W = I["w_in_odd"][0]
    first_w = done()
    for j in range(4):
        if j % 2 == 0:
            w = cols(W, j * 128, 256)
        b, t = fm(w, (j % 2) * 128, XT, 256, first_w if j == 0 else ())
        if j % 2:
            wfree(w, t)
        for i in range(2):
            s = slice(64 * i, 64 * i + 64)
            t = ts(qC[s, 2 * j + i, :], b[s, 0:256], 0.125, None, MUL, None, [t, t_z])
        give(b, t)
    for j in range(4):
        if j % 2 == 0:
            w = cols(W, 512 + j * 128, 256)
        b, t = fm(w, (j % 2) * 128, XT, 512)
        if j % 2:
            wfree(w, t)
        t = ev(kC[:, j, :], b[:, :], [t])
        give(b, t)
    for j in range(2):
        w = cols(W, 1024 + j * 256, 256)
        for k in range(4):
            b, t = tm(w, 0, 256, XT, k)
            t1 = ev(vC[:, k, j * 256:j * 256 + 256], b[:, 0:256], [t])
            give(b, t1)
        wfree(w, t)
    for j in range(4):
        if j % 2 == 0:
            w = cols(W, 1536 + j * 128, 256)
        b, t = fm(w, (j % 2) * 128, XT, 256)
        if j % 2:
            wfree(w, t)
        t = ev(qD[:, j, :], b[:, 0:256], [t])
        give(b, t)
    w = cols_of(W, [(2048, 64), (2048, 64), (2112, 64), (2112, 64)])
    for g in range(2):
        b, t = fm(w, g * 128, XT, 512)
        t1 = ev(kD[:, g, :], b[:, :], [t])
        give(b, t1)
    wfree(w, t)
    w = cols(W, 2176, 128)
    for k in range(4):
        b, t = tm(w, 0, 128, XT, k)
        t1 = ev(vD[:, k, :], b[:, 0:128], [t])
        give(b, t1)
    wfree(w, t)
    for qt in range(2):
        tt(bias[:, qt, :, :], bias[:, qt, :, :], cmask.unsqueeze(1).to_broadcast([128, 8, 256]), ADD, [t_c, t_b], q=GP)
    m = top[0]
    tmp, sq = sb(512), sb(512)
    qg = sb(1)
    ts(qg, col("d_q_gain"), 0.125, None, MUL)
    for x, n, g, o in [(qD[:, j, :], 256, qg, [qZ[:, 2 * j, :], qZ[:, 2 * j + 1, :]]) for j in range(4)] + \
            [(kD[:, j, :], 512, col("d_k_gain"), None) for j in range(2)]:
        b, t = head_sums(x, sq[:, 0:n], n, done())
        t = ts(tmp[:, 0:n], b[:, 0:n], 1.0 / 64, 1e-6, MUL, ADD, [t])
        give(b, t)
        t = act(tmp[:, 0:n], tmp[:, 0:n], ACT.Sqrt, [t])
        recip(tmp[:, 0:n], tmp[:, 0:n], [t])
        stt(x, x, g, tmp[:, 0:n], MUL, MUL)
        rotate(x[:, 0:256], 256, Rx, cosx, sinx, tmp[:, 0:256], [t_c, VE.last()], o)
    barrier()
    top[0] = m
    items = []
    for kind in "CD":
        for pair in range(4):
            for h in (2 * pair, 2 * pair + 1):
                po, g = 64 * (h % 2), h // 4
                for qt in range(2):
                    s = slice(qt * 128, qt * 128 + 128)
                    if kind == "C":
                        mms = [(qC[:, h, s], kC[:, pair, :], 0, 512), (flipm, bias[:, qt, h, :], 0, 256)]
                        kts = [(k * 128, 128, vC[:, k, h * 64:h * 64 + 64]) for k in range(4)]
                    else:
                        mms = [(qZ[:, h, s], kD[:, g, :], 0, 512)]
                        kts = [(k * 128, 128, vD[:, k, g * 64:g * 64 + 64]) for k in range(4)]
                    dst = OT[:, (0 if kind == "C" else 4) + pair, :]
                    items.append(dict(n=512, mms=mms, po=po, oc=qt * 128, begin=True, end=True, kts=kts,
                                      open=h % 2 == 0 and qt == 0, close=dst if h % 2 and qt else None))
    attend(items, done())
    top[0] = m_c
    gate_rows(1, "g_post_mix", 2, 2, 1)
    O = sb(2, 1024)
    r = out_proj([(I["w_out"][1], 0, 8)], OT, 2, O, done())
    add_normed(O, 2, r)
    barrier()
    top[0] = m_layer
    ffn(1, 2)

    norm_turn(2, lambda f, s: col("norm_mix_w_2", f), None)
    W = I["w_in_2"][0]
    Z = sb(2, 1024)
    ga = sb(2, 2048)
    m_n = top[0]
    first_w = done()
    for j in range(8):
        w = cols(W, 4376 + j * 256, 256)
        for k in range(2):
            b, t = tm(w, 0, 256, XT, k, first_w if j == 0 else ())
            t1 = act(ga[:, k, j * 256:j * 256 + 256], b[:, 0:256], ACT.Sigmoid, [t])
            give(b, t1)
        wfree(w, t)
    oN = sb(4, 256)
    Rn, cosn, sinn, caus, cm, c01 = sb(128), sb(256), sb(256), sb(128), sb(2, 16), sb(2, 16)
    w2k, w2v = sb(2, 128), sb(2, 64)
    t_c = load(SC, [(Rn, C["Rnsa"]), (cosn, C["cosnsa"]), (sinn, C["sinnsa"]), (caus, C["caus"]), (cm, C["cmpm"]), (c01, C["cmp01"]),
                    (w2k[:, :, 0:64], I["cmp_w2_k_2"][0].rearrange("(t p) d -> p t d", p=128)),
                    (w2k[:, :, 64:128], I["cmp_w2_k_2"][0].rearrange("(t p) d -> p t d", p=128)),
                    (w2v, I["cmp_w2_v_2"][0].rearrange("(t p) d -> p t d", p=128))], done())
    q, qZ = sb(4, 256), sb(8, 256)
    t_z = zero(qZ, done())
    for j in range(4):
        if j % 2 == 0:
            w = cols(W, j * 128, 256)
        b, t = fm(w, (j % 2) * 128, XT, 256)
        if j % 2:
            wfree(w, t)
        t = ts(q[:, j, :], b[:, 0:256], 0.125, None, MUL, None, [t])
        give(b, t)
    kv = {}
    for nm, c0 in (("kc", 512), ("vc", 640), ("ks", 768), ("kw", 1024)):
        kv[nm] = sb(2, 256)
        w = cols_of(W, [(c0, 64), (c0, 64), (c0 + 64, 64), (c0 + 64, 64)])
        for g in range(2):
            b, t = fm(w, g * 128, XT, 256)
            t1 = ev(kv[nm][:, g, :], b[:, 0:256], [t])
            give(b, t1)
        wfree(w, t)
    vsw = sb(2, 256)
    w = cols_of(W, [(896, 128), (1152, 128)])
    for k in range(2):
        b, t = tm(w, 0, 256, XT, k)
        t1 = ev(vsw[:, k, :], b[:, 0:256], [t])
        give(b, t1)
    wfree(w, t)
    gt = sb(2, 24)
    w = cols(W, 1280, 24)
    for k in range(2):
        b, t = tm(w, 0, 24, XT, k)
        t1 = act(gt[:, k, :], b[:, 0:24], ACT.Sigmoid, [t])
        give(b, t1)
    wfree(w, t)
    tmp = sb(256)
    t = [t_c, *done()]
    for x, o in [(q[:, j, :], [qZ[:, 2 * j, :], qZ[:, 2 * j + 1, :]]) for j in range(4)] + \
            [(kv[n_][:, g, :], None) for n_ in ("ks", "kw") for g in range(2)]:
        rotate(x, 256, Rn, cosn, sinn, tmp, t, o)
        t = [VE.last()]
    blk = sb(16, 2, 15)
    hid, hidT = sb(256), sb(2, 30)
    kcT, vcm = sb(30), sb(2, 64)
    for nm, pe, w1 in (("kc", "cmp_pe_k_2", "cmp_w1_k_2"), ("vc", "cmp_pe_v_2", "cmp_w1_v_2")):
        dep = done()
        for h in range(2):
            v = kv[nm][:, h, :].rearrange("p (c s) -> p s c", s=16)
            for par in range(2):
                s = slice(par * 64, par * 64 + 64)
                for e_ in range(2):
                    tt(blk[s, e_ * 8:e_ * 8 + 8, h, :], v[s, par::2, e_:e_ + 15],
                       col(pe, e_ * 8, 8)[s].unsqueeze(2).to_broadcast([64, 8, 15]), ADD, dep)
        b, free = take()
        for half in range(2):
            w = cols(I[w1][0], 0, 256, half * 8, 8)
            for k in range(8):
                t = mm(b[0:30, 0:256], blk[:, half * 8 + k, :, :], w.v[:, k, :], half == 0 and k == 0, half == 1 and k == 7,
                       [w.tok, VE.last(), *free] if k == 0 else ())
            wfree(w, t)
        t = act(hid[0:30, :], b[0:30, 0:256], ACT.Gelu_apprx_tanh, [t])
        give(b, t)
        b, free = take()
        for k in range(2):
            t = tr(b[:, k * 32:k * 32 + 30], hid[0:30, k * 128:k * 128 + 128], ident[0:30, 0:30], [t, *free])
        t = cp(hidT, b[:, 0:64].rearrange("p (k c) -> p k c", k=2)[:, :, 0:30], [t])
        give(b, t)
        b, free = take()
        if nm == "kc":
            for k in range(2):
                t = mm(b[:, 0:30], w2k[:, k, :], hidT[:, k, :], k == 0, k == 1, [t, t_c, *free])
            t = cp(kcT, b[:, 0:30], [t])
        else:
            for h in range(2):
                for k in range(2):
                    t = mm(b[0:15, h * 64:h * 64 + 64], hidT[:, k, h * 15:h * 15 + 15], w2v[:, k, :], k == 0, k == 1, [t, t_c, *free])
            t = cp(vcm[0:15], b[0:15, 0:128].rearrange("p (h d) -> p h d", h=2), [t])
        give(b, t)
    items = []
    for pair in range(4):
        for h in (2 * pair, 2 * pair + 1):
            po, g = 64 * (h % 2), h // 4
            for qt in range(2):
                s = slice(qt * 128, qt * 128 + 128)
                ql = qZ[:, h, s]
                n = 128 * (qt + 1)
                base = dict(po=po, oc=qt * 128, open=False, close=None, begin=False, end=False)
                items.append({**base, "n": 15, "mms": [(ql, kcT[:, g * 15:g * 15 + 15], 0, 15), (ident, cm[:, qt, 0:15], 0, 15)],
                              "m01": c01[:, qt, 0:15], "gate": gt[:, qt, 3 * h:3 * h + 1], "kts": [(0, 15, vcm[0:15, g, :])],
                              "begin": True, "open": h % 2 == 0 and qt == 0})
                for bi, (kn, vo) in enumerate((("ks", 0), ("kw", 128))):
                    items.append({**base, "n": n, "mms": [(ql, kv[kn][:, g, 0:n], 0, n), (ident, caus, n - 128, n)],
                                  "gate": gt[:, qt, 3 * h + 1 + bi:3 * h + 2 + bi],
                                  "kts": [(k * 128, 128, vsw[:, k, vo + g * 64:vo + g * 64 + 64]) for k in range(qt + 1)],
                                  "end": bi == 1, "close": oN[:, pair, :] if bi == 1 and h % 2 and qt else None})
    attend(items, done())

    def branch(Wb, xT, nk, g0, add, after):
        for c in range(4):
            bs = [take() for _ in range(2)]
            w = cols(Wb, c * 256, 256, 0, nk)
            for k in range(nk):
                for m_ in range(2):
                    b, free = bs[m_]
                    t = mm(b[:, 0:256], xT[:, k, m_ * 128:m_ * 128 + 128], w.v[:, k, :], k == 0, k == nk - 1,
                           [w.tok, *free, *after] if k == 0 else ())
            wfree(w, t)
            for m_ in range(2):
                g = ga[:, m_, g0 + c * 256:g0 + c * 256 + 256]
                z = Z[:, m_, c * 256:c * 256 + 256]
                if add:
                    t1 = tt(g, bs[m_][0][:, 0:256], g, MUL, [t])
                    tt(z, z, g, ADD)
                else:
                    t1 = tt(z, bs[m_][0][:, 0:256], g, MUL, [t])
                give(bs[m_][0], t1)

    branch(I["w_nsa_branch_2"][0], oN, 4, 0, False, done())
    barrier()
    top[0] = m_n
    Rr, cosr, sinr = sb(128), sb(256), sb(256)
    dec = sb(4, 384)
    gw = sb(1024)
    t_c = load(SC, [(Rr, C["Rret"]), (cosr, C["cosret"]), (sinr, C["sinret"]), (dec, C["dec"])], done())
    spread(lambda k: col("ret_gn_w_2", k), gw, done())
    qr, kr, vr, gr = sb(4, 256), sb(4, 256), sb(2, 1024), sb(2, 1024)
    for dst, c0, sc in ((qr, 1304, 1.0), (kr, 1816, 128 ** -0.5)):
        for j in range(4):
            if j % 2 == 0:
                w = cols(W, c0 + j * 128, 256)
            b, t = fm(w, (j % 2) * 128, XT, 256)
            if j % 2:
                wfree(w, t)
            t = ts(dst[:, j, :], b[:, 0:256], sc, None, MUL, None, [t, *done()])
            give(b, t)
    for dst, c0, f in ((vr, 2328, ACT.Copy), (gr, 3352, ACT.Silu)):
        for j in range(4):
            w = cols(W, c0 + j * 256, 256)
            for k in range(2):
                b, t = tm(w, 0, 256, XT, k)
                t1 = act(dst[:, k, j * 256:j * 256 + 256], b[:, 0:256], f, [t])
                give(b, t1)
            wfree(w, t)
    tmp = sb(256)
    t = [t_c, *done()]
    for x in [qr[:, j, :] for j in range(4)] + [kr[:, j, :] for j in range(4)]:
        rotate(x, 256, Rr, cosr, sinr, tmp, t)
        t = [VE.last()]
    ST = [sb(384) for _ in range(2)]
    oR, junk = sb(2, 1024), sb(256)
    st_free = [(), ()]
    for h in range(4):
        s = ST[h % 2]
        b, free = take()
        mm(b[:, 0:256], kr[:, h, 0:128], qr[:, h, :], after=[*done(), *free])
        t = mm(b[:, 256:384], kr[:, h, 128:256], qr[:, h, 128:256])
        t = tt(s, b[:, 0:384], dec[:, h, :], MUL, [t, t_c, *st_free[h % 2]])
        give(b, t)
        for i in range(2):
            b, free = take()
            v = lambda k: vr[:, k, h * 256:h * 256 + 256]
            if i == 0:
                t1 = mm(b[:, 0:256], s[:, 0:128], v(0), after=[t, *free])
            else:
                mm(b[:, 0:256], s[:, 128:256], v(0), True, False, [t, *free])
                t1 = mm(b[:, 0:256], s[:, 256:384], v(1), False, True)
                st_free[h % 2] = (t1,)
            o = oR[:, i, h * 256:h * 256 + 256]
            k0 = 4 * (2 * h + i)
            a0, a1, a2 = [tiny[:, k0 + x:k0 + x + 1] for x in range(3)]
            t1 = act(o, b[:, 0:256], ACT.Copy, [t1], accum_out=a0)
            give(b, t1)
            ts(a0, a0, -1.0 / 256, None, MUL, None, [t1])
            t1 = ts(o, o, a0, None, ADD)
            t1 = act(junk, o, ACT.Square, [t1], accum_out=a1)
            t1 = ts(a1, a1, 1.0 / 256, 1e-6, MUL, ADD, [t1])
            t1 = act(a1, a1, ACT.Sqrt, [t1])
            recip(a2, a1, [t1])
            stt(o, o, a2, gw[:, h * 256:h * 256 + 256], MUL, MUL)
            tt(o, o, gr[:, i, h * 256:h * 256 + 256], MUL)
    oT = sb(8, 256)
    r = turn(oR, 2, oT, after=done())
    branch(I["w_ret_branch_2"][0], oT, 8, 1024, True, r)
    zT = sb(8, 256)
    r = turn(Z, 2, zT, after=done())
    for c in range(4):
        w = cols(I["w_mix_out_2"][0], c * 256, 256)
        for m_ in range(2):
            b, t = tm(w, 0, 256, zT, m_, r)
            t1 = tt(H[:, m_, c * 256:c * 256 + 256], H[:, m_, c * 256:c * 256 + 256], b[:, 0:256], ADD, [t])
            give(b, t1)
        wfree(w, t)
    barrier()
    top[0] = m_layer
    norm_turn(2, lambda f, s: col("norm_ffn_w_2", f), None)
    aT = sb(22, 256)
    U = [sb(256) for _ in range(3)]
    u_free = [()] * 3
    W = I["w_ffn_up_2"][0]
    first_w = done()
    for j in range(44):
        if j % 2 == 0:
            w = cols(W, j * 128, 256)
        b, t = fm(w, (j % 2) * 128, XT, 256, first_w if j == 0 else ())
        if j % 2:
            wfree(w, t)
        u = U[j % 3]
        t = act(u, b[:, 0:256], ACT.Identity, [t, *u_free[j % 3]], scale=col("ffn_conv_w_2", 88 + j), bias=col("ffn_conv_b_2", j))
        stt(u[:, 1:256], b[:, 0:255], col("ffn_conv_w_2", 44 + j), u[:, 1:256], MUL, ADD, [t])
        t = stt(u[:, 2:256], b[:, 0:254], col("ffn_conv_w_2", j), u[:, 2:256], MUL, ADD)
        give(b, t)
        if j < 22:
            t = act(aT[:, j, :], u, ACT.Silu, [t])
        else:
            t = tt(aT[:, j - 22, :], aT[:, j - 22, :], u, MUL, [t], q=GP)
        u_free[j % 3] = (t,)
    W = I["w_ffn_down_2"][0]
    O = sb(2, 1024)
    out_proj([(W, 0, 8), (W, 8, 8), (W, 16, 6)], aT, 2, O, done())
    gw, junk, fin = sb(1024), sb(1024), sb(2, 1024)
    spread(lambda k: col("norm_final_w_2", k), gw, done())
    for k in range(2):
        t = tt(H[:, k, :], H[:, k, :], O[:, k, :], ADD, done())
        t, r = rstd_of(H[:, k, :], 1024, 1e-6, k, junk, [t])
        t = stt(fin[:, k, :], H[:, k, :], r, gw, MUL, MUL, [t])
        stores.append(load(SP, [(out[0, k * 128:k * 128 + 128, :], fin[:, k, :])], [t]))
    SP.ops.append([None, stores, False])

    for q_ in ENG + [SP]:
        n, q_.value = 0, []
        for op in q_.ops:
            n += op[2]
            q_.value.append(n)

    def emit(q_, e):
        seen = {}
        for fn, waits, marked in q_.ops:
            need = {}
            for w_ in waits:
                s_, v_ = (w_[1], w_[2]) if w_[0] == "dma" else (w_[0].sem, w_[0].value[w_[1]])
                if seen.get(id(s_), (s_, 0))[1] < v_ and need.get(id(s_), (s_, 0))[1] < v_:
                    need[id(s_)] = (s_, v_)
            for i_, (s_, v_) in need.items():
                e.wait_ge(s_, v_)
                seen[i_] = (s_, v_)
            if fn is not None:
                ins = fn(e)
                if marked:
                    ins.then_inc(q_.sem, 1)

    block = ctx.enter_context(nc.Block())
    block.sync(lambda e: emit(SP, e))
    block.scalar(lambda e: emit(SC, e))
    block.gpsimd(lambda e: emit(GP, e))
    block.vector(lambda e: emit(VE, e))
    block.tensor(lambda e: emit(PE, e))
    ctx.close()


def tables():
    import numpy as np
    f = np.float32
    p = np.arange(128)
    t = np.arange(256)
    T = {"ident": np.eye(128), "bones": np.kron(np.eye(2), np.ones((64, 64)))}

    def rot(n, half, width):
        m = np.zeros((128, 128))
        for base in range(0, 128, width):
            for i in range(half):
                m[base + half + i, base + i] = -1.0
                m[base + i, base + half + i] = 1.0
        return m

    T["sel"] = np.stack([p % 32 == 0, p % 32 == 1], axis=1)
    T["Rax"] = rot(128, 16, 32)
    inv = f(10000.0) ** (-np.arange(16, dtype=f) / f(16))
    ang = np.zeros((128, 256), f)
    for i in range(128):
        pos = (t // 64 if (i % 64) < 32 else t % 64).astype(f)
        ang[i] = pos * inv[i % 16]
    T["cosax"], T["sinax"] = np.cos(ang), np.sin(ang)
    T["Rnsa"] = rot(128, 8, 64)
    inv = np.power(f(500000.0), -np.arange(8, dtype=f) / f(8))
    c, s = np.ones((128, 256), f), np.zeros((128, 256), f)
    for i in range(128):
        if i % 64 < 16:
            a = t.astype(f) * inv[i % 8]
            c[i], s[i] = np.cos(a), np.sin(a)
    T["cosnsa"], T["sinnsa"] = c, s
    T["Rret"] = rot(128, 64, 128)
    inv = np.power(f(10000.0), -np.arange(64, dtype=f) / f(64))
    ang = t.astype(f)[None, :] * inv[p % 64][:, None]
    T["cosret"], T["sinret"] = np.cos(ang), np.sin(ang)
    NEG = f(-1e30)
    q = p[:, None, None] + 128 * np.arange(2)[None, :, None]
    T["wmask"] = np.where(np.abs(q - t[None, None, :]) <= 128, 0, NEG)
    cq = (p % 64)[:, None]
    ck = (t % 64)[None, :]
    ws = np.clip(cq - 8, 0, 48)
    flip = np.kron(np.eye(2), np.eye(64)[::-1])
    T["flip"] = flip
    T["cmask"] = np.where((ck >= ws) & (ck < ws + 16), 0, NEG)[np.argmax(flip, axis=1)]
    T["caus"] = np.where(p[None, :] <= p[:, None], 0, NEG)
    ce = np.arange(16)[None, None, :] * 16 + 31
    ok = ce <= q
    T["cmpm"], T["cmp01"] = np.where(ok, 0, NEG), ok.astype(f)
    T["scanm"] = np.broadcast_to((np.arange(512) % 64 != 0), (128, 512))
    i, j = (p % 64)[:, None], np.arange(64)[None, :]
    L = np.zeros((128, 2, 6, 64))
    for l in range(6):
        s_ = 1 << l
        same = (i // (2 * s_)) == (j // (2 * s_))
        L[:, 0, l, :] = same & (i % (2 * s_) >= s_) & (j % (2 * s_) < s_)
        L[:, 1, l, :] = same & (i % (2 * s_) < s_) & (j % (2 * s_) >= s_)
    T["lvl"] = L
    i, j = p[:, None], p[None, :]
    same = (i // 64) == (j // 64)
    T["tri"] = np.stack([np.stack([same & (i < j), same & (i <= j)], 1), np.stack([same & (i > j), same & (i >= j)], 1)], 1)
    lg = np.log1p(-np.exp2(-5.0 - np.arange(4)))
    dec = np.zeros((128, 4, 384))
    for h in range(4):
        d = t[None, :] - p[:, None]
        dec[:, h, 0:256] = np.where(d >= 0, np.exp(lg[h] * np.maximum(d, 0)), 0)
        dec[:, h, 256:384] = dec[:, h, 0:128]
    T["dec"] = dec
    return {k: np.ascontiguousarray(v, dtype=f) for k, v in T.items()}


_INS = ["x", "c", "ctx", "c_ctx", "w_ada", "b_ada", "g_pre_mix", "g_post_mix", "g_pre_ff", "g_post_ff", "w_in_even",
        "w_in_odd", "w_out", "w_ff1", "w_ff2", "a_mu_prev", "a_mu_next", "a_w0", "a_w2", "a_a0", "a_a2", "a_g2", "a_k_k",
        "a_k_a", "a_r_k", "a_gn_w", "a_gn_b", "b_sink", "c_rpb", "d_q_gain", "d_k_gain", "norm_mix_w_2", "w_in_2",
        "cmp_pe_k_2", "cmp_w1_k_2", "cmp_w2_k_2", "cmp_pe_v_2", "cmp_w1_v_2", "cmp_w2_v_2", "w_nsa_branch_2",
        "ret_gn_w_2", "w_ret_branch_2", "w_mix_out_2", "norm_ffn_w_2", "w_ffn_up_2", "ffn_conv_w_2",
        "ffn_conv_b_2", "w_ffn_down_2", "norm_final_w_2"]


def kernel(**inputs):
    import numpy as np
    import concourse.bacc as bacc
    from concourse import mybir
    from concourse.bass_utils import run_bass_kernel_spmd as run

    nc = bacc.Bacc("TRN2", target_bir_lowering=False, num_devices=1)
    arrays, I, C = {}, {}, {}
    for name in _INS:
        a = np.ascontiguousarray(inputs[name])
        arrays["in_" + name] = a
        I[name] = nc.dram_tensor("in_" + name, a.shape, mybir.dt.float32, kind="ExternalInput").ap()
    for name, a in tables().items():
        arrays["t_" + name] = a
        C[name] = nc.dram_tensor("t_" + name, a.shape, mybir.dt.float32, kind="ExternalInput").ap()
    out = nc.dram_tensor("out_0", (1, 256, 1024), mybir.dt.float32, kind="ExternalOutput").ap()
    program(nc, I, C, out)
    r = run(nc, [arrays], core_ids=[0])
    return r.results[0]["out_0"]
```

```python
def program(nc, I, C, out):
    import math
    import concourse.bass as bass
    from concourse import mybir
    from contextlib import ExitStack

    F32, F32R = mybir.dt.float32, mybir.dt.float32r
    ALU = mybir.AluOpType
    ACT = mybir.ActivationFunctionType
    AX = mybir.AxisListType
    MUL, ADD, SUB, MAX = ALU.mult, ALU.add, ALU.subtract, ALU.max

    ctx = ExitStack()
    AREA = 53200
    WIN = []
    with ExitStack() as under:
        for i in range(AREA // 2048):
            WIN.append(under.enter_context(nc.sbuf_tensor(f"window{i}", [128, 2048], F32R)))
    arena = ctx.enter_context(nc.sbuf_tensor("arena", [128, AREA], F32))
    extra = ctx.enter_context(nc.sbuf_tensor("extra", [128, 3584], F32))
    banks = [ctx.enter_context(nc.psum_tensor(f"bank{i}", [128, 512], F32)) for i in range(8)]

    class Op:
        def __init__(self, fn, waits, compute):
            self.fn, self.waits, self.compute, self.marked, self.value = fn, waits, compute, False, 0

    class Queue:
        def __init__(self, name, chain):
            self.name, self.chain, self.ops, self.tail, self.owed = name, chain, [], None, []
            self.sem = ctx.enter_context(nc.semaphore("s_" + name))

        def add(self, fn, after=(), compute=True, place=None):
            waits = [t for t in after if t is not None]
            if place is None:
                waits += self.owed
                self.owed = []
            for t in waits:
                if t[0] != "dma":
                    t[1].marked = True
            op = Op(fn, waits, compute)
            if place is None:
                self.ops.append(op)
            else:
                self.ops.insert(self.ops.index(place) + 1, op)
            if compute and (place is None or place is self.tail):
                self.tail = op
            return (self, op)

        def last(self):
            return None if self.tail is None else (self, self.tail)

    PE, VE, SC, GP, SP = Queue("pe", False), Queue("ve", True), Queue("sc", True), Queue("gp", True), Queue("sp", False)
    ENG = [PE, VE, SC, GP]

    def done():
        return [q.last() for q in ENG if q.last() is not None]

    def barrier(engines=None):
        t = done()
        for q in engines or ENG:
            q.owed = [x for x in t if x[0] is not q] + q.owed

    n_sem = [0]

    def new_sem():
        n_sem[0] += 1
        return ctx.enter_context(nc.semaphore(f"s_d{n_sem[0]}"))

    def load(q, pairs, after=()):
        s = new_sem()
        for i, (dst, src) in enumerate(pairs):
            q.add(lambda e, dst=dst, src=src: e.dma_start(dst, src).then_inc(s, 16) and None,
                  after if i == 0 else (), compute=False)
        return ("dma", s, 16 * len(pairs))

    top = [0]

    def sb(*shape):
        n = 1
        for x in shape:
            n *= x
        a = arena[:, top[0]:top[0] + n]
        top[0] += n
        assert top[0] <= AREA, top[0]
        if len(shape) == 2:
            a = a.rearrange("p (a b) -> p a b", a=shape[0])
        elif len(shape) == 3:
            a = a.rearrange("p (a b c) -> p a b c", a=shape[0], b=shape[1])
        return a

    def sb_aligned(*shape):
        top[0] = (top[0] + 2047) // 2048 * 2048
        return sb(*shape)

    def rr(a, dt=None):
        c = a.offset % AREA
        span = sum((n - 1) * step for step, n in list(a.ap)[1:])
        assert c // 2048 == (c + span) // 2048 < len(WIN), (c, span)
        w = WIN[c // 2048][:, :]
        if dt is not None:
            w = w.bitcast(dt)
        ap = [list(x) for x in a.ap]
        ap[0][0] = w.ap[0][0]
        return bass.AP(tensor=w.tensor, offset=(a.offset // AREA) * 2048 + c % 2048, ap=ap)

    class Pair:
        def __init__(self, hi, lo):
            self.hi, self.lo = hi, lo

    idle = [(b, ()) for b in banks]

    def take():
        assert idle, "no bank"
        return idle.pop(0)

    def give(b, *t):
        idle.append((b, t))

    def mm(o, l, r, start=True, stop=True, after=(), skip=False):
        return PE.add(lambda e: e.matmul(o, l, r, start=start, stop=stop, skip_group_check=skip), after)

    def tr(o, i, idn, after=()):
        return PE.add(lambda e: e.transpose(o, i, idn), after)

    def act(o, i, f, after=(), **k):
        return SC.add(lambda e: e.activation(o, i, f, **k), after)

    def tt(o, a, b, op, after=(), q=VE):
        return q.add(lambda e: e.tensor_tensor(o, a, b, op), after)

    def ts(o, a, s1, s2, op0, op1=None, after=(), q=VE):
        if op1 is None:
            return q.add(lambda e: e.tensor_scalar(o, a, s1, None, op0), after)
        return q.add(lambda e: e.tensor_scalar(o, a, s1, s2, op0, op1), after)

    def stt(o, a, s, b, op0, op1, after=(), q=VE):
        return q.add(lambda e: e.scalar_tensor_tensor(out=o, in0=a, scalar=s, in1=b, op0=op0, op1=op1), after)

    def cp(o, i, after=(), q=VE):
        if q is SC:
            return act(o, i, ACT.Copy, after)
        return q.add(lambda e: e.tensor_copy(o, i), after)

    def recip(o, i, after=()):
        return VE.add(lambda e: e.reciprocal(o, i), after)

    def rmax(o, i, after=()):
        return VE.add(lambda e: e.tensor_reduce(o, i, AX.X, MAX), after)

    def zero(o, after=(), q=GP, v=0.0):
        return q.add(lambda e: e.memset(o, v), after)

    flip = [0]

    def ev(o, i, after=()):
        flip[0] ^= 1
        return cp(o, i, after, SC if flip[0] else VE)

    def split(raw, hi, lo, after, q=None):
        t = act(rr(hi), raw, ACT.Copy, after)
        return tt(rr(lo), raw, rr(hi, F32), SUB, [t], q=q or VE)

    xt_at = top[0]
    XT, XH = sb(8, 512), sb(8, 512)
    X = Pair(XH, XT)
    NSLOT = 4
    RING = [sb(2048) for _ in range(NSLOT)]
    ring_top = top[0]
    HIGH = [sb(2048) for _ in range(3)]
    RING += HIGH
    high_top = top[0]
    h_at = top[0]
    H = sb(4, 1024)
    gb_at = top[0]
    GB = sb(2, 1024)
    VC = sb(512)
    MOD = [sb(48, 2), sb(48, 2)]
    DER = sb(8, 8, 2)
    SSQ = sb(4, 4)
    RS = sb(4, 4)
    DIAG = extra[:, 2048:2560].rearrange("p (a b) -> p a b", a=4)
    SV = sb(8, 32)
    arow, arow_free = [sb(256), sb(256)], [None, None]
    sel = sb(2)
    tiny = sb(64)
    ident = sb(128)
    bones = sb(128)
    JUNK = extra[:, 2560:3584]
    ring_sem = [new_sem() for _ in RING]
    ring_n = [0] * len(RING)
    ring_free = [()] * len(RING)
    ring_at = [0]
    live = list(range(len(RING)))

    class Slot:
        pass

    def wload(parts):
        s = live[ring_at[0] % len(live)]
        ring_at[0] += 1
        for i, (dst, src) in enumerate(parts(RING[s])):
            SP.add(lambda e, dst=dst, src=src, s=s: e.dma_start(dst, src).then_inc(ring_sem[s], 16) and None,
                   ring_free[s] if i == 0 else (), compute=False)
            ring_n[s] += 16
        w = Slot()
        w.i, w.ap, w.tok, w.high = s, RING[s], ("dma", ring_sem[s], ring_n[s]), None
        return w

    def wfree(w, t):
        ring_free[w.i] = (t,)
        if w.high is not None:
            high_free[w.high] = (t,)

    high_free, high_at = [()] * 3, [0]
    early = [None]

    def here():
        early[0] = (SC.ops[-1], VE.ops[-1])

    def part_ways(w, n):
        i = high_at[0] % 3
        high_at[0] += 1
        raw, hi = w.ap[:, 0:n], HIGH[i][:, 0:n]
        sc, ve = early[0] or (None, None)
        t = SC.add(lambda e: e.activation(rr(hi), raw, ACT.Copy), [w.tok, *high_free[i]], place=sc)
        t = VE.add(lambda e: e.tensor_tensor(rr(raw), raw, rr(hi, F32), SUB), [t], place=ve)
        here()
        w.high, w.tok = i, t
        return hi

    def cols(W, c0, n, k0=0, nk=8, whole=False):
        src = W[k0 * 128:(k0 + nk) * 128, c0:c0 + n].rearrange("(k p) f -> p k f", p=128)
        w = wload(lambda r: [(r[:, 0:nk * n].rearrange("p (k f) -> p k f", k=nk), src)])
        w.v = w.ap[:, 0:nk * n].rearrange("p (k f) -> p k f", k=nk)
        if whole:
            here()
        else:
            w.v = Pair(part_ways(w, nk * n).rearrange("p (k f) -> p k f", k=nk), w.v)
        w.nk = nk
        return w

    def cols_of(W, pieces, nk=8):
        tot = sum(n for _, n in pieces)

        def parts(r):
            v = r[:, 0:nk * tot].rearrange("p (k f) -> p k f", k=nk)
            at, res = 0, []
            for c0, n in pieces:
                res.append((v[:, :, at:at + n], W[0:nk * 128, c0:c0 + n].rearrange("(k p) f -> p k f", p=128)))
                at += n
            return res
        w = wload(parts)
        v = w.ap[:, 0:nk * tot].rearrange("p (k f) -> p k f", k=nk)
        w.v = Pair(part_ways(w, nk * tot).rearrange("p (k f) -> p k f", k=nk), v)
        w.nk = nk
        return w

    def mm3(o, l, r, start, stop, after=()):
        mm(o, rr(l[0]), rr(r[0]), start, False, after)
        mm(o, rr(l[0]), rr(r[1]), False, False)
        return mm(o, rr(l[1]), rr(r[0]), False, stop)

    def fm(w, f0, x, n, after=()):
        b, free = take()
        for k in range(w.nk):
            t = mm3(b[:, 0:n], [a[:, k, f0:f0 + 128] for a in (w.v.hi, w.v.lo)], [a[:, k, 0:n] for a in (x.hi, x.lo)],
                    k == 0, k == w.nk - 1, [w.tok, *free, *after] if k == 0 else ())
        return b, t

    def fm_first(w, x, after):
        bs = [take() for _ in range(2)]
        for h in range(2):
            s = slice(256 * h, 256 * h + 256)
            for f, (b, free) in enumerate(bs):
                for k in range(w.nk):
                    t = mm3(b[:, s], [a[:, k, f * 128:f * 128 + 128] for a in (w.v.hi, w.v.lo)], [a[:, k, s] for a in (x.hi, x.lo)],
                            k == 0, k == w.nk - 1, [w.tok, *free, *after[4 * h:4 * h + 4]] if k == 0 else ())
                    if k == w.nk - 1 and h:
                        bs[f] = (b, t)
        return bs

    def tm(w, f0, nf, x, tok, after=()):
        b, free = take()
        s = slice(tok * 128, tok * 128 + 128)
        for k in range(w.nk):
            t = mm3(b[:, 0:nf], [a[:, k, s] for a in (x.hi, x.lo)], [a[:, k, f0:f0 + nf] for a in (w.v.hi, w.v.lo)],
                    k == 0, k == w.nk - 1, [w.tok, *free, *after] if k == 0 else ())
        return b, t

    def by_tokens(w, f0, x, ntok, tmp):
        b, t = fm(w, f0, x, ntok * 128)
        t = cp(tmp[:, 0:ntok * 128], b[:, 0:ntok * 128], [t], SC)
        give(b, t)
        b, free = take()
        for k in range(ntok):
            t = tr(b[:, k * 128:k * 128 + 128], tmp[:, k * 128:k * 128 + 128], ident, [t, *free] if k == 0 else ())
        return b, t

    t_id = load(SP, [(ident, C["ident"])])

    def load_h(after=()):
        return load(SC, [(H[:, 0:2, :], I["x"][0].rearrange("(t p) d -> p t d", p=128)),
                         (H[:, 2:4, :], I["ctx"][0].rearrange("(t p) d -> p t d", p=128))], after)

    mark = top[0]
    VR = [sb(128) for _ in range(4)]
    place, row, pairs = {}, 0, []

    def vec(name, ap):
        nonlocal row
        n = ap.shape[0]
        place[name] = (row, n)
        done_ = 0
        while done_ < n:
            m = min(n - done_, 128 - row % 128)
            pairs.append((VR[row // 128][row % 128:row % 128 + m, :], ap[done_:done_ + m, :]))
            row += m
            done_ += m

    def rows(ap):
        return ap.rearrange("(n q) -> n q", q=128)

    vec("c", rows(I["c"][0]))
    vec("c_ctx", rows(I["c_ctx"]))
    def both(g):
        r, n = row, I[g].shape[1] // 128
        vec(g, I[g].rearrange("i (n q) -> (i n) q", q=128))
        for i in range(2):
            place[g + str(i)] = (r + i * n, n)

    both("b_ada")
    both("g_pre_mix")
    t_v0 = load(SP, pairs + [(sel, C["sel"])])
    assert row == 128
    pairs = []
    for g in ("g_post_mix", "g_pre_ff", "g_post_ff"):
        both(g)
    for g in ("a_mu_prev", "a_mu_next", "a_k_k", "a_k_a", "a_gn_w", "a_gn_b"):
        vec(g, rows(I[g][0]))
    for g in ("a_w0", "a_a0"):
        vec(g, I[g][0].rearrange("d (n q) -> (d n) q", q=128))
    vec("a_r_k", I["a_r_k"][0].rearrange("(n a) q -> n (a q)", a=2))
    for g in ("norm_mix_w_2", "norm_ffn_w_2", "ffn_conv_b_2"):
        vec(g, rows(I[g][0]))
    vec("norm_final_w_2", rows(I["norm_final_w_2"]))
    vec("ffn_conv_w_2", I["ffn_conv_w_2"][0].rearrange("j (n q) -> (j n) q", q=128))
    vec("ret_gn_w_2", I["ret_gn_w_2"][0].rearrange("h (n q) -> (h n) q", q=128))
    for g in ("cmp_pe_k_2", "cmp_pe_v_2"):
        vec(g, I[g][0].rearrange("(n a) q -> n (a q)", a=2))
    for g in ("d_q_gain", "d_k_gain"):
        place[g] = (row, 1)
        for a in range(2):
            pairs.append((VR[row // 128][row % 128:row % 128 + 1, a * 64:a * 64 + 64], I[g]))
        row += 1
    assert row <= 512
    pairs.append((bones, C["bones"]))
    b, free = take()
    t = tr(b[:, 0:128], VR[0], ident, [t_v0, t_id, *free])
    t0 = cp(VC[:, 0:128], b[:, 0:128], [t])
    give(b, t0)

    def col(name, j=0, n=1):
        r = place[name][0]
        return VC[:, r + j:r + j + n]

    act(SV[:, :, 0], col("c", 0, 8), ACT.Silu, [t0, zero(SV, q=VE)])
    t_sv = act(SV[:, :, 1], col("c_ctx", 0, 8), ACT.Silu)

    def modulation(i, f0=0, f1=24):
        last = None
        for s in range(f0, f1):
            w = cols(I["w_ada"][i], s * 256, 256, whole=True)
            b, free = take()
            for k in range(8):
                q = 32 * (k % 4)
                t = mm(b[q:q + 32, 0:256], SV[:, k, :], w.v[:, k, :], k < 4, k >= 4, [w.tok, t_sv, *free] if k == 0 else ())
            wfree(w, t)
            r = arow[s % 2]
            t = cp(r, b[:, 0:256], [t, arow_free[s % 2]], SC)
            give(b, t)
            if last is not None:
                turn_row(i, *last)
            last = s, t
            yield
        turn_row(i, *last)

    def turn_row(i, s, t):
        r = arow[s % 2]
        b, free = take()
        for f in range(2):
            t = mm(b[:, 2 * f:2 * f + 2], r[:, f * 128:f * 128 + 128], sel, after=[t, t_id, *free])
        arow_free[s % 2] = t
        bias = col("b_ada" + str(i), 2 * s, 2).unsqueeze(2).to_broadcast([128, 2, 2])
        t = tt(MOD[i][:, 2 * s:2 * s + 2, :], b[:, 0:4].rearrange("p (a s) -> p a s", s=2), bias, ADD, [t])
        give(b, t)

    def run(*gens):
        gens = list(gens)
        while gens:
            for g in list(gens):
                if next(g, done) is done:
                    gens.remove(g)

    def advance(gens):
        return [g for g in gens[::-1] if next(g, done) is not done][::-1]

    def staggered_(gens):
        going, gens = [], list(gens)
        while gens or going:
            if gens:
                going.append(gens.pop(0))
            going = advance(going)
            yield

    def staggered(gens):
        run(staggered_(gens))

    def slowed(g):
        for x in g:
            yield
            yield

    def by(n, g):
        for i, x in enumerate(g):
            if i % n == n - 1:
                yield x

    gain_made = []

    def gains(i, g, part, d):
        gain_made[:] = [stt(DER[:, d, :, :], MOD[i][:, part * 8:part * 8 + 8, :], 1.0,
                            col(g + str(i), 0, 8).unsqueeze(2).to_broadcast([128, 8, 2]), ADD, MUL)]

    def spread_(vecs, dst, after=()):
        for half in range(2):
            b, free = take()
            for j in range(4):
                t = mm(b[:, j * 128:j * 128 + 128], vecs(half * 4 + j).to_broadcast([128, 128]), ident,
                       after=[*after, *free] if j == 0 else ())
            t = ev(dst[:, half * 512:half * 512 + 512], b[:, :], [t])
            give(b, t)
            yield

    def spread(vecs, dst, after=()):
        run(spread_(vecs, dst, after))

    def gate_cols(i, g, part):
        d = 4 + 2 * i + (part == 5)
        return d, tt(DER[:, d, :, :], MOD[i][:, part * 8:part * 8 + 8, :],
                     col(g + str(i), 0, 8).unsqueeze(2).to_broadcast([128, 8, 2]), MUL)

    def gate_rows(dt, streams, after):
        run(gate_rows_(dt, streams, after))

    def gate_rows_(dt, streams, after):
        d, t = dt
        for s in range(streams):
            yield from spread_(lambda k: DER[:, d, k, s:s + 1], GB[:, s, :], [t, *after])

    def rstd_of(x, n, eps, k, junk, after=()):
        a, b_ = tiny[:, 4 * k:4 * k + 1], tiny[:, 4 * k + 1:4 * k + 2]
        t = act(junk, x, ACT.Square, after, accum_out=a)
        t = ts(b_, a, 1.0 / n, eps, MUL, ADD, [t])
        t = act(b_, b_, ACT.Sqrt, [t])
        return recip(tiny[:, 4 * k + 2:4 * k + 3], b_, [t]), tiny[:, 4 * k + 2:4 * k + 3]

    def turn(src, ntok, dst, gain=None, shift=None, after=(), nf=8):
        for k in range(ntok):
            for q in range(0, nf, 4):
                b, free = take()
                for j in range(4):
                    t = tr(b[:, j * 128:j * 128 + 128], src[:, k, (q + j) * 128:(q + j) * 128 + 128], ident,
                           [*after, *free] if j == 0 else ())
                hi, lo = [a[:, q:q + 4, k * 128:k * 128 + 128] for a in (dst.hi, dst.lo)]
                if gain is None:
                    tv = split(b[:, :].rearrange("p (a c) -> p a c", a=4), hi, lo, [t])
                    give(b, tv)
                    continue
                for j in range(4):
                    o, i = dst.lo[:, q + j, k * 128:k * 128 + 128], b[:, j * 128:j * 128 + 128]
                    s = 0 if k < 2 else 1
                    g = gain(q + j, s)
                    if q:
                        t1 = act(o, i, ACT.Identity, [t], scale=g, bias=shift(q + j, s) if shift else 0.0)
                    elif shift:
                        t1 = ts(o, i, g, shift(q + j, s), MUL, ADD, [t])
                    else:
                        t1 = ts(o, i, g, None, MUL, None, [t])
                give(b, t1)
                split(lo, hi, lo, [t1])
        return [SC.last(), VE.last()]

    x_made = []

    def x_ready():
        r = x_made[-8:]
        return r

    def normed(k, gain, shift, before=None, after=()):
        t = before(k) if before else None
        yield
        t = act(JUNK, H[:, k, :], ACT.Square, [t, *after], accum_out=RS[:, k, 0:1])
        yield
        t = ts(RS[:, k, 1:2], RS[:, k, 0:1], 1.0 / 1024, 1e-6, MUL, ADD, [t])
        t = act(RS[:, k, 1:2], RS[:, k, 1:2], ACT.Sqrt, [t])
        t = recip(RS[:, k, 2:3], RS[:, k, 1:2], [t])
        t = ts(DIAG[:, k, :], ident, RS[:, k, 2:3], None, MUL, None, after)
        yield
        s, made = 0 if k < 2 else 1, []
        for q in (0, 4):
            b, free = take()
            for j in range(4):
                tp = mm(b[:, j * 128:j * 128 + 128], H[:, k, (q + j) * 128:(q + j) * 128 + 128], DIAG[:, k, :],
                        after=[t, *free] if j == 0 else ())
            for j in range(4):
                o, i, g = X.lo[:, q + j, k * 128:k * 128 + 128], b[:, j * 128:j * 128 + 128], gain(q + j, s)
                if q:
                    t1 = act(o, i, ACT.Identity, [tp, *after, *gain_made], scale=g, bias=shift(q + j, s) if shift else 0.0)
                elif shift:
                    t1 = ts(o, i, g, shift(q + j, s), MUL, ADD, [tp, *after])
                else:
                    t1 = ts(o, i, g, None, MUL, None, [tp, *after])
            give(b, t1)
            made.append(t1)
        yield
        parts = [[a[:, q:q + 4, k * 128:k * 128 + 128] for a in (X.lo, X.hi)] for q in (0, 4)]
        th = [act(rr(hi), lo, ACT.Copy, [t]) for (lo, hi), t in zip(parts, made)]
        yield
        for (lo, hi), t, q in zip(parts, th, (VE, VE)):
            x_made.append(tt(rr(lo), lo, rr(hi, F32), SUB, [t], q=q))
        yield

    def norm_turn(ntok, gain, shift, before=None, after=()):
        staggered(normed(k, gain, shift, before, after) for k in range(ntok))
        return x_ready()

    def residual(O, after=()):
        def add(k):
            t = VE.add(lambda e: e.tensor_reduce(RS[:, k, 0:1], SSQ[:, k, :], AX.X, ADD), [SC.last()])
            t = ts(RS[:, k, 1:2], RS[:, k, 0:1], 1.0 / 1024, 1e-6, MUL, ADD, [t])
            t = act(RS[:, k, 1:2], RS[:, k, 1:2], ACT.Sqrt, [t])
            t = recip(RS[:, k, 2:3], RS[:, k, 1:2], [t])
            return stt(H[:, k, :], O[:, k, :], RS[:, k, 2:3], H[:, k, :], MUL, ADD, after)
        return add

    def out_proj(parts, x, ntok, O, after, ready=None, add=False, gate=False, then=(), order=range(8)):
        going = []
        for c in range(4):
            bs = [take() for _ in range(ntok)]
            at, tot = 0, sum(p[2] for p in parts)
            for W, k0, nk in parts:
                w = cols(W, c * 256, 256, k0, nk)
                end = c == 3 and at + nk == tot
                ks = [k for k in order if k < nk]
                steps = [(k, m) for m in range(ntok) for k in ks] if end else [(k, m) for k in ks for m in range(ntok)]
                for k, m_ in steps:
                    b, free = bs[m_]
                    s, i = slice(m_ * 128, m_ * 128 + 128), at + k
                    dep = [w.tok, *free, *after] if k == ks[0] else []
                    t = mm3(b[:, 0:256], [a[:, i, s] for a in (x.hi, x.lo)], [a[:, k, :] for a in (w.v.hi, w.v.lo)],
                            at == 0 and k == ks[0], at + nk == tot and k == ks[-1], dep + (ready[i] if ready and c == 0 else []))
                    if end and k == ks[-1]:
                        out_block(O, c, m_, b, t, add, gate)
                        if then:
                            going.append(then[m_])
                            going = advance(going)
                at += nk
                wfree(w, t)
            if c < 3:
                for m_ in range(ntok):
                    out_block(O, c, m_, bs[m_][0], t, add, gate)
        while going:
            going = advance(going)

    def out_block(O, c, m_, b, t, add, gate):
        s = slice(c * 256, c * 256 + 256)
        o, i, r = O[:, m_, s], b[:, 0:256], GB[:, m_ // 2, s]
        if add:
            te = tt(o, o, i, ADD, [t])
            give(b, te)
            if gate:
                te = act(JUNK[:, s], o, ACT.Square, [te], accum_out=SSQ[:, m_, c:c + 1])
                tt(o, o, r, MUL, [te])
        elif gate:
            te = act(JUNK[:, s], i, ACT.Square, [t], accum_out=SSQ[:, m_, c:c + 1])
            te = tt(o, i, r, MUL, [te])
            give(b, te)
        else:
            te = ev(o, i, [t])
            give(b, te)

    def ffn(i, ntok, xr, gain, shift):
        n = ntok * 128
        nt = 8192 // n
        h1 = Pair(sb_aligned(nt, n), sb_aligned(nt, n))
        O = sb(ntok, 1024)
        W = I["w_ff2"][i]
        gate = gate_cols(i, "g_post_ff", 5)
        for part in range(32 // nt):
            ready, later = [], []
            was = done() if part else xr
            for j in range(nt):
                if j % 2 == 0:
                    w = cols(I["w_ff1"][i], (part * nt + j) * 128, 256)
                if n == 512 and part == 0 and j == 0:
                    two_ = fm_first(w, X, xr)
                b, t = two_[j] if n == 512 and part == 0 and j < 2 else fm(w, (j % 2) * 128, X, n, xr if j == 0 else ())
                if j % 2:
                    wfree(w, t)
                raw, hi = h1.lo[:, j, :], h1.hi[:, j, :]
                if n == 512 or j % 2:
                    t1 = act(raw, b[:, 0:n], ACT.Relu, [t, *was])
                    give(b, t1)
                    t1 = tt(raw, raw, raw, MUL, [t1], q=GP if n == 256 else VE)
                else:
                    t1 = act(raw, b[:, 0:n], ACT.Relu, [t, *was])
                    give(b, t1)
                    t1 = tt(raw, raw, raw, MUL, [t1])
                later.append((raw, hi, raw, [t1]))
                if len(later) > 2:
                    ready.append([split(*later.pop(0))])
                if part == 0 and j == 3:
                    gate_rows(gate, ntok // 2, [VE.last()])
            ready += [[split(*x)] for x in later]
            parts = [(W, part * nt + k, 8) for k in range(0, nt, 8)]
            end = part == 32 // nt - 1
            x_read = [PE.last()]
            out_proj(parts, h1, ntok, O, (), ready, part > 0, end,
                     [normed(k, gain, shift, residual(O), x_read) for k in range(ntok)] if end else ())
        return x_ready()

    def attend(items, after):
        wide = 512 if max(it["n"] for it in items) > 256 else 256
        NP, NT = 2048 // wide, 1536 // wide
        P = [GB.rearrange("p a b -> p (a b)")[:, i * wide:i * wide + wide] for i in range(NP)]
        PT = [extra[:, i * wide:i * wide + wide] for i in range(NT)]
        lag = NP - 1 if NP == 4 else 5
        st = sb(NP, 8)
        p_free, pt_free = [()] * NP, [()] * NT
        ready, obank = {}, [None]

        def first(i):
            it = items[i]
            n = it["n"]
            b, free = take()
            for x, (l, r, c0, c1) in enumerate(it["mms"]):
                t = mm(b[:, c0:c1], l, r, x == 0, x == len(it["mms"]) - 1,
                       [*free, *(after if i == 0 else ())] if x == 0 else ())
            s = st[:, i % NP, :]
            p = P[i % NP][:, 0:n]
            rmax(s[:, 0:1], b[:, 0:n], [t, *p_free[i % NP]])
            if it.get("sink") is not None:
                t = ts(s[:, 1:2], s[:, 0:1], it["sink"], -1.0, MAX, MUL)
            else:
                t = ts(s[:, 1:2], s[:, 0:1], -1.0, None, MUL)
            t = act(p, b[:, 0:n], ACT.Exp, [t, *(after if i < NP else ())], bias=s[:, 1:2], accum_out=s[:, 2:3])
            give(b, t)
            if it.get("sink") is not None:
                t = act(s[:, 3:4], it["sink"], ACT.Exp, bias=s[:, 1:2])
            ready[i] = t

        def scaled(i):
            it, t = items[i], ready[i]
            s, p = st[:, i % NP, :], P[i % NP][:, 0:it["n"]]
            if it.get("sink") is not None:
                t = tt(s[:, 2:3], s[:, 2:3], s[:, 3:4], ADD, [t])
            if it.get("m01") is not None:
                t = tt(p, p, it["m01"], MUL, [t])
            recip(s[:, 4:5], s[:, 2:3], [t])
            if it.get("gate") is not None:
                t = ts(p, p, s[:, 4:5], it["gate"], MUL, MUL)
            else:
                t = ts(p, p, s[:, 4:5], None, MUL)
            ready[i] = t

        def second(i):
            it = items[i]
            b, free = take()
            for x, (c0, kw, _) in enumerate(it["kts"]):
                t = tr(b[0:kw, x * 128:x * 128 + 128], P[i % NP][:, c0:c0 + kw], ident,
                       [ready[i], *free] if x == 0 else ())
            p_free[i % NP] = (t,)
            nk = len(it["kts"])
            kw = max(k for _, k, _ in it["kts"])
            t = act(PT[i % NT][0:kw, 0:nk * 128], b[0:kw, 0:nk * 128], ACT.Copy, [t, *pt_free[i % NT], *(after if i < NT else ())])
            give(b, t)
            ready[i] = t

        def third(i):
            it = items[i]
            if it["open"]:
                obank[0] = take()
            b, free = obank[0]
            po, oc = it["po"], it["oc"]
            for x, (c0, kw, v) in enumerate(it["kts"]):
                t = mm(b[po:po + 64, oc:oc + 128], v, PT[i % NT][0:kw, x * 128:x * 128 + 128],
                       it["begin"] and x == 0, it["end"] and x == len(it["kts"]) - 1,
                       [ready[i], *free] if x == 0 else ())
            pt_free[i % NT] = (t,)
            if it["close"] is not None:
                tv = cp(it["close"], b[:, 0:256], [t])
                give(b, tv)

        for i in range(len(items) + lag + 1):
            if 0 <= i - lag < len(items):
                second(i - lag)
            if i < len(items):
                first(i)
            if 0 <= i - 1 < len(items):
                scaled(i - 1)
            if 0 <= i - lag - 1 < len(items):
                third(i - lag - 1)
            yield

    def rotate(x, n, R, cos, sin, tmp, after, outs=None):
        b, free = take()
        t = mm(b[:, 0:n], R, x, after=[*after, *free])
        t1 = tt(tmp, b[:, 0:n], sin, MUL, [t])
        give(b, t1)
        tt(x, x, cos, MUL)
        for i, o in enumerate(outs or ()):
            s = slice(64 * i, 64 * i + 64)
            t = tt(o[s], x[s], tmp[s], ADD)
        return t if outs else tt(x, x, tmp, ADD)

    def head_sums(x, sq, n, after, scale=None):
        k = {} if scale is None else {"scale": scale}
        t = act(sq, x, ACT.Square, after, **k)
        b, free = take()
        t = mm(b[:, 0:n], bones, sq, after=[t, *free])
        return b, t

    stores = []

    at_x = lambda i: (lambda f, s: DER[:, i, f, s:s + 1], lambda f, s: MOD[i][:, f, s:s + 1])
    h_here = []
    tiles = [normed(k, *at_x(0), after=h_here) for k in range(4)]
    t_h, t_v = load_h(), []
    h_here.append(t_h)
    assert len(pairs) <= 42
    for n, _ in enumerate(modulation(0, 0, 8)):
        few, pairs = pairs[:6], pairs[6:]
        if few:
            t_v.append(load(SC, few))
        if n == 5:
            for g in tiles * 3:
                next(g)
    del live[NSLOT:]
    high_free[:] = ring_free[NSLOT:]
    b, free = take()
    for i in range(1, 4):
        n = min(128, row - i * 128)
        t = tr(b[:, i * 128:i * 128 + n], VR[i][0:n, :], ident[0:n, 0:n], [*t_v, *free] if i == 1 else ())
    t = cp(VC[:, 128:row], b[:, 128:row], [t])
    give(b, t)
    top[0] = mark
    gains(0, "g_pre_mix", 1, 0)
    staggered(tiles)
    xr = x_ready()
    m_layer = top[0]
    OT = sb_aligned(8, 512)
    m_out = top[0]
    pA = sb(15, 512)
    m_b = top[0]
    qB, qZ = sb(4, 256), sb(8, 512)
    kB = sb(2, 512)
    vB = sb(4, 128)
    PT0 = GB[:, 0, 0:512]
    Rx, cosx, sinx, wmask = sb(128), sb(256), sb(256), sb(2, 256)
    snk = sb(8)
    mu0 = sb(15)
    t_z = zero(qZ, done())
    t_c = load(SC, [(Rx, C["Rax"]), (cosx, C["cosax"]), (sinx, C["sinax"]), (wmask, C["wmask"]),
                    (snk[0:1, :], I["b_sink"])], done())
    tt(mu0, col("a_mu_prev", 0, 15), col("a_mu_next", 0, 15), ADD)
    ts(mu0, mu0, -1.0, 1.0, MUL, ADD)
    W = I["w_in_even"][0]
    xb = xr

    def a_proj():
        for j in range(15):
            if j % 2 == 0:
                w = cols(W, j * 128, min(256, 1920 - j * 128))
            b, t = fm(w, (j % 2) * 128, X, 512)
            if j % 2 or j == 14:
                wfree(w, t)
            o = pA[:, j, :].rearrange("p (s t) -> p s t", s=2)
            i = b[:, :].rearrange("p (s t) -> p s t", s=2)
            t = act(pA[:, j, :], b[:, :], ACT.Identity, [t], scale=mu0[:, j:j + 1])
            stt(o[:, :, 1:256], i[:, :, 0:255], col("a_mu_prev", j), o[:, :, 1:256], MUL, ADD, [t])
            t = stt(o[:, :, 0:255], i[:, :, 1:256], col("a_mu_next", j), o[:, :, 0:255], MUL, ADD)
            give(b, t)
            yield
        act(pA[:, 12, :], pA[:, 12, :], ACT.Tanh, [t])
        act(pA[:, 14, :], pA[:, 14, :], ACT.Sigmoid)

    for j in range(4):
        if j % 2 == 0:
            w = cols(W, 1920 + j * 128, 256)
        if j == 0:
            first = fm_first(w, X, xb)
        b, t = first[j] if j < 2 else fm(w, (j % 2) * 128, X, 512)
        if j % 2:
            wfree(w, t)
        t = ts(qB[:, j, :], b[:, 0:256], 0.125, None, MUL, None, [t, t_z])
        for i in range(2):
            s = slice(64 * i, 64 * i + 64)
            t = ts(qZ[s, 2 * j + i, 256:512], b[s, 256:512], 0.125, None, MUL)
        give(b, t)
    w = cols_of(W, [(2432, 64), (2432, 64), (2496, 64), (2496, 64)])
    for g in range(2):
        b, t = fm(w, g * 128, X, 512)
        t1 = ev(kB[:, g, :], b[:, :], [t])
        give(b, t1)
    wfree(w, t)
    w = cols(W, 2560, 128)
    b, t = by_tokens(w, 0, X, 4, PT0)
    wfree(w, t)
    t1 = ev(vB, b[:, :].rearrange("p (k f) -> p k f", k=4), [t])
    give(b, t1)
    b, free = take()
    zero(tiny[0:1, 63:64], done(), VE)
    one = sb(128)
    t = zero(one, (), VE, 1.0)
    t = mm(b[:, 0:8], one[0:1, :], snk[0:1, :], after=[t, t_c, *free])
    snkb = sb(8)
    t = cp(snkb, b[:, 0:8], [t])
    give(b, t)
    tmp = sb(256)

    def b_rotate():
        t = [t_c, *done()]
        for j in range(4):
            rotate(qB[:, j, :], 256, Rx, cosx, sinx, tmp, t, [qZ[:, 2 * j + i, 0:256] for i in range(2)])
            yield
        for g in range(2):
            rotate(kB[:, g, 0:256], 256, Rx, cosx, sinx, tmp, t)
            yield
        yield from by(3, attend(items, [VE.last()]))

    items = []
    for pair in range(4):
        for h in (2 * pair, 2 * pair + 1):
            po, g = 64 * (h % 2), h // 4
            for qt in range(2):
                q = qZ[:, h, qt * 128:qt * 128 + 128]
                items.append(dict(
                    n=512, mms=[(q, kB[:, g, 0:512], 0, 512), (ident, wmask[:, qt, :], 0, 256)],
                    sink=snkb[:, h:h + 1], po=po, oc=qt * 128, begin=True, end=True,
                    kts=[(k * 128, 128, vB[:, k, g * 64:g * 64 + 64]) for k in range(4)],
                    open=h % 2 == 0 and qt == 0, close=OT[:, 4 + pair, 0:256] if h % 2 and qt else None))
        for h in (2 * pair, 2 * pair + 1):
            po, g = 64 * (h % 2), h // 4
            for qt in range(2):
                q = qZ[:, h, 256 + qt * 128:256 + qt * 128 + 128]
                items.append(dict(
                    n=256, mms=[(q, kB[:, g, 256:512], 0, 256)],
                    sink=snkb[:, h:h + 1], po=po, oc=qt * 128, begin=True, end=True,
                    kts=[(k * 128, 128, vB[:, 2 + k, g * 64:g * 64 + 64]) for k in range(2)],
                    open=h % 2 == 0 and qt == 0, close=OT[:, 4 + pair, 256:512] if h % 2 and qt else None))
    run(a_proj(), b_rotate(), slowed(modulation(0, 8, 16)))
    barrier()
    top[0] = m_b

    CH0 = math.exp(-0.5)
    NCH = 4
    del live[1:]
    spare = [(xt_at, xt_at + 8192), (ring_top - 6144, high_top), (gb_at, gb_at + 2048), (h_at, h_at + 4096)]

    def sp(*shape):
        n = 1
        for x in shape:
            n *= x
        for i, (a0, a1) in enumerate(spare):
            if a1 - a0 >= n:
                spare[i] = (a0 + n, a1)
                keep, top[0] = top[0], a0
                r = sb(*shape)
                top[0] = keep
                return r
        return sb(*shape)

    sets = []
    for _ in range(4):
        z = Slot()
        z.P, z.Q, z.T, z.TT, z.LT, z.LK = [sp(NCH, 128) for _ in range(6)]
        z.MB, z.MK = [sp(NCH, 64) for _ in range(2)]
        sets.append(z)
    wide = [extra[:, i * 1024:i * 1024 + 1024] for i in range(3)]
    AR = [[sp(2, 512) for _ in range(2)], [a.rearrange("p (a b) -> p a b", a=2) for a in wide[0:2]]]
    BE = [[sp(512) for _ in range(2)], [wide[2][:, 0:512], wide[2][:, 512:1024]]]
    KA = [[sp(512) for _ in range(2)] for _ in range(2)]
    VB = [sp(8, 128) for _ in range(2)]
    ET, FF = [[sb(8, 128) for _ in range(2)] for _ in range(2)]
    RT = [sb(8, 64) for _ in range(2)]
    kb, sg, cu, ex, kk = [sp(512) for _ in range(5)]
    w2s, a2s, scanm = [sp(512) for _ in range(3)]
    g2s = sb(512)
    tri, incl, lvl = sp(2, 128), sp(2, 64), sp(2, 6, 128)
    PC = sp(2, 8)
    Zb = extra[:, 3072:3584].rearrange("p (a b c) -> p a b c", a=2, b=2)
    ka1 = sp(4)
    start = done()
    t_c = load(SP, [(w2s, I["a_w2"][0].rearrange("d l c -> (d l) c")), (a2s, I["a_a2"][0].rearrange("d l c -> (d l) c")),
                    (g2s, I["a_g2"][0]), (scanm, C["scanm"]), (lvl, C["lvl"]), (tri, C["tri"]), (incl, C["incl"])], start)
    for a in VB:
        t_zero = zero(a, start)
    c8 = lambda a: a.rearrange("p (c t) -> p c t", t=64)
    for z in sets:
        zero(z.P, start)
        z.free = [zero(z.Q)]
    ts(ka1, col("a_k_a", 0, 4), -1.0, 1.0, MUL, ADD)
    v4 = lambda b: b[:, :].rearrange("p (c t) -> p c t", t=128)
    twice = lambda a: a.unsqueeze(2).to_broadcast([128, NCH, 2, 64])
    two = lambda a: a.rearrange("p c (h t) -> p c h t", h=2)
    HV = [(0, 64), (64, 128)]

    def product(l, r, after, n=128):
        b, free = take()
        l, r = (x if isinstance(x, list) else [x] for x in (l, r))
        for c in range(NCH):
            for i in range(len(l)):
                t = mm(b[:, c * n:c * n + n], l[i](c), r[i](c), i == 0, i == len(l) - 1,
                       [*after, *free] if c == 0 and i == 0 else ())
        return b, t

    def turned(src, dst, after):
        b, free = take()
        for c in range(3):
            tr(b[:, c * 128:c * 128 + 128], src[:, c * 64:c * 64 + 128], ident, [*after, *free] if c == 0 else ())
        mm(b[0:64, 384:448], src[:, 192:256], ident[:, 0:64])
        t = mm(b[64:128, 448:512], src[:, 0:64], ident[:, 64:128])
        cp(dst[0:64, :, 0:64], v4(b)[0:64, :, 0:64], [t], SC)
        cp(dst[64:128, 1:4, 64:128], v4(b)[64:128, 0:3, 64:128], (), SC)
        t = cp(dst[64:128, 0, 64:128], v4(b)[64:128, 3, 64:128], (), SC)
        give(b, t)
        return t

    at_ = lambda m: (lambda c: m[:, c, :])

    def unit(z, p, d, half):
        ar, be, ka, Vbd, PN = AR[p % 2], BE[p % 2], KA[p % 2], VB[p % 2], PNs[p]
        c0 = half * NCH
        w0, w1 = c0 * 64, c0 * 64 + 256
        arv = ar[d].rearrange("p a (c t) -> p c a t", t=64)[:, c0:c0 + NCH]
        bev, kav, vv = (a[:, c0:c0 + NCH, :] for a in (c8(be[d]), c8(ka[d]), Vbd))
        while (p, d) not in prepared:
            yield
        ok = prepared[p, d]
        for h0, h1 in HV:
            cp(z.P[h0:h1, :, h0:h1], bev[h0:h1], [*z.free, *ok], SC)
            cp(z.Q[h0:h1, :, h0:h1], kav[h0:h1], [*z.free, *ok], GP)
        dep = [SC.last(), GP.last(), *ok, *z.free]
        yield
        b, t = product(at_(z.P), at_(arv), dep)
        tl = tt(two(z.LT), twice(v4(b)[:, :, 0:64]), two(tri[:, d:d + 1, :].to_broadcast([128, NCH, 128])), MUL, [t, t_c])
        b2, t2 = product(at_(z.Q), at_(arv), dep)
        t = cp(z.MB, v4(b)[:, :, 64:128], [tl], SC)
        give(b, t)
        cp(two(z.LK), twice(v4(b2)[:, :, 0:64]), [t2], SC)
        t2 = cp(z.MK, v4(b2)[:, :, 64:128], (), SC)
        give(b2, t2)
        tt(two(z.LK), two(z.LK), two(tri[:, d:d + 1, :].to_broadcast([128, NCH, 128])), MUL, [t2, t_c], q=GP)
        for m in (z.MB, z.MK):
            tm_ = tt(m, m, incl[:, d:d + 1, :].to_broadcast([128, NCH, 64]), MUL, q=GP)
        yield
        lm = lambda d_, l: two(lvl[:, d_, l:l + 1, :].to_broadcast([128, NCH, 128]))
        idc = ident.unsqueeze(1).to_broadcast([128, NCH, 128])
        tt(two(z.TT), two(z.LT), lm(1 - d, 0), MUL)
        t = tt(z.TT, idc, z.TT, SUB)
        yield
        for l in range(1, 6):
            b, free = take()
            for c in range(NCH):
                t1 = tr(b[:, c * 128:c * 128 + 128], z.TT[:, c, :], ident, [t, *free] if c == 0 else ())
            t1 = cp(z.T, v4(b), [t1], SC)
            give(b, t1)
            yield
            b, t = product(at_(z.LT), at_(z.T), [t1])
            t = tt(two(z.P), two(v4(b)), lm(d, l), MUL, [t])
            give(b, t)
            yield
            b, t2 = product(at_(z.P), at_(z.TT), [t])
            t = tt(z.TT, z.TT, v4(b), SUB, [t2])
            give(b, t)
            yield
        b, t1 = product(at_(z.LK), at_(vv), [t, tm_])
        t1 = cp(z.Q, v4(b), [t1], SC)
        give(b, t1)
        t2 = turned(ar[d][:, 0, w0:w1], z.LT, [t])
        yield
        b, t3 = product(at_(z.TT), at_(z.LT), [t2])
        t3 = act(z.P, v4(b), ACT.Copy, [t3], scale=-1.0)
        give(b, t3)
        b, t4 = product(at_(z.TT), at_(z.Q), [t1])
        t4 = act(z.T, v4(b), ACT.Copy, [t4], scale=-1.0)
        give(b, t4)
        yield
        while chains:
            yield
        b, t = product(at_(z.P), at_(z.MB), [t3, tm_], 64)
        t = tt(RT[d][:, c0:c0 + NCH, :], c8(b[:, 0:256]), arv[:, :, 1, :], ADD, [t, *chain_read])
        give(b, t)
        turned(be[d][:, w0:w1], z.LK, [t3])
        t5 = turned(ka[d][:, w0:w1], z.TT, [t4])
        yield
        b, t = product(at_(z.P), at_(z.LK), [t5])
        t = tt(ET[d][:, c0:c0 + NCH, :], v4(b), idc, ADD, [t])
        give(b, t)
        b, t = product([at_(z.TT), at_(z.LK)], [at_(vv), at_(z.T)], [t5])
        t = tt(FF[d][:, c0:c0 + NCH, :], v4(b), PN[:, d, c0:c0 + NCH].unsqueeze(2).to_broadcast([128, NCH, 128]), MUL, [t])
        give(b, t)
        b, t = product([at_(vv), at_(z.T)], [at_(z.MK), at_(z.MB)], [t4], 64)
        y = c8(OT[:, p, :])[:, c0:c0 + NCH, :]
        t = cp(y, c8(b[:, 0:256]), [t]) if d == 0 else tt(y, y, c8(b[:, 0:256]), ADD, [t])
        give(b, t)
        z.free = [t]

    def prepare(p, free_):
        ar, be, ka, Vbd, PN = AR[p % 2], BE[p % 2], KA[p % 2], VB[p % 2], PNs[p]
        LQ = GP if p else VE
        r, k, v = pA[:, p, :], pA[:, 4 + p, :], pA[:, 8 + p, :]
        b, t = head_sums(k, sg, 512, [*free_, *sg_read], col("a_k_k", p))
        yield
        t = ts(sg, b[:, :], 1e-24, None, MAX, None, [t])
        give(b, t)
        t = act(sg, sg, ACT.Sqrt, [t])
        yield
        for i in range(4):
            recip(sg[:, 128 * i:128 * i + 128], sg[:, 128 * i:128 * i + 128], [t])
            yield
        tv = stt(kk, k, col("a_k_k", p), sg, MUL, MUL, cu_read)
        for q in range(2):
            turned(v[:, 256 * q:256 * q + 256], Vbd[:, 4 * q:4 * q + 4, :], [*free_, t_zero])
            yield
        for d in range(2):
            s = slice(64 * d, 64 * d + 64)
            b, free = take()
            t = mm(b[:, :], w2s[s, p * 128:p * 128 + 128], pA[s, 12, :], after=[t_c, *free_, *free])
            t = act(sg, b[:, :], ACT.Sigmoid, [t, tv], bias=col("a_w0", 4 * d + p))
            give(b, t)
            b, free = take()
            t2 = mm(b[:, :], a2s[s, p * 128:p * 128 + 128], pA[s, 13, :], after=free)
            t2 = act(be[d], b[:, :], ACT.Sigmoid, [t2], bias=col("a_a0", 4 * d + p))
            give(b, t2)
            yield
            tv = VE.add(lambda e: e.tensor_tensor_scan(cu, scanm, sg, 0.0, MUL, ADD), [t, *cu_read])
            t = act(PC[:, d, :], c8(cu)[:, :, 63], ACT.Exp, [tv], scale=-CH0)
            if d == 0:
                tt(c8(ex), c8(cu)[:, :, 63:64].to_broadcast([128, 8, 64]), c8(cu), SUB)
                tv = tt(cu, ex, sg, ADD, [t])
            else:
                tv = tt(ex, cu, sg, SUB)
            yield
            t = act(sg, ex, ACT.Exp, [tv], scale=-CH0)
            act(ex, ex, ACT.Exp, scale=CH0)
            t1 = act(cu, cu, ACT.Exp, scale=CH0)
            t2 = ts(ka[d], be[d], col("a_k_a", p), ka1[:, p:p + 1], MUL, ADD, [t2])
            tt(ka[d], ka[d], k, MUL, [t2], q=LQ)
            if d == 0:
                cp(kb, ka[d], (), LQ)
            else:
                tt(kb, kb, ka[d], ADD, q=LQ)
            yield
            tt(be[d], be[d], kk, MUL, q=LQ)
            tt(be[d], be[d], sg, MUL, [t], q=LQ)
            tv = tt(ka[d], ka[d], sg, MUL, q=LQ)
            yield
            tt(ar[d][:, 0, :], cu, kk, MUL, [t1], q=LQ)
            cu_read[:] = [tt(ar[d][:, 1, :], ex, r, MUL, q=LQ)]
            if d == 0:
                cp(PN[:, d, 0:7], PC[:, d, 1:8], [t1])
                cp(PN[:, d, 7:8], PC[:, d, 0:1])
            else:
                cp(PN[:, d, 1:8], PC[:, d, 0:7], [t1])
                cp(PN[:, d, 0:1], PC[:, d, 7:8])
            prepared[p, d] = [SC.last(), VE.last(), GP.last()]
            yield
        t = stt(kb, kb, col("a_r_k", p), r, MUL, MUL, cu_read)
        b, free = take()
        t = mm(b[:, :], bones, kb, after=[t, *free])
        t = tt(k, b[:, :], v, MUL, [t])
        give(b, t)
        sg_read[:] = [t]

    order = [[4, 5, 6, 7, 0, 1, 2, 3], [7, 6, 5, 4, 3, 2, 1, 0]]
    chains = []

    def chain(p, finished, pn):
        dep = finished
        yacc, tmp = OT[:, p, :], pA[:, p, :]
        z = [FF[d][:, order[d][0], :] for d in range(2)]
        for i in range(1, 8):
            cs = [order[d][i] for d in range(2)]
            if i < 7:
                b, free = take()
                for d in range(2):
                    t = mm(b[:, d * 128:d * 128 + 128], ET[d][:, cs[d], :], z[d], after=[*dep, *free] if d == 0 else ())
                zn = [Zb[:, i % 2, d, :] for d in range(2)]
                for d in range(2):
                    tz = stt(zn[d], b[:, d * 128:d * 128 + 128], pn[:, d, cs[d]:cs[d] + 1], FF[d][:, cs[d], :], MUL, ADD, [t])
                give(b, tz)
            b2, free2 = take()
            for d in range(2):
                t = mm(b2[:, d * 64:d * 64 + 64], z[d], RT[d][:, cs[d], :], after=[*dep, *free2] if d == 0 else ())
            chain_read[:] = [t]
            for d in range(2):
                y = yacc[:, cs[d] * 64:cs[d] * 64 + 64]
                t = tt(y, y, b2[:, d * 64:d * 64 + 64], ADD, [t])
            give(b2, t)
            z, dep = zn, [tz]
            yield
        chains.pop(0)
        t_y = VE.last()
        yield
        b, free = take()
        t = mm(b[:, :], bones, yacc, after=[t_y, *free])
        t = stt(yacc, b[:, :], -1.0 / 64, yacc, MUL, ADD, [t])
        give(b, t)
        yield
        b, t = head_sums(yacc, tmp, 512, [t])
        t = ts(tmp, b[:, :], 1.0 / 64, 64e-5, MUL, ADD, [t])
        give(b, t)
        t = act(tmp, tmp, ACT.Sqrt, [t])
        yield
        for i in range(4):
            recip(tmp[:, 128 * i:128 * i + 128], tmp[:, 128 * i:128 * i + 128], [t])
            yield
        tt(yacc, yacc, tmp, MUL)
        ts(yacc, yacc, col("a_gn_w", p), col("a_gn_b", p), MUL, ADD)
        tt(yacc, yacc, pA[:, 4 + p, :], ADD)
        b, free = take()
        t = mm(b[:, :], g2s[:, p * 128:p * 128 + 128], pA[:, 14, :], after=free)
        t = tt(yacc, b[:, :], yacc, MUL, [t])
        give(b, t)

    PNs = [sp(2, 8) for _ in range(4)]
    cu_read, sg_read, chain_read, prepared, pending = [], [], [], {}, []
    now = prepare(0, start)
    while (0, 0) not in prepared:
        next(now)
    left = iter([(0, i) for i in range(16, 24)] + [(1, i) for i in range(24)])

    def conditions(n):
        for i, f in [x for _, x in zip(range(n), left)]:
            for t in modulation(i, f, f + 1):
                yield
                yield

    for p in range(4):
        units = [unit(sets[2 * d + h], p, d, h) for d in range(2) for h in range(2)]

        def coming(now, free_):
            yield from now
            if p < 3:
                for _ in range(2 if p else 0):
                    yield
                yield from prepare(p + 1, free_)

        run(*pending, *units, coming(now, [*start, *([] if p == 0 else ended)]), conditions(8))
        now = ()
        chains.append(p)
        ended = done()
        pending = [chain(p, ended, PNs[p])]
    gate = gate_cols(0, "g_post_mix", 2)
    live.extend((1, 2, 3))
    ring_free[1:NSLOT] = [tuple(ended)] * 3
    high_free[:] = [tuple(ended)] * 3
    here()
    OP = Pair(XH, OT)
    FIRST = [4, 5, 6, 7, 0, 1, 2, 3]
    ready = {}

    def others():
        for k in FIRST[:7]:
            cp(rr(OP.hi[:, k, :]), OT[:, k, :], ended, GP)
            ready[k] = [tt(rr(OT[:, k, :]), OT[:, k, :], rr(OP.hi[:, k, :], F32), SUB, q=GP)]
            yield

    assert all(a.offset % AREA >= high_top and not gb_at <= a.offset % AREA < gb_at + 2048 for b in (ET, FF, RT, [g2s]) for a in b)
    run(*pending, others(), slowed(gate_rows_(gate, 2, ended)))
    ready[3] = [split(OT[:, 3, :], OP.hi[:, 3, :], OT[:, 3, :], done())]
    was = [VE.last(), SC.last(), GP.last()]
    t_h = load_h(done())
    top[0] = m_out
    O = sb(4, 1024)
    gains(0, "g_pre_ff", 4, 1)
    ff_x = lambda i, d: (lambda f, s: DER[:, d, f, s:s + 1], lambda f, s: MOD[i][:, 24 + f, s:s + 1])
    out_proj([(I["w_out"][0], 0, 8)], OP, 4, O, (), ready, gate=True, order=FIRST,
             then=[normed(k, *ff_x(0, 1), residual(O, [t_h]), [t_h, *was]) for k in range(4)])
    xr = x_ready()
    barrier([VE, SC, GP])
    top[0] = m_layer
    gains(1, "g_pre_mix", 1, 2)
    xr = ffn(0, 4, xr, lambda f, s: DER[:, 2, f, s:s + 1], lambda f, s: MOD[1][:, f, s:s + 1])

    barrier([VE, SC, GP])
    top[0] = m_layer
    OT = sb_aligned(8, 256)
    m_c = top[0]
    Rx, cosx, sinx, cmask, flipm = sb(128), sb(256), sb(256), sb(256), sb(128)
    t_c = load(SC, [(Rx, C["Rax"]), (cosx, C["cosax"]), (sinx, C["sinax"]), (cmask, C["cmask"]), (flipm, C["flip"])], done())
    bias = sb(2, 8, 256)
    rp = I["c_rpb"]
    pairs = []
    for qt in range(2):
        for rq in range(2):
            for h in range(8):
                src = bass.AP(tensor=rp.tensor, offset=rp.offset + (h * 15 + 7 - (2 * qt + rq)) * 31 + 15 - 63,
                              ap=[[1, 64], [31, 4], [1, 64]])
                pairs.append((bias[rq * 64:rq * 64 + 64, qt, h, :].rearrange("p (a b) -> p a b", a=4), src))
    at_start = done()
    qC, kC, vC = sb(8, 256), sb(4, 512), sb(4, 512)
    PT0 = GB[:, 0, 0:512]
    qD, qZ, kD, vD = sb(4, 256), sb(8, 256), sb(2, 512), sb(4, 128)
    zero(qC, done())
    t_z = zero(qZ)
    W = I["w_in_odd"][0]
    for j in range(4):
        if j % 2 == 0:
            w = cols(W, 1536 + j * 128, 256)
        b, t = fm(w, (j % 2) * 128, X, 256, xr[:4])
        if j % 2:
            wfree(w, t)
        t = ev(qD[:, j, :], b[:, 0:256], [t])
        give(b, t)
    w = cols_of(W, [(2048, 64), (2048, 64), (2112, 64), (2112, 64)])
    for g in range(2):
        b, t = fm(w, g * 128, X, 512, xr)
        t1 = ev(kD[:, g, :], b[:, :], [t])
        give(b, t1)
    wfree(w, t)
    w = cols(W, 2176, 128)
    b, t = by_tokens(w, 0, X, 4, PT0)
    wfree(w, t)
    t1 = ev(vD, b[:, :].rearrange("p (k f) -> p k f", k=4), [t])
    give(b, t1)
    t_b = load(SP, pairs, at_start)

    def c_proj():
        for j in range(4):
            if j % 2 == 0:
                w = cols(W, j * 128, 256)
            b, t = fm(w, (j % 2) * 128, X, 256)
            if j % 2:
                wfree(w, t)
            for i in range(2):
                s = slice(64 * i, 64 * i + 64)
                t = ts(qC[s, 2 * j + i, :], b[s, 0:256], 0.125, None, MUL, None, [t, t_z])
            give(b, t)
            yield
        for j in range(4):
            if j % 2 == 0:
                w = cols(W, 512 + j * 128, 256)
            b, t = fm(w, (j % 2) * 128, X, 512)
            if j % 2:
                wfree(w, t)
            t = ev(kC[:, j, :], b[:, :], [t])
            give(b, t)
            yield
        for j in range(2):
            w = cols(W, 1024 + j * 256, 256)
            for k in range(4):
                b, t = tm(w, 0, 256, X, k)
                t1 = ev(vC[:, k, j * 256:j * 256 + 256], b[:, 0:256], [t])
                give(b, t1)
                yield
            wfree(w, t)

    for qt in range(2):
        tt(bias[:, qt, :, :], bias[:, qt, :, :], cmask.unsqueeze(1).to_broadcast([128, 8, 256]), ADD, [t_c, t_b], q=GP)
    TMP, SQ = [sb(512) for _ in range(2)], [sb(512) for _ in range(2)]
    qg = sb(1)
    ts(qg, col("d_q_gain"), 0.125, None, MUL)

    def d_rotate(n_):
        tmp, sq = TMP[n_], SQ[n_]
        start, was = done(), ()
        for x, n, g, o in ([(qD[:, j, :], 256, qg, [qZ[:, 2 * j, :], qZ[:, 2 * j + 1, :]]) for j in range(4)] +
                           [(kD[:, j, :], 512, col("d_k_gain"), None) for j in range(2)])[n_::2]:
            b, t = head_sums(x, sq[:, 0:n], n, start)
            yield
            t = ts(tmp[:, 0:n], b[:, 0:n], 1.0 / 64, 1e-6, MUL, ADD, [t, *was])
            give(b, t)
            t = act(tmp[:, 0:n], tmp[:, 0:n], ACT.Sqrt, [t])
            yield
            recip(tmp[:, 0:n], tmp[:, 0:n], [t])
            yield
            t = stt(x, x, g, tmp[:, 0:n], MUL, MUL)
            yield
            rotate(x[:, 0:256], 256, Rx, cosx, sinx, tmp[:, 0:256], [t_c, t], o)
            yield

    run(c_proj(), d_rotate(0), d_rotate(1))
    items = []
    for kind in "CD":
        for pair in range(4):
            for h in (2 * pair, 2 * pair + 1):
                po, g = 64 * (h % 2), h // 4
                for qt in range(2):
                    s = slice(qt * 128, qt * 128 + 128)
                    if kind == "C":
                        mms = [(qC[:, h, s], kC[:, pair, :], 0, 512), (flipm, bias[:, qt, h, :], 0, 256)]
                        kts = [(k * 128, 128, vC[:, k, h * 64:h * 64 + 64]) for k in range(4)]
                    else:
                        mms = [(qZ[:, h, s], kD[:, g, :], 0, 512)]
                        kts = [(k * 128, 128, vD[:, k, g * 64:g * 64 + 64]) for k in range(4)]
                    dst = OT[:, (0 if kind == "C" else 4) + pair, :]
                    items.append(dict(n=512, mms=mms, po=po, oc=qt * 128, begin=True, end=True, kts=kts,
                                      open=h % 2 == 0 and qt == 0, close=dst if h % 2 and qt else None))
    run(attend(items, done()))
    barrier()
    top[0] = m_c
    OP = Pair(sb_aligned(8, 256), OT)
    gate_rows(gate_cols(1, "g_post_mix", 2), 1, done())
    ready = []
    for k in range(0, 8, 2):
        ready += [[split(OT[:, k:k + 2, :], OP.hi[:, k:k + 2, :], OT[:, k:k + 2, :], ())]] * 2
    O = sb(2, 1024)
    gains(1, "g_pre_ff", 4, 3)
    x_read = [PE.last()]
    out_proj([(I["w_out"][1], 0, 8)], OP, 2, O, (), ready, gate=True,
             then=[normed(k, *ff_x(1, 3), residual(O), x_read) for k in range(2)])
    xr = x_ready()
    barrier([VE, SC, GP])
    top[0] = m_layer
    xr = ffn(1, 2, xr, lambda f, s: col("norm_mix_w_2", f), None)

    barrier([VE, SC, GP])
    top[0] = m_layer
    W = I["w_in_2"][0]
    oN, oNh = sb_aligned(4, 256), sb(4, 256)
    ga = sb(2, 2048)
    qr, kr, vr, gr = sb(4, 256), sb(4, 256), sb(2, 1024), sb(2, 1024)
    Rr, cosr, sinr, tmpr = sb(128), sb(256), sb(256), sb(256)
    m_n = top[0]
    Rn, cosn, sinn, caus, cm, c01 = sb(128), sb(256), sb(256), sb(128), sb(2, 16), sb(2, 16)
    w2k, w2v = sb(2, 128), sb(2, 64)
    t_r = load(SC, [(Rr, C["Rret"]), (cosr, C["cosret"]), (sinr, C["sinret"])], done())
    t_c = load(SC, [(Rn, C["Rnsa"]), (cosn, C["cosnsa"]), (sinn, C["sinnsa"]), (caus, C["caus"]), (cm, C["cmpm"]), (c01, C["cmp01"]),
                    (w2k[:, :, 0:64], I["cmp_w2_k_2"][0].rearrange("(t p) d -> p t d", p=128)),
                    (w2k[:, :, 64:128], I["cmp_w2_k_2"][0].rearrange("(t p) d -> p t d", p=128)),
                    (w2v, I["cmp_w2_v_2"][0].rearrange("(t p) d -> p t d", p=128))], done())
    q, qZ = sb(4, 256), sb(8, 256)
    t_z = zero(qZ, done())
    for j in range(4):
        if j % 2 == 0:
            w = cols(W, j * 128, 256)
        b, t = fm(w, (j % 2) * 128, X, 256, xr)
        if j % 2:
            wfree(w, t)
        t = ts(q[:, j, :], b[:, 0:256], 0.125, None, MUL, None, [t])
        give(b, t)
    kv = {}
    for nm, c0 in (("kc", 512), ("vc", 640), ("ks", 768), ("kw", 1024)):
        kv[nm] = sb(2, 256)
        w = cols_of(W, [(c0, 64), (c0, 64), (c0 + 64, 64), (c0 + 64, 64)])
        for g in range(2):
            b, t = fm(w, g * 128, X, 256)
            t1 = ev(kv[nm][:, g, :], b[:, 0:256], [t])
            give(b, t1)
        wfree(w, t)
    vsw = sb(2, 256)
    w = cols_of(W, [(896, 128), (1152, 128)])
    for k in range(2):
        b, t = tm(w, 0, 256, X, k)
        t1 = ev(vsw[:, k, :], b[:, 0:256], [t])
        give(b, t1)
    wfree(w, t)
    gt = sb(2, 24)
    w = cols(W, 1280, 128)
    b, t = by_tokens(w, 0, X, 2, GB[:, 0, :])
    wfree(w, t)
    t1 = act(gt, b[:, 0:256].rearrange("p (k f) -> p k f", k=2)[:, :, 0:24], ACT.Sigmoid, [t])
    give(b, t1)
    tmp = sb(256)
    blk = sb(16, 2, 15)
    hid, hidT = sb(256), sb(2, 30)
    kcT, vcm = sb(30), sb(2, 64)
    def n_prepare():
        t = [t_c, t_z, *done()]
        for x, o in [(q[:, j, :], [qZ[:, 2 * j, :], qZ[:, 2 * j + 1, :]]) for j in range(4)] + \
                [(kv[n_][:, g, :], None) for n_ in ("ks", "kw") for g in range(2)]:
            rotate(x, 256, Rn, cosn, sinn, tmp, t, o)
            yield
        for nm, pe, w1 in (("kc", "cmp_pe_k_2", "cmp_w1_k_2"), ("vc", "cmp_pe_v_2", "cmp_w1_v_2")):
            dep = [SC.last(), VE.last()]
            for h in range(2):
                v = kv[nm][:, h, :].rearrange("p (c s) -> p s c", s=16)
                for par in range(2):
                    s = slice(par * 64, par * 64 + 64)
                    for e_ in range(2):
                        tt(blk[s, e_ * 8:e_ * 8 + 8, h, :], v[s, par::2, e_:e_ + 15],
                           col(pe, e_ * 8, 8)[s].unsqueeze(2).to_broadcast([64, 8, 15]), ADD, dep)
            b, free = take()
            for half in range(2):
                w = cols(I[w1][0], 0, 256, half * 8, 8, whole=True)
                for k in range(8):
                    t = mm(b[0:30, 0:256], blk[:, half * 8 + k, :, :], w.v[:, k, :], half == 0 and k == 0, half == 1 and k == 7,
                           [w.tok, VE.last(), *free] if k == 0 else ())
                wfree(w, t)
                yield
            t = act(hid[0:30, :], b[0:30, 0:256], ACT.Gelu_apprx_tanh, [t])
            give(b, t)
            yield
            b, free = take()
            for k in range(2):
                t = tr(b[:, k * 32:k * 32 + 30], hid[0:30, k * 128:k * 128 + 128], ident[0:30, 0:30], [t, *free])
            t = cp(hidT, b[:, 0:64].rearrange("p (k c) -> p k c", k=2)[:, :, 0:30], [t])
            give(b, t)
            yield
            b, free = take()
            if nm == "kc":
                for k in range(2):
                    t = mm(b[:, 0:30], w2k[:, k, :], hidT[:, k, :], k == 0, k == 1, [t, t_c, *free])
                t = cp(kcT, b[:, 0:30], [t])
            else:
                for h in range(2):
                    for k in range(2):
                        t = mm(b[0:15, h * 64:h * 64 + 64], hidT[:, k, h * 15:h * 15 + 15], w2v[:, k, :], k == 0, k == 1, [t, t_c, *free])
                t = cp(vcm[0:15], b[0:15, 0:128].rearrange("p (h d) -> p h d", h=2), [t])
            give(b, t)
        yield from attend(items, [VE.last(), GP.last()])

    items = []
    for pair in range(4):
        for h in (2 * pair, 2 * pair + 1):
            po, g = 64 * (h % 2), h // 4
            for qt in range(2):
                s = slice(qt * 128, qt * 128 + 128)
                ql = qZ[:, h, s]
                n = 128 * (qt + 1)
                base = dict(po=po, oc=qt * 128, open=False, close=None, begin=False, end=False)
                items.append({**base, "n": 15, "mms": [(ql, kcT[:, g * 15:g * 15 + 15], 0, 15), (ident, cm[:, qt, 0:15], 0, 15)],
                              "m01": c01[:, qt, 0:15], "gate": gt[:, qt, 3 * h:3 * h + 1], "kts": [(0, 15, vcm[0:15, g, :])],
                              "begin": True, "open": h % 2 == 0 and qt == 0})
                for bi, (kn, vo) in enumerate((("ks", 0), ("kw", 128))):
                    items.append({**base, "n": n, "mms": [(ql, kv[kn][:, g, 0:n], 0, n), (ident, caus, n - 128, n)],
                                  "gate": gt[:, qt, 3 * h + 1 + bi:3 * h + 2 + bi],
                                  "kts": [(k * 128, 128, vsw[:, k, vo + g * 64:vo + g * 64 + 64]) for k in range(qt + 1)],
                                  "end": bi == 1, "close": oN[:, pair, :] if bi == 1 and h % 2 and qt else None})
    def r_proj():
        for dst, c0, sc in ((qr, 1304, 1.0), (kr, 1816, 128 ** -0.5)):
            for j in range(4):
                if j % 2 == 0:
                    w = cols(W, c0 + j * 128, 256)
                b, t = fm(w, (j % 2) * 128, X, 256)
                if j % 2:
                    wfree(w, t)
                t = ts(dst[:, j, :], b[:, 0:256], sc, None, MUL, None, [t])
                give(b, t)
                yield
        turns = iter([qr[:, j, :] for j in range(4)] + [kr[:, j, :] for j in range(4)])
        ready = [t_r, t]
        for dst, c0, n in ((vr, 2328, 4), (gr, 3352, 4), (ga, 4376, 8)):
            for j in range(n):
                w = cols(W, c0 + j * 256, 256)
                for k in range(2):
                    b, t = tm(w, 0, 256, X, k)
                    t1 = ev(dst[:, k, j * 256:j * 256 + 256], b[:, 0:256], [t])
                    give(b, t1)
                    if k:
                        wfree(w, t)
                        for x in [x for _, x in zip(range(1), turns)]:
                            rotate(x, 256, Rr, cosr, sinr, tmpr, ready)
                    yield

    run(n_prepare(), r_proj())

    def branch(Wb, x, nk, g0, add, after, t_g=None):
        for c in range(4):
            bs = [take() for _ in range(2)]
            w = cols(Wb, c * 256, 256, 0, nk)
            for k in range(nk):
                for m_ in range(2):
                    b, free = bs[m_]
                    t = mm3(b[:, 0:256], [a[:, k, m_ * 128:m_ * 128 + 128] for a in (x.hi, x.lo)],
                            [a[:, k, :] for a in (w.v.hi, w.v.lo)], k == 0, k == nk - 1, [w.tok, *free, *after] if k == 0 else ())
            wfree(w, t)
            for m_ in range(2):
                g = ga[:, m_, g0 + c * 256:g0 + c * 256 + 256]
                z = Z[:, m_, c * 256:c * 256 + 256]
                if add:
                    t1 = tt(g, bs[m_][0][:, 0:256], g, MUL, [t])
                    tt(z, z, g, ADD)
                else:
                    t1 = tt(z, bs[m_][0][:, 0:256], g, MUL, [t, t_g])
                give(bs[m_][0], t1)
            yield

    barrier()
    top[0] = m_n
    Z = sb(2, 1024)
    dec, gw = sb(4, 384), sb(1024)
    t_c = load(SC, [(dec, C["dec"])], done())
    was = done()
    t_n = split(oN, oNh, oN, ())
    act(ga, ga, ACT.Sigmoid)
    t_g = act(gr, gr, ACT.Silu)
    ST = [sb(384) for _ in range(4)]
    oR = sb(2, 1024)
    a0, a1, a2 = tiny[:, 0:8], tiny[:, 8:16], tiny[:, 16:24]

    def retention(h):
        s = ST[h]
        b, free = take()
        mm(b[:, 0:256], kr[:, h, 0:128], qr[:, h, :], after=[*was, *free])
        t = mm(b[:, 256:384], kr[:, h, 128:256], qr[:, h, 128:256])
        t = tt(s, b[:, 0:384], dec[:, h, :], MUL, [t, t_c])
        give(b, t)
        yield
        for i in range(2):
            b, free = take()
            v = lambda k: vr[:, k, h * 256:h * 256 + 256]
            if i == 0:
                t1 = mm(b[:, 0:256], s[:, 0:128], v(0), after=[t, *free])
            else:
                mm(b[:, 0:256], s[:, 128:256], v(0), True, False, [t, *free])
                t1 = mm(b[:, 0:256], s[:, 256:384], v(1), False, True)
            o, c = oR[:, i, h * 256:h * 256 + 256], 4 * i + h
            t1 = act(o, b[:, 0:256], ACT.Copy, [t1], accum_out=a0[:, c:c + 1])
            give(b, t1)
            ts(a0[:, c:c + 1], a0[:, c:c + 1], -1.0 / 256, None, MUL, None, [t1])
            t1 = ts(o, o, a0[:, c:c + 1], None, ADD)
            yield
            act(JUNK[:, 0:256], o, ACT.Square, [t1], accum_out=a1[:, c:c + 1])
        yield

    spread(lambda k: col("ret_gn_w_2", k), gw, was)
    for i in range(2):
        t_gw = tt(gr[:, i, :], gr[:, i, :], gw, MUL, [t_g, SC.last(), VE.last()], q=GP)
    run(branch(I["w_nsa_branch_2"][0], Pair(oNh, oN), 4, 0, False, [t_n], t_g), staggered_(retention(h) for h in range(4)))
    t = ts(a1, a1, 1.0 / 256, 1e-6, MUL, ADD, [SC.last()])
    t = act(a1, a1, ACT.Sqrt, [t])
    recip(a2, a1, [t])
    oT = Pair(*[XH[:, i:i + 4, :].rearrange("p a (b c) -> p (a b) c", b=2) for i in (0, 4)])
    for i in range(2):
        for h in range(4):
            o, c = oR[:, i, h * 256:h * 256 + 256], 4 * i + h
            t = stt(o, o, a2[:, c:c + 1], gr[:, i, h * 256:h * 256 + 256], MUL, MUL, [t_gw])
        for q in (0, 4):
            b, free = take()
            for j in range(4):
                t1 = tr(b[:, j * 128:j * 128 + 128], oR[:, i, (q + j) * 128:(q + j) * 128 + 128], ident, [t, *free] if j == 0 else ())
            hi, lo = [a[:, q:q + 4, i * 128:i * 128 + 128] for a in (oT.hi, oT.lo)]
            give(b, split(b[:, :].rearrange("p (a c) -> p a c", a=4), hi, lo, [t1]))
    r = [VE.last()]
    zT = Pair(*[XT[:, i:i + 4, :].rearrange("p a (b c) -> p (a b) c", b=2) for i in (0, 4)])

    def z_turn(c):
        b, free = take()
        for j in range(2):
            for k in range(2):
                t = tr(b[:, (2 * j + k) * 128:(2 * j + k) * 128 + 128], Z[:, k, c * 256 + j * 128:c * 256 + j * 128 + 128],
                       ident, [VE.last(), *free] if j + k == 0 else ())
        hi, lo = [a[:, 2 * c:2 * c + 2, :].rearrange("p a b -> p (a b)") for a in (zT.hi, zT.lo)]
        give(b, split(b[:, :], hi, lo, [t]))
        return [VE.last()]

    for c, _ in enumerate(branch(I["w_ret_branch_2"][0], oT, 8, 1024, True, r)):
        if c:
            z_turn(c - 1)
    r = z_turn(3)
    for c in range(4):
        w = cols(I["w_mix_out_2"][0], c * 256, 256)
        for m_ in range(2):
            b, t = tm(w, 0, 256, zT, m_, r)
            t1 = tt(H[:, m_, c * 256:c * 256 + 256], H[:, m_, c * 256:c * 256 + 256], b[:, 0:256], ADD, [t])
            give(b, t1)
        wfree(w, t)
    barrier()
    top[0] = m_layer
    xr = norm_turn(2, lambda f, s: col("norm_ffn_w_2", f), None, None, done())
    aT = Pair(sb_aligned(24, 256), sb(24, 256))
    U = [sb(256) for _ in range(4)]
    u_free, ready, later = [()] * 4, [], []

    def gated(j, t):
        u = U[j % 4]
        if j < 22:
            u_free[j % 4] = (act(aT.lo[:, j, :], u, ACT.Silu, [t]),)
        else:
            a, ah = aT.lo[:, j - 22, :], aT.hi[:, j - 22, :]
            ready.append([split(a, ah, a, [t])])

    W = I["w_ffn_up_2"][0]
    for j in range(44):
        if j % 2 == 0:
            w = cols(W, j * 128, 256)
        b, t = fm(w, (j % 2) * 128, X, 256, xr if j == 0 else ())
        if j % 2:
            wfree(w, t)
        u = U[j % 4]
        t = act(u, b[:, 0:256], ACT.Identity, [t, *u_free[j % 4]], scale=col("ffn_conv_w_2", 88 + j), bias=col("ffn_conv_b_2", j))
        stt(u[:, 1:256], b[:, 0:255], col("ffn_conv_w_2", 44 + j), u[:, 1:256], MUL, ADD, [t])
        t = stt(u[:, 2:256], b[:, 0:254], col("ffn_conv_w_2", j), u[:, 2:256], MUL, ADD)
        give(b, t)
        if j >= 22:
            a = aT.lo[:, j - 22, :]
            t = tt(a, a, u, MUL, [t, SC.last()], q=GP)
            u_free[j % 4] = (t,)
        later.append((j, t))
        if len(later) > 2:
            gated(*later.pop(0))
    for x in later:
        gated(*x)
    W = I["w_ffn_down_2"][0]
    O = sb(2, 1024)
    out_proj([(W, 0, 8), (W, 8, 8), (W, 16, 6)], aT, 2, O, (), ready)
    gw, junk, fin = sb(1024), sb(1024), sb(2, 1024)
    spread(lambda k: col("norm_final_w_2", k), gw, done())
    for k in range(2):
        t = tt(H[:, k, :], H[:, k, :], O[:, k, :], ADD, done())
        t, r = rstd_of(H[:, k, :], 1024, 1e-6, k, junk, [t])
        t = stt(fin[:, k, :], H[:, k, :], r, gw, MUL, MUL, [t])
        stores.append(load(SP, [(out[0, k * 128:k * 128 + 128, :], fin[:, k, :])], [t]))
    SP.ops.append(Op(None, stores, False))

    for q_ in ENG + [SP]:
        if q_.chain:
            prev = None
            for op in q_.ops:
                if op.compute:
                    if prev is not None:
                        op.waits.append((q_, prev))
                        prev.marked = True
                    prev = op
    for q_ in ENG + [SP]:
        n = 0
        for op in q_.ops:
            n += op.marked
            op.value = n

    def emit(q_, e):
        seen = {}
        for op in q_.ops:
            need = {}
            for w_ in op.waits:
                s_, v_ = (w_[1], w_[2]) if w_[0] == "dma" else (w_[0].sem, w_[1].value)
                if seen.get(id(s_), (s_, 0))[1] < v_ and need.get(id(s_), (s_, 0))[1] < v_:
                    need[id(s_)] = (s_, v_)
            for i_, (s_, v_) in need.items():
                e.wait_ge(s_, v_)
                seen[i_] = (s_, v_)
            if op.fn is not None:
                ins = op.fn(e)
                if op.marked:
                    ins.then_inc(q_.sem, 1)

    block = ctx.enter_context(nc.Block())
    block.sync(lambda e: emit(SP, e))
    block.scalar(lambda e: emit(SC, e))
    block.gpsimd(lambda e: emit(GP, e))
    block.vector(lambda e: emit(VE, e))
    block.tensor(lambda e: emit(PE, e))
    ctx.close()


def tables():
    import numpy as np
    f = np.float32
    p = np.arange(128)
    t = np.arange(256)
    T = {"ident": np.eye(128), "bones": np.kron(np.eye(2), np.ones((64, 64)))}

    def rot(n, half, width):
        m = np.zeros((128, 128))
        for base in range(0, 128, width):
            for i in range(half):
                m[base + half + i, base + i] = -1.0
                m[base + i, base + half + i] = 1.0
        return m

    T["sel"] = np.stack([p % 32 == 0, p % 32 == 1], axis=1)
    T["Rax"] = rot(128, 16, 32)
    inv = f(10000.0) ** (-np.arange(16, dtype=f) / f(16))
    ang = np.zeros((128, 256), f)
    for i in range(128):
        pos = (t // 64 if (i % 64) < 32 else t % 64).astype(f)
        ang[i] = pos * inv[i % 16]
    T["cosax"], T["sinax"] = np.cos(ang), np.sin(ang)
    T["Rnsa"] = rot(128, 8, 64)
    inv = np.power(f(500000.0), -np.arange(8, dtype=f) / f(8))
    c, s = np.ones((128, 256), f), np.zeros((128, 256), f)
    for i in range(128):
        if i % 64 < 16:
            a = t.astype(f) * inv[i % 8]
            c[i], s[i] = np.cos(a), np.sin(a)
    T["cosnsa"], T["sinnsa"] = c, s
    T["Rret"] = rot(128, 64, 128)
    inv = np.power(f(10000.0), -np.arange(64, dtype=f) / f(64))
    ang = t.astype(f)[None, :] * inv[p % 64][:, None]
    T["cosret"], T["sinret"] = np.cos(ang), np.sin(ang)
    NEG = f(-1e30)
    q = p[:, None, None] + 128 * np.arange(2)[None, :, None]
    T["wmask"] = np.where(np.abs(q - t[None, None, :]) <= 128, 0, NEG)
    cq = (p % 64)[:, None]
    ck = (t % 64)[None, :]
    ws = np.clip(cq - 8, 0, 48)
    flip = np.kron(np.eye(2), np.eye(64)[::-1])
    T["flip"] = flip
    T["cmask"] = np.where((ck >= ws) & (ck < ws + 16), 0, NEG)[np.argmax(flip, axis=1)]
    T["caus"] = np.where(p[None, :] <= p[:, None], 0, NEG)
    ce = np.arange(16)[None, None, :] * 16 + 31
    ok = ce <= q
    T["cmpm"], T["cmp01"] = np.where(ok, 0, NEG), ok.astype(f)
    T["scanm"] = np.broadcast_to((np.arange(512) % 64 != 0), (128, 512))
    i, j = (p % 64)[:, None], np.arange(64)[None, :]
    L = np.zeros((128, 2, 6, 64))
    for l in range(6):
        s_ = 1 << l
        same = (i // (2 * s_)) == (j // (2 * s_))
        L[:, 0, l, :] = same & (i % (2 * s_) >= s_) & (j % (2 * s_) < s_)
        L[:, 1, l, :] = same & (i % (2 * s_) < s_) & (j % (2 * s_) >= s_)
    T["lvl"] = np.concatenate([L * (p < 64)[:, None, None, None], L * (p >= 64)[:, None, None, None]], 3)
    i, j = p[:, None], p[None, :]
    same = (i // 64) == (j // 64)
    T["tri"] = np.stack([same & (i < j), same & (i > j)], 1)
    u, v = (p % 64)[:, None], np.arange(64)[None, :]
    T["incl"] = np.stack([u <= v, u >= v], 1)
    lg = np.log1p(-np.exp2(-5.0 - np.arange(4)))
    dec = np.zeros((128, 4, 384))
    for h in range(4):
        d = t[None, :] - p[:, None]
        dec[:, h, 0:256] = np.where(d >= 0, np.exp(lg[h] * np.maximum(d, 0)), 0)
        dec[:, h, 256:384] = dec[:, h, 0:128]
    T["dec"] = dec
    return {k: np.ascontiguousarray(v, dtype=f) for k, v in T.items()}


_INS = ["x", "c", "ctx", "c_ctx", "w_ada", "b_ada", "g_pre_mix", "g_post_mix", "g_pre_ff", "g_post_ff", "w_in_even",
        "w_in_odd", "w_out", "w_ff1", "w_ff2", "a_mu_prev", "a_mu_next", "a_w0", "a_w2", "a_a0", "a_a2", "a_g2", "a_k_k",
        "a_k_a", "a_r_k", "a_gn_w", "a_gn_b", "b_sink", "c_rpb", "d_q_gain", "d_k_gain", "norm_mix_w_2", "w_in_2",
        "cmp_pe_k_2", "cmp_w1_k_2", "cmp_w2_k_2", "cmp_pe_v_2", "cmp_w1_v_2", "cmp_w2_v_2", "w_nsa_branch_2",
        "ret_gn_w_2", "w_ret_branch_2", "w_mix_out_2", "norm_ffn_w_2", "w_ffn_up_2", "ffn_conv_w_2",
        "ffn_conv_b_2", "w_ffn_down_2", "norm_final_w_2"]


def kernel(**inputs):
    import numpy as np
    import concourse.bacc as bacc
    from concourse import mybir
    from concourse.bass_utils import run_bass_kernel_spmd as run

    nc = bacc.Bacc("TRN2", target_bir_lowering=False, num_devices=1, dynamic_dma_scratch_size=1024)
    arrays, I, C = {}, {}, {}
    for name in _INS:
        a = np.ascontiguousarray(inputs[name])
        arrays["in_" + name] = a
        I[name] = nc.dram_tensor("in_" + name, a.shape, mybir.dt.float32, kind="ExternalInput").ap()
    for name, a in tables().items():
        arrays["t_" + name] = a
        C[name] = nc.dram_tensor("t_" + name, a.shape, mybir.dt.float32, kind="ExternalInput").ap()
    out = nc.dram_tensor("out_0", (1, 256, 1024), mybir.dt.float32, kind="ExternalOutput").ap()
    program(nc, I, C, out)
    r = run(nc, [arrays], core_ids=[0])
    return r.results[0]["out_0"]
```
